# Optimizing a Trainium2 kernel written in Bass

```python
import math
import jax, jax.numpy as jnp
from jax import lax
import numpy as np

D_MODEL = 1024
BATCH = 1
SEQ = 512
DEPTH = 2
DEC_BATCH = 1
DEC_SEQ = 256
PAST_LEN = 128

N_META = 16
RMS_EPS = 1e-6
NEG = -1e30
M_HEADS = 4
M_DK = 128
M_DV = 256
M_CHUNK = 64
M_PAD = M_CHUNK - N_META
M_QK_W = M_HEADS * M_DK
M_V_W = M_HEADS * M_DV
M_IN_W = 2 * M_QK_W + 2 * M_V_W + 4 * M_HEADS
D_HEADS = 8
D_HD = 64
D_QK_W = D_HEADS * 2 * D_HD
D_V_W = D_HEADS * 2 * D_HD
D_IN_W = 2 * D_QK_W + D_V_W
ROPE_THETA = 500000.0
ROPE_DIM = D_HD // 4
Q_BLOCK = 128
FF = -(-8 * D_MODEL // (3 * 256)) * 256
N_M_LAYERS = (DEPTH + 1) // 2
N_D_LAYERS = DEPTH // 2

kernel_name = "hybrid_bidir_mlstm_diffattn_encoder"

def _rms_f32(x, g):
    xf = x.astype(jnp.float32)
    y = xf * lax.rsqrt(jnp.mean(xf * xf, axis=-1, keepdims=True) + RMS_EPS)
    return y * g.astype(jnp.float32)

def rmsnorm(x, g):
    return _rms_f32(x, g).astype(x.dtype)

def mlstm_cell(q, k, v, ig, lf):
    B, H, Lp, dk = q.shape
    dv = v.shape[-1]
    nc = Lp // M_CHUNK

    def chunks(t):
        return jnp.moveaxis(t.reshape((B, H, nc, M_CHUNK) + t.shape[3:]), 2, 0)

    tril = jnp.tril(jnp.ones((M_CHUNK, M_CHUNK), dtype=bool))

    def step(carry, xs):
        C, n, m = carry
        qc, kc, vc, igc, lfc = xs
        b = jnp.cumsum(lfc, axis=-1)
        dmat = jnp.where(tril, b[..., :, None] - b[..., None, :] + igc[..., None, :], -jnp.inf)
        m_inter = b + m[..., None]
        m_comb = jnp.maximum(jnp.max(dmat, axis=-1), m_inter)
        w_ts = jnp.exp(dmat - m_comb[..., None]) * jnp.einsum("bhtk,bhsk->bhts", qc, kc)
        scale = jnp.exp(m_inter - m_comb)
        num = jnp.einsum("bhts,bhsv->bhtv", w_ts, vc) + scale[..., None] * jnp.einsum("bhtk,bhvk->bhtv", qc, C)
        den = jnp.sum(w_ts, axis=-1) + scale * jnp.einsum("bhtk,bhk->bht", qc, n)
        h = num / jnp.maximum(jnp.abs(den), jnp.exp(-m_comb))[..., None]
        b_last = b[..., -1]
        a = b_last[..., None] - b + igc
        m_new = jnp.maximum(b_last + m, jnp.max(a, axis=-1))
        decay = jnp.exp(b_last + m - m_new)
        wk = jnp.exp(a - m_new[..., None])
        C_new = decay[..., None, None] * C + jnp.einsum("bhsv,bhsk->bhvk", vc * wk[..., None], kc)
        n_new = decay[..., None] * n + jnp.einsum("bhs,bhsk->bhk", wk, kc)
        return (C_new, n_new, m_new), h

    init = (jnp.zeros((B, H, dv, dk), jnp.float32),
            jnp.zeros((B, H, dk), jnp.float32),
            jnp.zeros((B, H), jnp.float32))
    _, h = lax.scan(step, init, (chunks(q), chunks(k), chunks(v), chunks(ig), chunks(lf)))
    return jnp.moveaxis(h, 0, 2).reshape(B, H, Lp, dv)

def mlstm_mixer(xn, w_in, b_gate, g_head, w_out):
    B, L, _ = xn.shape
    proj = xn @ w_in
    q = proj[..., :M_QK_W]
    k = proj[..., M_QK_W:2 * M_QK_W]
    v = proj[..., 2 * M_QK_W:2 * M_QK_W + M_V_W]
    o = proj[..., 2 * M_QK_W + M_V_W:2 * M_QK_W + 2 * M_V_W]
    gpre = proj[..., 2 * M_QK_W + 2 * M_V_W:]

    def heads(t, d):
        t = t.astype(jnp.float32).reshape(B, L, M_HEADS, d)
        t = jnp.pad(t, ((0, 0), (M_PAD, 0), (0, 0), (0, 0)))
        return t.transpose(0, 2, 1, 3)

    qh = heads(q, M_DK) * (M_DK ** -0.5)
    kh = heads(k, M_DK)
    vh = heads(v, M_DV)
    gates = (gpre.astype(jnp.float32) + b_gate.astype(jnp.float32)).reshape(B, L, 4, M_HEADS)
    gates = jnp.pad(gates, ((0, 0), (M_PAD, 0), (0, 0), (0, 0))).transpose(2, 0, 3, 1)
    valid = jnp.arange(L + M_PAD) >= M_PAD
    ig = jnp.where(valid, gates[0::2], NEG)
    lf = jnp.where(valid, jax.nn.log_sigmoid(gates[1::2]), 0.0)

    def flip(t):
        return jnp.flip(t, axis=2)

    h_f = mlstm_cell(qh, kh, vh, ig[0], lf[0])
    h_b = flip(mlstm_cell(flip(qh), flip(kh), flip(vh), flip(ig[1]), flip(lf[1])))
    h = (h_f + h_b)[:, :, M_PAD:]
    h = _rms_f32(h, g_head)
    h = h.transpose(0, 2, 1, 3).reshape(B, L, M_V_W)
    h = (h * jax.nn.sigmoid(o.astype(jnp.float32))).astype(xn.dtype)
    return h @ w_out

def rope_tables(L):
    pos = jnp.arange(L, dtype=jnp.float32)
    inv = ROPE_THETA ** (-jnp.arange(0, ROPE_DIM, 2, dtype=jnp.float32) / ROPE_DIM)
    ang = pos[:, None] * inv[None, :]
    return jnp.cos(ang), jnp.sin(ang)

def partial_rope(x, cos, sin):
    half = ROPE_DIM // 2
    x1 = x[..., :half]
    x2 = x[..., half:ROPE_DIM]
    rest = x[..., ROPE_DIM:]
    c = cos[None, :, None, None, :]
    s = sin[None, :, None, None, :]
    return jnp.concatenate([x1 * c - x2 * s, x2 * c + x1 * s, rest], axis=-1)

def diff_attn(xn, w_in, g_q, g_k, lam_q1, lam_k1, lam_q2, lam_k2, g_sub, w_out, lambda_init):
    B, L, _ = xn.shape
    proj = xn @ w_in
    q = proj[..., :D_QK_W].reshape(B, L, D_HEADS, 2, D_HD)
    k = proj[..., D_QK_W:2 * D_QK_W].reshape(B, L, D_HEADS, 2, D_HD)
    v = proj[..., 2 * D_QK_W:].reshape(B, L, D_HEADS, 2 * D_HD).astype(jnp.float32)
    cos, sin = rope_tables(L)
    q = partial_rope(_rms_f32(q, g_q), cos, sin) * (D_HD ** -0.5)
    k = partial_rope(_rms_f32(k, g_k), cos, sin)
    q = q.transpose(0, 2, 3, 1, 4)
    k = k.transpose(0, 2, 3, 1, 4)
    v = v.transpose(0, 2, 1, 3)
    lam = (jnp.exp(jnp.sum(lam_q1.astype(jnp.float32) * lam_k1.astype(jnp.float32)))
           - jnp.exp(jnp.sum(lam_q2.astype(jnp.float32) * lam_k2.astype(jnp.float32)))
           + lambda_init)
    nb = -(-L // Q_BLOCK)
    Lq = nb * Q_BLOCK
    qb = jnp.pad(q, ((0, 0), (0, 0), (0, 0), (0, Lq - L), (0, 0))).reshape(B, D_HEADS, 2, nb, Q_BLOCK, D_HD)
    qb = jnp.moveaxis(qb, 3, 0)

    def block(qblk):
        s = jnp.einsum("bhcqd,bhckd->bhcqk", qblk, k)
        p = jax.nn.softmax(s, axis=-1)
        a = p[:, :, 0] - lam * p[:, :, 1]
        return jnp.einsum("bhqk,bhkv->bhqv", a, v)

    o = lax.map(block, qb)
    o = jnp.moveaxis(o, 0, 2).reshape(B, D_HEADS, Lq, 2 * D_HD)[:, :, :L]
    o = _rms_f32(o, g_sub) * (1.0 - lambda_init)
    o = o.transpose(0, 2, 1, 3).reshape(B, L, D_V_W).astype(xn.dtype)
    return o @ w_out

def swiglu(xn, w_in, w_out):
    gu = xn @ w_in
    g = gu[..., :FF]
    u = gu[..., FF:]
    return (jax.nn.silu(g) * u) @ w_out

def trunk(x, meta_tokens, norm_mix, norm_ffn, m_w_in, m_b_gate, m_g_head, m_w_out,
          d_w_in, d_g_q, d_g_k, d_lam_q1, d_lam_k1, d_lam_q2, d_lam_k2, d_g_sub, d_w_out,
          ffn_w_in, ffn_w_out):
    B = x.shape[0]
    meta = jnp.broadcast_to(meta_tokens[None].astype(x.dtype), (B, N_META, D_MODEL))
    h = jnp.concatenate([meta, x], axis=1)
    for i in range(DEPTH):
        j = i // 2
        xn = rmsnorm(h, norm_mix[i])
        if i % 2 == 0:
            h = h + mlstm_mixer(xn, m_w_in[j], m_b_gate[j], m_g_head[j], m_w_out[j])
        else:
            lambda_init = 0.8 - 0.6 * math.exp(-0.3 * i)
            h = h + diff_attn(xn, d_w_in[j], d_g_q[j], d_g_k[j], d_lam_q1[j], d_lam_k1[j],
                              d_lam_q2[j], d_lam_k2[j], d_g_sub[j], d_w_out[j], lambda_init)
        xn = rmsnorm(h, norm_ffn[i])
        h = h + swiglu(xn, ffn_w_in[i], ffn_w_out[i])
    return h[:, N_META:]

def setup_inputs(seed: int = 0) -> dict:
    key = jax.random.key(seed)
    ks = jax.random.split(key, 24)
    f32 = jnp.float32

    def nrm(k, shape, scale):
        return jax.random.normal(k, shape, f32) * scale

    fg_off = jnp.concatenate([jnp.zeros((M_HEADS,), f32), jnp.linspace(3.0, 6.0, M_HEADS, dtype=f32),
                              jnp.zeros((M_HEADS,), f32), jnp.linspace(3.0, 6.0, M_HEADS, dtype=f32)])
    return {
        "x_prompt": nrm(ks[0], (BATCH, SEQ, D_MODEL), 1.0),
        "x_sample": nrm(ks[1], (DEC_BATCH, DEC_SEQ, D_MODEL), 1.0),
        "meta_tokens": nrm(ks[2], (N_META, D_MODEL), 1.0),
        "norm_mix": 1.0 + nrm(ks[3], (DEPTH, D_MODEL), 0.05),
        "norm_ffn": 1.0 + nrm(ks[4], (DEPTH, D_MODEL), 0.05),
        "m_w_in": nrm(ks[5], (N_M_LAYERS, D_MODEL, M_IN_W), D_MODEL ** -0.5),
        "m_b_gate": fg_off[None, :] + nrm(ks[6], (N_M_LAYERS, 4 * M_HEADS), 0.1),
        "m_g_head": 1.0 + nrm(ks[7], (N_M_LAYERS, M_DV), 0.05),
        "m_w_out": nrm(ks[8], (N_M_LAYERS, M_V_W, D_MODEL), M_V_W ** -0.5),
        "d_w_in": nrm(ks[9], (N_D_LAYERS, D_MODEL, D_IN_W), D_MODEL ** -0.5),
        "d_g_q": 1.0 + nrm(ks[10], (N_D_LAYERS, D_HD), 0.05),
        "d_g_k": 1.0 + nrm(ks[11], (N_D_LAYERS, D_HD), 0.05),
        "d_lam_q1": nrm(ks[12], (N_D_LAYERS, D_HD), 0.1),
        "d_lam_k1": nrm(ks[13], (N_D_LAYERS, D_HD), 0.1),
        "d_lam_q2": nrm(ks[14], (N_D_LAYERS, D_HD), 0.1),
        "d_lam_k2": nrm(ks[15], (N_D_LAYERS, D_HD), 0.1),
        "d_g_sub": 1.0 + nrm(ks[16], (N_D_LAYERS, 2 * D_HD), 0.05),
        "d_w_out": nrm(ks[17], (N_D_LAYERS, D_V_W, D_MODEL), D_V_W ** -0.5),
        "ffn_w_in": nrm(ks[18], (DEPTH, D_MODEL, 2 * FF), D_MODEL ** -0.5),
        "ffn_w_out": nrm(ks[19], (DEPTH, FF, D_MODEL), FF ** -0.5),
    }

def reference(x_prompt, x_sample, meta_tokens, norm_mix, norm_ffn, m_w_in, m_b_gate, m_g_head, m_w_out,
              d_w_in, d_g_q, d_g_k, d_lam_q1, d_lam_k1, d_lam_q2, d_lam_k2, d_g_sub, d_w_out,
              ffn_w_in, ffn_w_out):
    y_prompt = trunk(x_prompt, meta_tokens, norm_mix, norm_ffn, m_w_in, m_b_gate, m_g_head, m_w_out,
                     d_w_in, d_g_q, d_g_k, d_lam_q1, d_lam_k1, d_lam_q2, d_lam_k2, d_g_sub, d_w_out,
                     ffn_w_in, ffn_w_out)
    y_sample = trunk(x_sample, meta_tokens, norm_mix, norm_ffn, m_w_in, m_b_gate, m_g_head, m_w_out,
                     d_w_in, d_g_q, d_g_k, d_lam_q1, d_lam_k1, d_lam_q2, d_lam_k2, d_g_sub, d_w_out,
                     ffn_w_in, ffn_w_out)
    return (y_prompt, y_sample)


_drawn_inputs = setup_inputs


def setup_inputs(seed=0):
    import zlib

    import numpy as np

    out = dict(_drawn_inputs(seed))
    spreads = {}
    factors = {'d_lam_q2': 200.0, 'd_lam_q1': 2.996}
    for name, (base, spread) in spreads.items():
        noise = np.random.default_rng([zlib.crc32(name.encode()), seed]).standard_normal(out[name].shape)
        drawn = base * np.exp(spread * noise) if base else spread * noise
        out[name] = __import__('jax').numpy.asarray(drawn.astype(out[name].dtype))
    for name, factor in factors.items():
        out[name] = (out[name] * factor).astype(out[name].dtype)
    return out
```

```python
import math
from contextlib import ExitStack

import concourse.bass as bass
from concourse import mybir

F32 = mybir.dt.float32
F32R = mybir.dt.float32r
ALU = mybir.AluOpType
ACT = mybir.ActivationFunctionType
AX = mybir.AxisListType

P = 128
D = 1024
KT = D // P
META = 16
LENS = (META + 512, META + 256)
T = sum(LENS)
HT = T // 2
FF = 2816
FT = FF // P
GROUPS = (8, 8, 6)
M_HEADS, M_DK, M_DV = 4, 128, 256
D_HEADS, D_HD = 8, 64
EPS = 1e-6
FAR = 1e30
LAMBDA_INIT = 0.8 - 0.6 * math.exp(-0.3)
ROPE_THETA, ROPE_DIM = 500000.0, D_HD // 4

TILES = [(s, t0, min(P, LENS[s] - a)) for s in (0, 1) for a in range(0, LENS[s], P)
         for t0 in (sum(LENS[:s]) + a,)]
START = (0, LENS[0])
OF_SEQ = ([0, 1, 2, 3, 4], [5, 6, 7])
NT = len(TILES)
WIDE = [(0, 4), (5, 7)]

MIX0 = 0
OUT0 = MIX0 + 6 * M_HEADS
FFN0 = OUT0 + KT
NFF = 2 * FT + KT * len(GROUPS)
MIX1 = FFN0 + NFF
OUT1 = MIX1 + 3 * D_HEADS
FFN1 = OUT1 + KT
BLOCKS = FFN1 + NFF
XT = 6
YL_AT = {OUT0: 2 * M_HEADS, FFN0: 2 * M_HEADS, MIX1: 2 * M_HEADS + FT,
         OUT1: 2 * M_HEADS + FT + D_HEADS, FFN1: 2 * M_HEADS + FT + D_HEADS}
GATE_COLS = 2 * M_HEADS * M_DK + 2 * M_HEADS * M_DV
M_PER = 57
A_PER = 78
ATTN_SET = 7

MIXN, FFNN, GHEAD, GSUB, GQ, GK, BGATE = 0, 16, 32, 34, 35, 36, 37
NPAR = 38
IDENT, MASKF, MASKB, PERM, ONEHOT, COMP, NCONST = 0, 128, 256, 384, 512, 516, 518


def host_constants():
    import numpy as np
    c = np.zeros((P, NCONST), np.float32)
    r = np.arange(P)
    c[r, IDENT + r] = 1.0
    c[:, MASKF:MASKF + P] = np.where(r[None, :] >= r[:, None], 0.0, FAR)
    c[:, MASKB:MASKB + P] = np.where(r[None, :] <= r[:, None], 0.0, FAR)
    half = ROPE_DIM // 2
    for base in (0, D_HD):
        for f in range(half):
            c[base + f + half, PERM + base + f] = 1.0
            c[base + f, PERM + base + f + half] = 1.0
    for h in range(M_HEADS):
        c[h, ONEHOT + h] = 1.0
        c[64 + h, ONEHOT + h] = 1.0
    c[0:D_HD, COMP] = 1.0
    c[D_HD:P, COMP + 1] = 1.0
    inv = np.float32(ROPE_THETA) ** (-np.arange(0, ROPE_DIM, 2, dtype=np.float32) / np.float32(ROPE_DIM))
    rope = np.zeros((P, 2, T), np.float32)
    rope[:, 0, :] = 1.0
    for s in (0, 1):
        ang = np.arange(LENS[s], dtype=np.float32)[:, None] * inv.astype(np.float32)[None, :]
        cos, sin = np.cos(ang).T, np.sin(ang).T
        cols = slice(START[s], START[s] + LENS[s])
        for base in (0, D_HD):
            rope[base:base + half, 0, cols] = cos
            rope[base + half:base + ROPE_DIM, 0, cols] = cos
            rope[base:base + half, 1, cols] = -sin
            rope[base + half:base + ROPE_DIM, 1, cols] = sin
    return c, rope


class Steps:

    def __init__(self, eng, sem):
        self.eng, self.sem, self.base, self.n = eng, sem, 0, 0

    def __call__(self, ins):
        ins.then_inc(self.sem, 1)
        self.n += 1

    def wait(self):
        self.eng.wait_ge(self.sem, self.base + self.n)

    def loop_start(self, i, per):
        self.entry = self.base + self.n
        self.base = i * per + self.entry
        self.n = 0

    def loop_end(self, count, per):
        assert self.n == per, (self.n, per)
        self.base, self.n = self.entry + count * per, 0


def trunk(nc, x_prompt, x_sample, meta_tokens, norm_mix, norm_ffn, m_w_in, m_b_gate, m_g_head, m_w_out,
          d_w_in, d_g_q, d_g_k, d_lam_q1, d_lam_k1, d_lam_q2, d_lam_k2, d_g_sub, d_w_out,
          ffn_w_in, ffn_w_out, consts, rope, y_prompt, y_sample):
    ctx = ExitStack()
    with ctx:
        def sb(name, shape, dt=F32, where=None):
            return (where or ctx).enter_context(nc.sbuf_tensor(name, shape, dt))

        def sem(name):
            return ctx.enter_context(nc.semaphore(name))

        h = sb("h", [P, KT, T])
        xh, xl = sb("xh", [P, KT, T], F32R), sb("xl", [P, KT, T], F32R)
        yh, yl = sb("yh", [P, KT, T], F32R), sb("yl", [P, KT, T], F32R)
        raw = sb("raw", [P, 2, KT * P])
        wh, wl = sb("wh", [P, 2, KT * P], F32R), sb("wl", [P, 2, KT * P], F32R)
        rstd = sb("rstd", [P, T])
        cst = sb("cst", [P, NCONST])
        ones = sb("ones", [P, P])
        par = sb("par", [P, NPAR])
        small = sb("small", [P, 4])
        ss = sb("ss", [P, NT])
        rs = sb("rs", [P, NT])
        wk = sb("wk", [P, 9, T])
        wkf = wk[:, :, :].rearrange("p a b -> p (a b)")
        epsc = small[:, 0:1]

        gate_phase = ExitStack()
        graw = sb("graw", [P, KT, 16], F32, gate_phase)
        gwh = sb("gwh", [P, KT, P], F32R, gate_phase)
        gwl = sb("gwl", [P, KT, P], F32R, gate_phase)
        prow = sb("prow", [NPAR, P], F32, gate_phase)
        gate_phase.close()

        mlstm_phase = ExitStack()
        vn = sb("vn", [P, NT, M_DV + 1], F32, mlstm_phase)
        wt = sb("wt", [P, 5, LENS[0] + P], F32, mlstm_phase)
        mrow = sb("mrow", [P, T], F32, mlstm_phase)
        ce = sb("ce", [P, NT, 4], F32, mlstm_phase)
        dd = sb("dd", [P, 2, 2], F32, mlstm_phase)
        rd = sb("rd", [P, 2, 2], F32, mlstm_phase)
        mlstm_phase.close()

        attn_phase = ExitStack()
        cq = sb("cq", [P, T], F32, attn_phase)
        ck = sb("ck", [P, T], F32, attn_phase)
        sn = sb("sn", [P, T], F32, attn_phase)
        permq = sb("permq", [P, P], F32, attn_phase)
        permk = sb("permk", [P, P], F32, attn_phase)
        va = sb("va", [P, NT, P], F32, attn_phase)
        at = sb("at", [P, 2, 5, P], F32, attn_phase)
        qk2 = sb("qk2", [P, NT, 4], F32, attn_phase)
        qkr = sb("qkr", [P, NT, 4], F32, attn_phase)
        mx = sb("mx", [P, NT, 2], F32, attn_phase)
        nb = sb("nb", [P, NT, 2], F32, attn_phase)
        sums = sb("sums", [P, NT, 2], F32, attn_phase)
        rsum = sb("rsum", [P, NT, 2], F32, attn_phase)
        ratio = sb("ratio", [P, NT], F32, attn_phase)
        lv = sb("lv", [P, 4, D_HD], F32, attn_phase)
        lam = sb("lam", [P, 8], F32, attn_phase)
        gsub = sb("gsub", [P, 1], F32, attn_phase)
        attn_phase.close()

        ps = ctx.enter_context(nc.psum_tensor("ps", [P, 8, 512], F32))

        def pair(p, rows=P):
            return ps[0:rows, 2 * p:2 * p + 2, 0:HT]

        def flat(p):
            return ps[:, 2 * p:8 if p == 2 else 2 * p + 2, :].rearrange("p a b -> p (a b)")

        def two(x):
            return x.rearrange("p (a b) -> p a b", a=2)

        ident = cst[:, IDENT:IDENT + P]

        cerow = wk[:, 8, :]
        sqp = wkf[:, 2 * T:3 * T + P]
        lall = wkf[:, 6 * T:6 * T + NT * P].rearrange("p (i c f) -> p i c f", i=NT, c=2)

        def hn(i):
            at_col = {4: T, 7: T + M_DV}[i] if TILES[i][2] < P else 6 * T + (i - (i > 4)) * M_DV
            return wkf[:, at_col:at_col + M_DV]

        def on(i):
            return wkf[:, 6 * T + i * P:6 * T + (i + 1) * P]

        ltile = on

        def prob(i, c):
            at_col = (2 + 2 * (i % 2)) * T + c * LENS[0]
            return wkf[:, at_col:at_col + LENS[0]]

        consts_in, params_in, meta_in, gate_in = sem("consts_in"), sem("params_in"), sem("meta_in"), sem("gate_in")
        x_in = [sem(f"x_in{r}") for r in range(XT)]
        raw_in = [sem("raw_in0"), sem("raw_in1")]
        rope_in, lam_in, out_done = sem("rope_in"), sem("lam_in"), sem("out_done")
        pool_set, w_hi, w_split = sem("pool_set"), sem("w_hi"), sem("w_split")
        gate_split = sem("gate_split")
        x_turned, meta_turned, par_turned, par_ready = sem("x_turned"), sem("meta_turned"), sem("par_turned"), sem("par_ready")
        h_ready, act_h = sem("h_ready"), sem("act_h")
        acc_free, block_done = sem("acc_free"), sem("block_done")
        xh_ready, xl_ready, sq_ready, sq_summed = sem("xh_ready"), sem("xl_ready"), sem("sq_ready"), sem("sq_summed")
        norm_sum, norm_root, rstd_ready = sem("norm_sum"), sem("norm_root"), sem("rstd_ready")
        vstep, astep, ones_set = sem("vstep"), sem("astep"), sem("ones_set")
        gates_done, gate_x, gate_soft, gate_m, gate_e = (sem(n) for n in ("gates_done", "gate_x", "gate_soft", "gate_m", "gate_e"))
        mrow_masked, mrep_done, mrep_ready = sem("mrow_masked"), sem("mrep_done"), sem("mrep_ready")
        ce_turned, ce_ready = sem("ce_turned"), sem("ce_ready")
        v_turned, vn_ready = sem("v_turned"), sem("vn_ready")
        s_ready, diag_ready, e_ready, wt_ready = sem("s_ready"), sem("diag_ready"), sem("e_ready"), sem("wt_ready")
        pv_done, hn_ready, hsq_ready, hroot = sem("pv_done"), sem("hn_ready"), sem("hsq_ready"), sem("hroot")
        hs_ready, sig_ready = sem("hs_ready"), sem("sig_ready")
        y_turned, yt_ready, yh_ready, yl_ready = sem("y_turned"), sem("yt_ready"), sem("yh_ready"), sem("yl_ready")
        gate_in_ready, silu_ready = sem("gate_in_ready"), sem("silu_ready")
        qsq_ready, rot_done, rot_free, qks_done = sem("qsq_ready"), sem("rot_done"), sem("rot_free"), sem("qks_done")
        qk_root, lt_ready, lt_turned, qkrope_ready, kn_ready = (sem(n) for n in ("qk_root", "lt_ready", "lt_turned", "qkrope_ready", "kn_ready"))
        va_turned, va_ready = sem("va_turned"), sem("va_ready")
        sc_ready, nb_ready, probs_ready, a_ready = sem("sc_ready"), sem("nb_ready"), sem("probs_ready"), sem("a_ready")
        a_turned, at_ready, o_done, o_ready, osq_ready, oroot = (sem(n) for n in ("a_turned", "at_ready", "o_done", "o_ready", "osq_ready", "oroot"))
        os_ready, o_turned = sem("os_ready"), sem("o_turned")
        lam_sums, lam_exp, attn_set = sem("lam_sums"), sem("lam_exp"), sem("attn_set")
        out_turned, out_copied = sem("out_turned"), sem("out_copied")
        pool_passed, scalar_passed, tensor_passed = sem("pool_passed"), sem("scalar_passed"), sem("tensor_passed")

        block = ctx.enter_context(nc.Block())

        @block.sync
        def _(sp):
            def weights(n, slot, src, k=KT, wait=True):
                if wait:
                    sp.wait_ge(w_split, n - 1)
                sp.dma_start(raw[:, slot, 0:k * P].rearrange("p (k c) -> p k c", k=k),
                             src).then_inc(raw_in[slot], 16)

            def cols(w, c):
                return w.rearrange("(k p) n -> p k n", p=P)[:, :, bass.ds(c, P)]

            def mlstm_cols(hd, j):
                qk, v = M_HEADS * M_DK, M_HEADS * M_DV
                return cols(m_w_in[0], (hd * M_DK, qk + hd * M_DK, 2 * qk + hd * M_DV, 2 * qk + hd * M_DV + P,
                                        2 * qk + v + hd * M_DV, 2 * qk + v + hd * M_DV + P)[j])

            def out_blocks(n0, w):
                with sp.Fori(0, KT // 2) as i:
                    for j in range(2):
                        weights(n0 + 2 * i + j, j, cols(w, i * (2 * P) + j * P))

            def ffn_blocks(n0, layer):
                w_in, w_out = ffn_w_in[layer], ffn_w_out[layer]
                at_tile = 0
                for tiles in GROUPS:
                    with sp.Fori(0, tiles) as i:
                        for j in range(2):
                            weights(n0 + 2 * i + j, j, cols(w_in, i * P + (at_tile * P + j * FF)))
                    n0 += 2 * tiles
                    rows = w_out[at_tile * P:(at_tile + tiles) * P, :]
                    with sp.Fori(0, KT // 2) as i:
                        for j in range(2):
                            weights(n0 + 2 * i + j, j, cols(rows, i * (2 * P) + j * P), tiles)
                    n0 += KT
                    at_tile += tiles

            sp.dma_start(cst[:, :], consts).then_inc(consts_in, 16)
            for r in range(XT):
                src = x_prompt[0, r * P:(r + 1) * P, :] if r < 4 else x_sample[0, (r - 4) * P:(r - 3) * P, :]
                sp.dma_start(wkf[:, r * D:(r + 1) * D], src).then_inc(x_in[r], 16)
                if r == 0:
                    sp.dma_start(wkf[0:META, XT * D:(XT + 1) * D], meta_tokens).then_inc(meta_in, 16)
                    sp.wait_ge(pool_set, 1)
                    for at_row, src in ((MIXN, norm_mix.rearrange("l (k p) -> (l k) p", p=P)),
                                        (FFNN, norm_ffn.rearrange("l (k p) -> (l k) p", p=P)),
                                        (GHEAD, m_g_head[0].rearrange("(k p) -> k p", p=P)), (GSUB, d_g_sub)):
                        sp.dma_start(prow[at_row:at_row + src.shape[0], :], src).then_inc(params_in, 16)
                    for at_row, src in ((GQ, d_g_q), (GK, d_g_k)):
                        for c in range(2):
                            sp.dma_start(prow[at_row:at_row + 1, c * D_HD:(c + 1) * D_HD], src).then_inc(params_in, 16)
                    for g in range(4):
                        sp.dma_start(prow[BGATE:BGATE + 1, 32 * g:32 * g + M_HEADS],
                                     m_b_gate[:, M_HEADS * g:M_HEADS * (g + 1)]).then_inc(params_in, 16)
                    with nc.allow_non_contiguous_dma(reason="16 gate columns"):
                        sp.dma_start(graw[:, :, :], m_w_in[0].rearrange("(k p) n -> p k n", p=P)[:, :, GATE_COLS:GATE_COLS + 16])\
                          .then_inc(gate_in, 16)
            for j in range(6):
                weights(MIX0 + j, j % 2, mlstm_cols(0, j), wait=j >= 2)
            with sp.Fori(1, M_HEADS) as hd:
                for j in range(6):
                    weights(MIX0 + hd * 6 + j, j % 2, mlstm_cols(hd, j))
            out_blocks(OUT0, m_w_out[0])
            ffn_blocks(FFN0, 0)
            with sp.Fori(0, D_HEADS // 2) as i:
                for j in range(6):
                    weights(MIX1 + i * 6 + j, j % 2, cols(d_w_in[0], i * (2 * P) + (j // 3) * P + (j % 3) * D))
            out_blocks(OUT1, d_w_out[0])
            ffn_blocks(FFN1, 1)
            for r in range(XT):
                dst = y_prompt[0, r * P:(r + 1) * P, :] if r < 4 else y_sample[0, (r - 4) * P:(r - 3) * P, :]
                sp.wait_ge(out_copied, r + 1)
                sp.dma_start(dst, wkf[:, r * D:(r + 1) * D]).then_inc(out_done, 16)
            sp.wait_ge(out_done, 16 * XT)

        @block.gpsimd
        def _(pool):
            pool.memset(prow[:, :], 0.0).then_inc(pool_set, 1)
            pool.memset(gwh[:, :, :].bitcast(F32), 0.0).then_inc(pool_set, 1)
            pool.memset(gwl[:, :, :].bitcast(F32), 0.0).then_inc(pool_set, 1)
            pool.wait_ge(pool_set, 3)
            pool.wait_ge(gate_in, 16)
            spread = [x[:, :, :].rearrange("p k (g c) -> p k g c", g=4)[:, :, :, 0:M_HEADS] for x in (gwh, gwl)]
            source = graw[:, :, :].rearrange("p k (g c) -> p k g c", g=4)
            for k in range(KT):
                pool.tensor_copy(spread[0][:, k], source[:, k]).then_inc(gate_split, 1)
            pool.wait_ge(gate_split, KT)
            for k in range(KT):
                pool.tensor_tensor(spread[1][:, k], source[:, k], spread[0][:, k].bitcast(F32),
                                   ALU.subtract).then_inc(gate_split, 1)

            def split(n, slot, times, wait=True):
                if wait:
                    pool.wait_ge(block_done, n - 1)
                pool.wait_ge(raw_in[slot], 16 * times)
                pool.sem_inc(pool_passed, 1)
                pool.tensor_copy(wh[:, slot, :], raw[:, slot, :]).then_inc(w_hi, 1)
                pool.wait_ge(w_hi, n + 1)
                pool.tensor_tensor(wl[:, slot, :], raw[:, slot, :], wh[:, slot, :].bitcast(F32),
                                   ALU.subtract).then_inc(w_split, 1)

            for slot in range(2):
                split(slot, slot, 1, wait=False)
            with pool.Fori(1, BLOCKS // 2) as i:
                for slot in range(2):
                    split(i * 2 + slot, slot, i + 1)

        @block.tensor
        def _(pe):
            def products(n, slot, p, k, xs):
                first = k == 0
                for w, x in ((wh, xs[0]), (wh, xs[1]), (wl, xs[0])):
                    for half in range(2):
                        yield dict(out=ps[:, 2 * p + half, 0:HT], lhsT=w[:, slot, k * P:(k + 1) * P],
                                   rhs=x[:, k, half * HT:(half + 1) * HT], start=first)
                    first = False

            def run_block(n, slot, p, xs=(xh, xl), k_tiles=KT, between={}):
                pe.wait_ge(w_split, n + 1)
                pe.wait_ge(acc_free, n + XT - 1)
                for k in range(k_tiles):
                    todo = list(products(n, slot, p, k, xs))
                    for q, a in enumerate(todo):
                        mm = pe.matmul(a["out"], a["lhsT"], a["rhs"], start=a["start"],
                                       stop=(k == k_tiles - 1 and q >= len(todo) - 2), skip_group_check=True)
                    if k == k_tiles - 1:
                        mm.then_inc(block_done, 1)
                    for f in between.get(k, ()):
                        f()

            def sum_squares(count):
                pe.wait_ge(sq_summed, KT * count)
                for half in range(2):
                    mm = pe.matmul(ps[:, 6 + half, 0:HT], ones[:, :], wk[:, 6, half * HT:(half + 1) * HT],
                                   start=True, stop=True)
                mm.then_inc(norm_sum, 1)

            def out_blocks(n0):
                pe.wait_ge(yl_ready, YL_AT[n0])
                with pe.Fori(0, KT // 2) as i:
                    for j in range(2):
                        run_block(n0 + 2 * i + j, j, j, (yh, yl))

            def ffn(n0, layer):
                pe.wait_ge(xl_ready, KT * (2 * layer + 2))
                sum_squares(2 * layer + 2)
                y = YL_AT[n0]
                for tiles in GROUPS:
                    with pe.Fori(0, tiles) as i:
                        for j in range(2):
                            run_block(n0 + 2 * i + j, j, j)
                    n0 += 2 * tiles
                    y += tiles
                    pe.wait_ge(yl_ready, y)
                    with pe.Fori(0, KT // 2) as i:
                        for j in range(2):
                            run_block(n0 + 2 * i + j, j, j, (yh, yl), tiles)
                    n0 += KT

            pe.wait_ge(consts_in, 16)
            for r in range(XT):
                pe.wait_ge(x_in[r], 16)
                if r >= 2:
                    pe.wait_ge(acc_free, r - 1)
                for k in range(KT):
                    mm = pe.transpose(flat(r % 2)[:, k * P:(k + 1) * P], wkf[:, r * D + k * P:r * D + (k + 1) * P], ident)
                mm.then_inc(x_turned, 1)
                if r == 0:
                    pe.wait_ge(meta_in, 16)
                    for k in range(KT):
                        mm = pe.transpose(ps[:, 4, k * META:(k + 1) * META],
                                          wkf[0:META, XT * D + k * P:XT * D + (k + 1) * P], ident[0:META, 0:META])
                    mm.then_inc(meta_turned, 1)
                    pe.wait_ge(params_in, 16 * 12)
                    pe.transpose(ps[:, 5, 0:NPAR], prow[:, :], ident[0:NPAR, 0:NPAR]).then_inc(par_turned, 1)

            pe.wait_ge(gate_split, 2 * KT)
            pe.wait_ge(par_ready, 1)
            pe.wait_ge(h_ready, 2)
            for k in range(KT):
                pe.wait_ge(xl_ready, k + 1)
                first = k == 0
                for w, x in ((gwh, xh), (gwh, xl), (gwl, xh)):
                    for half in range(2):
                        mm = pe.matmul(ps[:, 4 + half, 0:HT], w[:, k, :], x[:, k, half * HT:(half + 1) * HT],
                                       start=first, stop=(k == KT - 1 and w is gwl), skip_group_check=True)
                    first = False
            mm.then_inc(gates_done, 1)
            sum_squares(1)

            with pe.Fori(0, M_HEADS) as hd:
                n = MIX0 + hd * 6

                def repeat_m():
                    pe.wait_ge(mrow_masked, hd + 1)
                    for d in range(2):
                        for half in range(2):
                            mm = pe.matmul(ps[:, 4 + 2 * d + half, 0:HT], ones[64 * d:64 * d + 32, :],
                                           wk[64 * d:64 * d + 32, 4, half * HT:(half + 1) * HT], start=True, stop=True)
                    mm.then_inc(mrep_done, 1)

                def turn_ce():
                    pe.wait_ge(mrep_ready, hd * 2 + 2)
                    pe.wait_ge(gate_e, 2)
                    for i, (_, t0, tz) in enumerate(TILES):
                        mm = pe.transpose(flat(2)[0:tz, i * P:(i + 1) * P], cerow[:, t0:t0 + tz], ident)
                    mm.then_inc(ce_turned, 1)

                def turn_v():
                    pe.wait_ge(ce_ready, hd * 4 + 4)
                    pe.wait_ge(acc_free, n + XT + 4)
                    for i, (_, t0, tz) in enumerate(TILES):
                        at_col = (i if i < 4 else {5: 4, 6: 5, 4: 6, 7: 7}[i]) * M_DV
                        for c in range(2):
                            mm = pe.transpose(flat(2)[0:tz, at_col + c * P:at_col + (c + 1) * P],
                                              wk[:, 6 + c, t0:t0 + tz], ident)
                    mm.then_inc(v_turned, 1)

                def scores(j):
                    s, t0, tz = TILES[j]
                    if j == 0:
                        pe.wait_ge(vn_ready, hd * 3 + 3)
                    elif j == 5:
                        pe.wait_ge(hn_ready, hd * 8 + 5)
                    elif j not in (1, 6):
                        pe.wait_ge(wt_ready, hd * 8 + (j - 1))
                    for a in range(0, LENS[s], 512):
                        b = min(a + 512, LENS[s])
                        mm = pe.matmul(flat(2 + 0)[0:tz, (j % 2) * 1024 + a:(j % 2) * 1024 + b], wk[:, 1, t0:t0 + tz],
                                       wk[:, 0, START[s] + a:START[s] + b], start=True, stop=True)
                    mm.then_inc(s_ready, 1)

                def read_state(i):
                    s, t0, tz = TILES[i]
                    tiles, a = OF_SEQ[s], t0 - START[s]
                    if i == tiles[0]:
                        pe.wait_ge(wt_ready, hd * 8 + (tiles[-1] + 1))
                    elif i not in (1, 6):
                        pe.wait_ge(hn_ready, hd * 8 + (i - 1))
                    for d in range(2):
                        js = [j for j in tiles if (j <= i if d == 0 else j >= i)]
                        for j in js:
                            sz = TILES[j][2]
                            off = a + (sz if d == 0 else 0)
                            mm = pe.matmul(ps[0:tz, 4 + 2 * (i % 2) + d, 0:M_DV + 1],
                                           wt[0:sz, j - tiles[0], off:off + tz], vn[0:sz, j, :],
                                           start=(j == js[0]), stop=(j == js[-1]))
                    mm.then_inc(pv_done, 1)

                run_block(n, 0, 0)
                run_block(n + 1, 1, 1, between={3: [repeat_m]})
                run_block(n + 2, 0, 0, between={3: [turn_ce]})
                run_block(n + 3, 1, 1)
                turn_v()
                run_block(n + 4, 0, 0, between={j: [lambda j=j: scores(j)] for j in range(5)})
                for i in OF_SEQ[0]:
                    read_state(i)
                run_block(n + 5, 1, 1, between={0: [lambda: scores(5)], 1: [lambda: scores(6)], 2: [lambda: scores(7)],
                                                4: [lambda i=i: read_state(i) for i in OF_SEQ[1]]})
                for c in range(2):
                    pe.wait_ge(hs_ready, hd + 1)
                    for i, (_, t0, tz) in enumerate(TILES):
                        mm = pe.transpose(flat(2)[:, c * 1024 + t0:c * 1024 + t0 + tz],
                                          hn(i)[0:tz, c * P:(c + 1) * P], ident[0:tz, 0:tz])
                    mm.then_inc(y_turned, 1)

            out_blocks(OUT0)
            ffn(FFN0, 0)

            pe.wait_ge(xl_ready, KT * 3)
            sum_squares(3)
            pe.wait_ge(attn_set, ATTN_SET)
            with pe.Fori(0, D_HEADS // 2) as it:
                for sub in range(2):
                    hd = it * 2 + sub
                    n = MIX1 + it * 6 + 3 * sub

                    def rotate(which):
                        pe.wait_ge(acc_free, n + XT + 1 + which)
                        if which == 0:
                            pe.wait_ge(yt_ready, hd + YL_AT[MIX1])
                        else:
                            pe.wait_ge(rot_free, hd * 2 + 1)
                        for half in range(2):
                            mm = pe.matmul(ps[:, 4 + half, 0:HT], (permq, permk)[which][:, :],
                                           wk[:, which, half * HT:(half + 1) * HT], start=True, stop=True)
                        mm.then_inc(rot_done, 1)

                    def square_sums(which):
                        pe.wait_ge(qsq_ready, hd * 2 + which + 1)
                        for i, (_, t0, tz) in enumerate(TILES):
                            mm = pe.matmul(ps[:, 6, i * 4 + 2 * which:i * 4 + 2 * which + 2], sqp[:, t0:t0 + P],
                                           cst[:, COMP:COMP + 2], start=True, stop=True, skip_group_check=True)
                        mm.then_inc(qks_done, 1)

                    def attn_scores(i):
                        s, t0, tz = TILES[i]
                        for c in range(2):
                            if i:
                                pe.wait_ge(probs_ready, hd * 16 + (2 * i - 1 + c))
                                if tz < P:
                                    pe.sem_inc(tensor_passed, 1)
                            rows = slice(D_HD * c, D_HD * (c + 1))
                            for a in range(0, LENS[s], 512):
                                b = min(a + 512, LENS[s])
                                mm = pe.matmul(flat(c)[0:tz, a:b], wk[rows, 0, t0:t0 + tz],
                                               wk[rows, 1, START[s] + a:START[s] + b], start=True, stop=True)
                            mm.then_inc(sc_ready, 1)

                    def turn_attention(i):
                        s, t0, tz = TILES[i]
                        pe.wait_ge(a_ready, hd * 8 + (i + 1))
                        if i:
                            pe.wait_ge(at_ready, hd * 8 + i)
                        else:
                            pe.wait_ge(kn_ready, hd + 1)
                        if tz < P:
                            pe.sem_inc(tensor_passed, 1)
                        for q, j in enumerate(OF_SEQ[s]):
                            sz = TILES[j][2]
                            mm = pe.transpose(flat(2)[0:sz, q * P:q * P + tz], prob(i, 0)[0:tz, q * P:q * P + sz],
                                              ident[0:tz, 0:tz])
                        mm.then_inc(a_turned, 1)

                    def attend(i):
                        s, t0, tz = TILES[i]
                        pe.wait_ge(at_ready, hd * 8 + (i + 1))
                        if i >= 2:
                            pe.wait_ge(o_ready, hd * 8 + (i - 1))
                        elif i == 0:
                            pe.wait_ge(va_ready, hd * 2 + 2)
                        for q, j in enumerate(OF_SEQ[s]):
                            sz = TILES[j][2]
                            mm = pe.matmul(ps[0:tz, 6 + i % 2, 0:P], at[0:sz, i % 2, q, 0:tz], va[0:sz, j, :],
                                           start=(q == 0), stop=(j == OF_SEQ[s][-1]))
                        mm.then_inc(o_done, 1)

                    run_block(n, (3 * sub) % 2, 0)
                    run_block(n + 1, (3 * sub + 1) % 2, 1, between={4: [lambda: rotate(0)], 5: [lambda: square_sums(0)]})
                    run_block(n + 2, (3 * sub + 2) % 2, 0, between={4: [lambda: rotate(1)], 5: [lambda: square_sums(1)]})
                    pe.wait_ge(acc_free, n + XT + 3)
                    pe.wait_ge(qk_root, hd * 1 + 1)
                    for i, (_, t0, tz) in enumerate(TILES):
                        at_col = (i if i < 4 else {5: 4, 6: 5, 4: 6, 7: 7}[i]) * P
                        mm = pe.transpose(flat(3)[0:tz, at_col:at_col + P], wk[:, 5, t0:t0 + tz], ident)
                    mm.then_inc(va_turned, 1)
                    pe.wait_ge(lt_ready, hd + 1)
                    pe.wait_ge(rot_free, hd * 2 + 2)
                    for i, (_, t0, tz) in enumerate(TILES):
                        mm = pe.transpose(flat(2)[:, t0:t0 + tz], ltile(i)[0:tz, :], ident[0:tz, 0:tz])
                    mm.then_inc(lt_turned, 1)
                    pe.wait_ge(kn_ready, hd + 1)
                    attn_scores(0)
                    for i in range(NT + 1):
                        if i + 1 < NT:
                            attn_scores(i + 1)
                        if i >= 1:
                            attend(i - 1)
                        if i < NT:
                            turn_attention(i)
                    pe.wait_ge(os_ready, hd + 1)
                    pe.wait_ge(at_ready, hd * 8 + 8)
                    for i, (_, t0, tz) in enumerate(TILES):
                        mm = pe.transpose(flat(2)[:, t0:t0 + tz], on(i)[0:tz, :], ident[0:tz, 0:tz])
                    mm.then_inc(o_turned, 1)

            out_blocks(OUT1)
            ffn(FFN1, 1)

            pe.wait_ge(acc_free, BLOCKS + XT)
            for r in range(XT):
                t0 = META + r * P if r < 4 else LENS[0] + META + (r - 4) * P
                if r >= 2:
                    pe.wait_ge(out_copied, r - 1)
                for k in range(KT):
                    mm = pe.transpose(flat(r % 2)[:, k * P:(k + 1) * P], h[:, k, t0:t0 + P], ident)
                mm.then_inc(out_turned, 1)

        @block.vector
        def _(ve):
            v = Steps(ve, vstep)

            def evacuate(n, p, dst):
                ve.wait_ge(block_done, n + 1)
                ve.tensor_tensor(two(dst), pair(p), two(rstd[:, :]), ALU.mult).then_inc(acc_free, 1)

            def split_low(src, dst_h, dst_l, ready, done):
                ve.wait_ge(yh_ready, ready)
                ve.tensor_tensor(dst_l, src, dst_h.bitcast(F32), ALU.subtract).then_inc(done, 1)

            def fold(count, k, gain):
                ve.wait_ge(xh_ready, count + 1)
                ve.scalar_tensor_tensor(xl[:, k, :], h[:, k, :], gain, xh[:, k, :].bitcast(F32),
                                        ALU.mult, ALU.subtract).then_inc(xl_ready, 1)

            def add_square(count, src, first):
                ve.wait_ge(sq_ready, count + 1)
                if first:
                    ve.tensor_copy(wk[:, 6, :], wk[:, src, :]).then_inc(sq_summed, 1)
                else:
                    ve.wait_ge(sq_summed, count)
                    ve.tensor_tensor(wk[:, 6, :], wk[:, 6, :], wk[:, src, :], ALU.add).then_inc(sq_summed, 1)

            def invert(count):
                ve.wait_ge(norm_root, count)
                ve.reciprocal(rstd[:, :], rstd[:, :]).then_inc(rstd_ready, 1)
                ve.wait_ge(rstd_ready, count)

            def out_blocks(n0, norm, gain_at):
                if norm is not None:
                    ve.memset(wk[:, 6, :], 0.0).then_inc(ones_set, 1)
                    ve.wait_ge(ones_set, 1 + norm)
                with ve.Fori(0, KT // 2) as i:
                    for j in range(2):
                        m = i * 2 + j
                        ve.wait_ge(block_done, n0 + m + 1)
                        hm = h[:, bass.ds(m, 1), :].rearrange("p a b -> p (a b)")
                        ve.tensor_tensor(two(hm), two(hm), pair(j), ALU.add).then_inc(acc_free, 1)
                        if norm is not None:
                            c = m + KT * norm
                            ve.wait_ge(xh_ready, c + 1)
                            ve.scalar_tensor_tensor(
                                xl[:, bass.ds(m, 1), :].rearrange("p a b -> p (a b)"), hm,
                                par[:, bass.ds(m + gain_at, 1)],
                                xh[:, bass.ds(m, 1), :].rearrange("p a b -> p (a b)").bitcast(F32),
                                ALU.mult, ALU.subtract).then_inc(xl_ready, 1)
                            ve.wait_ge(sq_ready, c + 1)
                            ve.wait_ge(sq_summed, c)
                            ve.tensor_tensor(wk[:, 6, :], wk[:, 6, :], wk[:, 7, :], ALU.add).then_inc(sq_summed, 1)
                if norm is not None:
                    invert(norm + 1)

            def ffn(n0, layer):
                y0 = YL_AT[n0]
                for g, tiles in enumerate(GROUPS):
                    with ve.Fori(0, tiles) as i:
                        ft = y0 - YL_AT[FFN0] + i if layer == 0 else y0 - YL_AT[FFN1] + FT + i
                        evacuate(n0 + 2 * i, 0, wk[:, 0, :])
                        evacuate(n0 + 2 * i + 1, 1, wk[:, 2, :])
                        ve.wait_ge(silu_ready, ft + 1)
                        ve.wait_ge(acc_free, n0 + 2 * i + 2 + XT)
                        ve.wait_ge(yl_ready, y0 + i)
                        ve.tensor_tensor(wk[:, 3, :], wk[:, 1, :], wk[:, 2, :], ALU.mult).then_inc(yt_ready, 1)
                        split_low(wk[:, 3, :], yh[:, bass.ds(i, 1), :].rearrange("p a b -> p (a b)"),
                                  yl[:, bass.ds(i, 1), :].rearrange("p a b -> p (a b)"), y0 + i + 1, yl_ready)
                    n0 += 2 * tiles
                    y0 += tiles
                    last = g == len(GROUPS) - 1
                    out_blocks(n0, {0: 2, 1: None}[layer] if last else None, MIXN + KT)
                    n0 += KT

            ve.memset(ones[:, :], 1.0).then_inc(ones_set, 1)
            v(ve.memset(epsc, EPS))
            v(ve.memset(ss[:, :], 1.0))
            for r in range(XT):
                t0 = META + r * P if r < 4 else LENS[0] + META + (r - 4) * P
                ve.wait_ge(x_turned, r + 1)
                ve.tensor_copy(h[:, :, t0:t0 + P], flat(r % 2).rearrange("p (k c) -> p k c", k=KT)).then_inc(acc_free, 1)
                if r == 0:
                    ve.wait_ge(meta_turned, 1)
                    for s in range(2):
                        ve.tensor_copy(h[:, :, START[s]:START[s] + META],
                                       ps[:, 4, 0:KT * META].rearrange("p (k c) -> p k c", k=KT)).then_inc(h_ready, 1)
                    ve.wait_ge(par_turned, 1)
                    ve.tensor_copy(par[:, :], ps[:, 5, 0:NPAR]).then_inc(par_ready, 1)
            ve.wait_ge(acc_free, XT)
            ve.wait_ge(h_ready, 2)
            ve.wait_ge(par_ready, 1)
            for k in range(KT):
                fold(k, k, par[:, MIXN + k:MIXN + k + 1])
                add_square(k, 7, k == 0)
            invert(1)

            ve.wait_ge(gates_done, 1)
            v(ve.tensor_tensor(two(wk[:, 0, :]), pair(2), two(rstd[:, :]), ALU.mult))
            v.wait()
            ve.tensor_scalar(wk[:, 0, :], wk[:, 0, :], par[:, BGATE:BGATE + 1], None, ALU.add).then_inc(gate_x, 1)
            v(ve.memset(wk[:, 4, :], 0.0))
            v(ve.memset(mrow[:, :], 0.0))
            v(ve.memset(vn[:, :, M_DV:M_DV + 1], 1.0))
            ve.wait_ge(gate_soft, 1)
            ve.wait_ge(gate_x, 1)
            v(ve.scalar_tensor_tensor(wk[:, 3, :], wk[:, 0, :], 0.0, wk[:, 5, :], ALU.min, ALU.subtract))
            v.wait()

            def span(s, back):
                a, b = START[s], START[s] + LENS[s]
                return slice(a, b) if not back else slice(b - 1, a - 1 if a else None, -1)

            for s in range(2):
                zero = small[:, 1:2]
                if s == 0:
                    v(ve.memset(zero, 0.0))
                    v.wait()
                for d in range(2):
                    src, dst = slice(32 + 64 * d, 36 + 64 * d), slice(64 * d, 64 * d + M_HEADS)
                    v(ve.tensor_tensor_scan(wk[dst, 4, span(s, d)], wk[src, 3, span(s, d)],
                                            small[src, 1:2].to_broadcast([M_HEADS, LENS[s]]), 0.0, ALU.add, ALU.add))
            v.wait()
            v(ve.tensor_tensor(cerow, wk[:, 0, :], wk[:, 4, :], ALU.subtract))
            v.wait()
            for s in range(2):
                for d in range(2):
                    rows = slice(64 * d, 64 * d + M_HEADS)
                    v(ve.tensor_tensor_scan(mrow[rows, span(s, d)], cerow[rows, span(s, d)],
                                            small[rows, 1:2].to_broadcast([M_HEADS, LENS[s]]), 0.0, ALU.max, ALU.add))
            v.wait()
            ve.tensor_tensor(wk[:, 5, :], wk[:, 4, :], mrow[:, :], ALU.add).then_inc(gate_m, 1)

            with ve.Fori(0, M_HEADS) as hd:
                v.loop_start(hd, M_PER)
                n = MIX0 + hd * 6
                ve.wait_ge(gate_m, 1)
                evacuate(n, 0, wk[:, 0, :])
                ve.tensor_scalar(wk[:, 4, :], mrow[:, :], cst[:, bass.ds(hd + ONEHOT, 1)], None, ALU.mult)\
                  .then_inc(mrow_masked, 1)
                evacuate(n + 1, 1, wk[:, 1, :])
                ve.wait_ge(ce_turned, hd + 1)
                turned = flat(2).rearrange("p (i g c) -> p i g c", i=2 * NT, g=4)
                for a, b, rows in ((0, 4, P), (5, 7, P), (4, 5, META), (7, 8, META)):
                    ve.tensor_copy(ce[0:rows, a:b, :],
                                   turned[0:rows, a:b, :, bass.ds(hd, 1)].rearrange("p i g c -> p i (g c)"))\
                      .then_inc(ce_ready, 1)
                evacuate(n + 2, 0, wk[:, 6, :])
                evacuate(n + 3, 1, wk[:, 7, :])

                def diagonals(j):
                    s, t0, tz = TILES[j]
                    q, a = j - OF_SEQ[s][0], t0 - START[s]
                    for d, mask in ((0, MASKF), (1, MASKB)):
                        off = a + (tz if d == 0 else 0)
                        ve.tensor_tensor(wt[0:tz, q, off:off + tz], wk[0:tz, 2 + d, t0:t0 + tz],
                                         cst[0:tz, mask:mask + tz], ALU.add).then_inc(diag_ready, 1)

                def state_weights(j):
                    s, t0, tz = TILES[j]
                    q, a = j - OF_SEQ[s][0], t0 - START[s]
                    ve.wait_ge(s_ready, hd * 8 + (j + 1))
                    ve.wait_ge(e_ready, hd * 8 + (j + 1))
                    base = (j % 2) * 1024
                    fwd = wt[0:tz, q, a + tz:LENS[s] + tz]
                    bwd = wt[0:tz, q, 0:a + tz]
                    v(ve.scalar_tensor_tensor(fwd, flat(2)[0:tz, base + a:base + LENS[s]], M_DK ** -0.5, fwd,
                                              ALU.mult, ALU.mult))
                    ve.scalar_tensor_tensor(bwd, flat(2)[0:tz, base:base + a + tz], M_DK ** -0.5, bwd,
                                            ALU.mult, ALU.mult).then_inc(wt_ready, 1)

                def normalise(i):
                    s, t0, tz = TILES[i]
                    ve.wait_ge(pv_done, hd * 8 + (i + 1))
                    den = [ps[0:tz, 4 + 2 * (i % 2) + d, M_DV:M_DV + 1] for d in range(2)]
                    low = [dd[0:tz, i % 2, d:d + 1] for d in range(2)]
                    for d in range(2):
                        v(ve.tensor_scalar(low[d], den[d], -1.0, ce[0:tz, i, 2 * d + 1:2 * d + 2], ALU.mult, ALU.max))
                    v.wait()
                    for d in range(2):
                        v(ve.tensor_scalar(low[d], den[d], low[d], None, ALU.max))
                    v.wait()
                    v(ve.reciprocal(rd[0:tz, i % 2, :], dd[0:tz, i % 2, :]))
                    v.wait()
                    v(ve.tensor_scalar(hn(i)[0:tz, :], ps[0:tz, 4 + 2 * (i % 2), 0:M_DV], rd[0:tz, i % 2, 0:1], None,
                                       ALU.mult))
                    v.wait()
                    ve.scalar_tensor_tensor(hn(i)[0:tz, :], ps[0:tz, 5 + 2 * (i % 2), 0:M_DV], rd[0:tz, i % 2, 1:2],
                                            hn(i)[0:tz, :], ALU.mult, ALU.add).then_inc(hn_ready, 1)

                ve.wait_ge(mrep_ready, hd * 2 + 2)
                for j in OF_SEQ[0]:
                    diagonals(j)
                for j in OF_SEQ[0]:
                    state_weights(j)
                evacuate(n + 4, 0, wk[:, 4, :])
                for i in OF_SEQ[0]:
                    normalise(i)
                for j in OF_SEQ[1]:
                    diagonals(j)
                for j in OF_SEQ[1]:
                    state_weights(j)
                for i in OF_SEQ[1]:
                    normalise(i)
                evacuate(n + 5, 1, wk[:, 5, :])
                ve.wait_ge(hroot, hd + 1)
                v(ve.reciprocal(rs[:, :], rs[:, :]))
                v.wait()
                ve.wait_ge(hn_ready, hd * 8 + 8)
                for i, (_, t0, tz) in enumerate(TILES):
                    ins = ve.tensor_scalar(hn(i)[0:tz, :], hn(i)[0:tz, :], rs[0:tz, i:i + 1], None, ALU.mult)
                ins.then_inc(hs_ready, 1)
                for c in range(2):
                    ve.wait_ge(y_turned, hd * 2 + (c + 1))
                    ve.wait_ge(sig_ready, hd * 2 + (c + 1))
                    ve.scalar_tensor_tensor(wk[:, c, :], flat(2)[:, c * 1024:c * 1024 + T],
                                            par[:, GHEAD + c:GHEAD + c + 1], wk[:, 4 + c, :],
                                            ALU.mult, ALU.mult).then_inc(yt_ready, 1)
                for c in range(2):
                    split_low(wk[:, c, :], yh[:, bass.ds(hd * 2 + c, 1), :].rearrange("p a b -> p (a b)"),
                              yl[:, bass.ds(hd * 2 + c, 1), :].rearrange("p a b -> p (a b)"), hd * 2 + (c + 1), yl_ready)
                ve.wait_ge(yl_ready, hd * 2 + 2)
            v.loop_end(M_HEADS, M_PER)

            out_blocks(OUT0, 1, FFNN)
            ve.wait_ge(rope_in, 32)
            ve.tensor_scalar(cq[:, :], ck[:, :], par[:, GQ:GQ + 1], None, ALU.mult).then_inc(attn_set, 1)
            ve.wait_ge(attn_set, 1)
            ve.tensor_scalar(ck[:, :], ck[:, :], par[:, GK:GK + 1], None, ALU.mult).then_inc(attn_set, 1)
            for g, dst in ((GQ, permq), (GK, permk)):
                ve.tensor_scalar(dst[:, :], cst[:, PERM:PERM + P], par[:, g:g + 1], None, ALU.mult).then_inc(attn_set, 1)
            ve.tensor_scalar(gsub[:, :], par[:, GSUB:GSUB + 1], 1.0 - LAMBDA_INIT, None, ALU.mult).then_inc(attn_set, 1)
            ve.wait_ge(lam_in, 64)
            for q in range(2):
                ve.tensor_tensor_reduce(lv[:, 2 * q, :], lv[:, 2 * q, :], lv[:, 2 * q + 1, :], 1.0, 0.0,
                                        ALU.mult, ALU.add, lam[:, q:q + 1]).then_inc(lam_sums, 1)
            ve.wait_ge(lam_exp, 1)
            v(ve.tensor_tensor(lam[:, 6:7], lam[:, 5:6], lam[:, 4:5], ALU.subtract))
            v.wait()
            ve.tensor_scalar(lam[:, 7:8], lam[:, 6:7], -LAMBDA_INIT, None, ALU.add).then_inc(attn_set, 1)
            ffn(FFN0, 0)
            ve.memset(sqp[:, T:T + P], 0.0).then_inc(attn_set, 1)
            ve.wait_ge(attn_set, ATTN_SET)

            with ve.Fori(0, D_HEADS // 2) as it:
                v.loop_start(it, A_PER)
                for sub in range(2):
                    hd = it * 2 + sub
                    n = MIX1 + it * 6 + 3 * sub

                    def rope_of(which):
                        tab = (cq, ck)[which]
                        ve.wait_ge(acc_free, n + XT + 1 + which)
                        v.wait()
                        v(ve.tensor_tensor(wk[:, 4, :], wk[:, which, :], tab[:, :], ALU.mult))
                        v.wait()
                        ve.wait_ge(rot_done, hd * 2 + (which + 1))
                        ve.wait_ge(qsq_ready, hd * 2 + (which + 1))
                        ve.tensor_tensor(two(wk[:, which, :]), pair(2), two(sn[:, :]), ALU.mult).then_inc(rot_free, 1)
                        ve.wait_ge(rot_free, hd * 2 + (which + 1))
                        v.wait()
                        v(ve.tensor_tensor(wk[:, which, :], wk[:, which, :], wk[:, 4, :], ALU.add))

                    def steps(i):
                        s, t0, tz = TILES[i]
                        for c in range(2):
                            ve.wait_ge(sc_ready, hd * 16 + (2 * i + c + 1))
                            v(ve.tensor_reduce(mx[0:tz, i, c:c + 1], flat(c)[0:tz, 0:LENS[s]], AX.X, ALU.max))
                            v.wait()
                            ve.tensor_scalar(nb[0:tz, i, c:c + 1], mx[0:tz, i, c:c + 1], qkr[0:tz, i, c:c + 1], -1.0,
                                             ALU.mult, ALU.mult).then_inc(nb_ready, 1)
                        if i >= 2:
                            output(i - 2)
                        ve.wait_ge(probs_ready, hd * 16 + (2 * i + 2))
                        v(ve.reciprocal(rsum[0:tz, i, :], sums[0:tz, i, :]))
                        v.wait()
                        v(ve.scalar_tensor_tensor(ratio[0:tz, i:i + 1], sums[0:tz, i, 0:1], lam[0:tz, 7:8],
                                                  rsum[0:tz, i, 1:2], ALU.mult, ALU.mult))
                        v.wait()
                        ve.scalar_tensor_tensor(prob(i, 0)[0:tz, 0:LENS[s]], prob(i, 1)[0:tz, 0:LENS[s]],
                                                ratio[0:tz, i:i + 1], prob(i, 0)[0:tz, 0:LENS[s]],
                                                ALU.mult, ALU.add).then_inc(a_ready, 1)

                    def output(i):
                        s, t0, tz = TILES[i]
                        ve.wait_ge(o_done, hd * 8 + (i + 1))
                        ve.tensor_scalar(on(i)[0:tz, :], ps[0:tz, 6 + i % 2, 0:P], rsum[0:tz, i, 0:1], None,
                                         ALU.mult).then_inc(o_ready, 1)

                    evacuate(n, 0, wk[:, 0, :])
                    rope_of(0)
                    evacuate(n + 1, 1, wk[:, 1, :])
                    rope_of(1)
                    evacuate(n + 2, 0, wk[:, 5, :])
                    ve.wait_ge(qk_root, hd + 1)
                    v(ve.reciprocal(qkr[:, :, :], qk2[:, :, :]))
                    v.wait()
                    ve.tensor_copy(lall, qkr[:, :, 2:4].unsqueeze(3).to_broadcast([P, NT, 2, D_HD])).then_inc(lt_ready, 1)
                    v(ve.tensor_scalar(qkr[:, :, 0:2], qkr[:, :, 0:2], D_HD ** -0.5, None, ALU.mult))
                    ve.wait_ge(lt_turned, hd + 1)
                    v.wait()
                    ve.tensor_tensor(wk[:, 1, :], flat(2)[:, 0:T], wk[:, 1, :], ALU.mult).then_inc(kn_ready, 1)
                    for i in range(NT):
                        steps(i)
                    output(NT - 2)
                    output(NT - 1)
                    ve.wait_ge(oroot, hd + 1)
                    v(ve.reciprocal(rs[:, :], rs[:, :]))
                    v.wait()
                    ve.wait_ge(o_ready, hd * 8 + 8)
                    for i, (_, t0, tz) in enumerate(TILES):
                        ins = ve.tensor_scalar(on(i)[0:tz, :], on(i)[0:tz, :], rs[0:tz, i:i + 1], None, ALU.mult)
                    ins.then_inc(os_ready, 1)
                    ve.wait_ge(o_turned, hd + 1)
                    ve.tensor_scalar(wk[:, 8, :], flat(2)[:, 0:T], gsub[:, 0:1], None, ALU.mult).then_inc(yt_ready, 1)
                    split_low(wk[:, 8, :], yh[:, bass.ds(hd, 1), :].rearrange("p a b -> p (a b)"),
                              yl[:, bass.ds(hd, 1), :].rearrange("p a b -> p (a b)"),
                              hd + (YL_AT[MIX1] + 1), yl_ready)
                v.loop_end(D_HEADS // 2, A_PER)
            out_blocks(OUT1, 3, FFNN + KT)
            ffn(FFN1, 1)
            for r in range(XT):
                ve.wait_ge(out_turned, r + 1)
                ve.tensor_copy(wkf[:, r * D:(r + 1) * D], flat(r % 2)).then_inc(out_copied, 1)

        @block.scalar
        def _(sc):
            def high(src, dst, ready, done=yh_ready):
                sc.wait_ge(yt_ready, ready)
                sc.sem_inc(scalar_passed, 1)
                sc.activation(dst, src, ACT.Copy).then_inc(done, 1)

            def root(count):
                sc.wait_ge(norm_sum, count)
                sc.activation(two(rstd[:, :]), pair(3), ACT.Sqrt, bias=epsc, scale=1.0 / D).then_inc(norm_root, 1)

            def out_blocks(n0, norm, gain_at):
                if norm is None:
                    return
                with sc.Fori(0, KT // 2) as i:
                    for j in range(2):
                        m = i * 2 + j
                        c = m + KT * norm
                        hm = h[:, bass.ds(m, 1), :].rearrange("p a b -> p (a b)")
                        sc.wait_ge(acc_free, n0 + m + 1 + XT)
                        sc.sem_inc(scalar_passed, 1)
                        sc.activation(xh[:, bass.ds(m, 1), :].rearrange("p a b -> p (a b)"), hm, ACT.Copy,
                                      scale=par[:, bass.ds(m + gain_at, 1)]).then_inc(xh_ready, 1)
                        sc.wait_ge(sq_summed, c)
                        sc.sem_inc(scalar_passed, 1)
                        sc.activation(wk[:, 7, :], hm, ACT.Square).then_inc(sq_ready, 1)
                root(norm + 1)

            def ffn(n0, layer):
                y0 = YL_AT[n0]
                for g, tiles in enumerate(GROUPS):
                    with sc.Fori(0, tiles) as i:
                        sc.wait_ge(acc_free, n0 + 2 * i + 1 + XT)
                        sc.activation(wk[:, 1, :], wk[:, 0, :], ACT.Silu).then_inc(silu_ready, 1)
                        high(wk[:, 3, :], yh[:, bass.ds(i, 1), :].rearrange("p a b -> p (a b)"), y0 + i + 1)
                    n0 += 2 * tiles
                    y0 += tiles
                    last = g == len(GROUPS) - 1
                    out_blocks(n0, {0: 2, 1: None}[layer] if last else None, MIXN + KT)
                    n0 += KT

            sc.wait_ge(acc_free, XT)
            sc.wait_ge(h_ready, 2)
            sc.wait_ge(par_ready, 1)
            for k in range(KT):
                sc.activation(xh[:, k, :], h[:, k, :], ACT.Copy, scale=par[:, MIXN + k:MIXN + k + 1]).then_inc(xh_ready, 1)
                if k:
                    sc.wait_ge(sq_summed, k)
                sc.activation(wk[:, 7, :], h[:, k, :], ACT.Square).then_inc(sq_ready, 1)
            root(1)

            a = Steps(sc, astep)
            sc.wait_ge(gate_x, 1)
            a(sc.activation(wk[:, 5, :], wk[:, 0, :], ACT.Abs))
            a.wait()
            a(sc.activation(wk[:, 5, :], wk[:, 5, :], ACT.Exp, scale=-1.0))
            a.wait()
            sc.wait_ge(ones_set, 1)
            sc.activation(wk[:, 5, :], wk[:, 5, :], ACT.Ln, bias=ones[:, 0:1]).then_inc(gate_soft, 1)
            sc.wait_ge(gate_m, 1)
            for d in range(2):
                sc.activation(cerow[32 + 64 * d:36 + 64 * d, :], wk[64 * d:64 * d + M_HEADS, 5, :], ACT.Exp,
                              scale=-1.0).then_inc(gate_e, 1)

            with sc.Fori(0, M_HEADS) as hd:
                sc.wait_ge(mrep_done, hd + 1)
                for d in range(2):
                    sc.activation(two(wk[:, 2 + d, :]), pair(2 + d), ACT.Copy).then_inc(mrep_ready, 1)
                sc.wait_ge(v_turned, hd + 1)
                sc.activation(vn[:, 0:4, 0:M_DV], flat(2)[:, 0:4 * M_DV].rearrange("p (i c) -> p i c", i=4),
                              ACT.Copy).then_inc(vn_ready, 1)
                sc.activation(vn[:, 5:7, 0:M_DV], flat(2)[:, 4 * M_DV:6 * M_DV].rearrange("p (i c) -> p i c", i=2),
                              ACT.Copy).then_inc(vn_ready, 1)
                sc.activation(vn[0:META, 4:8:3, 0:M_DV],
                              flat(2)[0:META, 6 * M_DV:8 * M_DV].rearrange("p (i c) -> p i c", i=2),
                              ACT.Copy).then_inc(vn_ready, 1)

                def decays(j):
                    s, t0, tz = TILES[j]
                    q, a = j - OF_SEQ[s][0], t0 - START[s]
                    first = OF_SEQ[s][0] if s else 0
                    sc.wait_ge(diag_ready, hd * 16 + (2 * j + 2))
                    ops = [(wt[0:tz, q, a + tz:a + 2 * tz], wt[0:tz, q, a + tz:a + 2 * tz], 0)]
                    if a + tz < LENS[s]:
                        ops.append((wt[0:tz, q, a + 2 * tz:LENS[s] + tz], wk[0:tz, 2, t0 + tz:START[s] + LENS[s]], 0))
                    if a:
                        ops.append((wt[0:tz, q, 0:a], wk[0:tz, 3, START[s]:t0], 1))
                    ops.append((wt[0:tz, q, a:a + tz], wt[0:tz, q, a:a + tz], 1))
                    for dst, src, d in ops:
                        ins = sc.activation(dst, src, ACT.Exp, bias=ce[0:tz, j, 2 * d:2 * d + 1], scale=-1.0)
                    ins.then_inc(e_ready, 1)

                def squares(i):
                    s, t0, tz = TILES[i]
                    sc.wait_ge(hn_ready, hd * 8 + (i + 1))
                    if i:
                        sc.wait_ge(hsq_ready, hd * 8 + i)
                    sc.activation(wkf[0:tz, 0:M_DV], hn(i)[0:tz, :], ACT.Square, accum_out=ss[0:tz, i:i + 1])\
                      .then_inc(hsq_ready, 1)

                sc.wait_ge(ce_ready, hd * 4 + 4)
                for j in OF_SEQ[0]:
                    decays(j)
                for i in OF_SEQ[0]:
                    squares(i)
                for j in OF_SEQ[1]:
                    decays(j)
                for i in OF_SEQ[1]:
                    squares(i)
                sc.wait_ge(hsq_ready, hd * 8 + 8)
                sc.activation(rs[:, :], ss[:, :], ACT.Sqrt, bias=epsc, scale=1.0 / M_DV).then_inc(hroot, 1)
                for c in range(2):
                    sc.wait_ge(acc_free, MIX0 + hd * 6 + (5 + c + XT))
                    sc.activation(wk[:, 4 + c, :], wk[:, 4 + c, :], ACT.Sigmoid).then_inc(sig_ready, 1)
                for c in range(2):
                    high(wk[:, c, :], yh[:, bass.ds(hd * 2 + c, 1), :].rearrange("p a b -> p (a b)"), hd * 2 + (c + 1))

            out_blocks(OUT0, 1, FFNN)
            sc.dma_start(ck[:, :], rope[:, 0, :]).then_inc(rope_in, 16)
            sc.dma_start(sn[:, :], rope[:, 1, :]).then_inc(rope_in, 16)
            for q, src in enumerate((d_lam_q1, d_lam_k1, d_lam_q2, d_lam_k2)):
                sc.dma_start(lv[:, q, :], src.to_broadcast([P, D_HD])).then_inc(lam_in, 16)
            sc.wait_ge(lam_sums, 2)
            sc.activation(lam[:, 4:6], lam[:, 0:2], ACT.Exp).then_inc(lam_exp, 1)
            ffn(FFN0, 0)

            with sc.Fori(0, D_HEADS // 2) as it:
                for sub in range(2):
                    hd = it * 2 + sub
                    n = MIX1 + it * 6 + 3 * sub
                    for which in range(2):
                        sc.wait_ge(acc_free, n + (XT + 1 + which))
                        if which:
                            sc.wait_ge(qks_done, hd * 2 + 1)
                        sc.activation(sqp[:, 0:T], wk[:, which, :], ACT.Square).then_inc(qsq_ready, 1)
                    sc.wait_ge(qks_done, hd * 2 + 2)
                    sc.activation(qk2[:, :, :].rearrange("p i c -> p (i c)"), ps[:, 6, 0:4 * NT], ACT.Sqrt,
                                  bias=epsc, scale=1.0 / D_HD).then_inc(qk_root, 1)
                    sc.wait_ge(va_turned, hd + 1)
                    sc.activation(va[:, 0:4, :], flat(3)[:, 0:4 * P].rearrange("p (i c) -> p i c", i=4), ACT.Copy)
                    sc.activation(va[:, 5:7, :], flat(3)[:, 4 * P:6 * P].rearrange("p (i c) -> p i c", i=2),
                                  ACT.Copy).then_inc(va_ready, 1)
                    sc.activation(va[0:META, 4:8:3, :], flat(3)[0:META, 6 * P:8 * P].rearrange("p (i c) -> p i c", i=2),
                                  ACT.Copy).then_inc(va_ready, 1)

                    def turned(i):
                        s, t0, tz = TILES[i]
                        sc.wait_ge(a_turned, hd * 8 + (i + 1))
                        full = len(OF_SEQ[s]) - 1
                        sc.activation(at[:, i % 2, 0:full, 0:tz],
                                      flat(2)[:, 0:full * P].rearrange("p (q c) -> p q c", q=full)[:, :, 0:tz], ACT.Copy)
                        sc.activation(at[0:META, i % 2, full, 0:tz], flat(2)[0:META, full * P:full * P + tz],
                                      ACT.Copy).then_inc(at_ready, 1)

                    def squared(i):
                        s, t0, tz = TILES[i]
                        sc.wait_ge(o_ready, hd * 8 + (i + 1))
                        if i:
                            sc.wait_ge(osq_ready, hd * 8 + i)
                        sc.activation(wkf[0:tz, 7 * T + T // 2:7 * T + T // 2 + P], on(i)[0:tz, :], ACT.Square, accum_out=ss[0:tz, i:i + 1])\
                          .then_inc(osq_ready, 1)

                    for i, (s, t0, tz) in enumerate(TILES):
                        if i >= 2:
                            sc.wait_ge(a_turned, hd * 8 + (i - 1))
                        for c in range(2):
                            sc.wait_ge(nb_ready, hd * 16 + (2 * i + c + 1))
                            sc.activation(prob(i, c)[0:tz, 0:LENS[s]], flat(c)[0:tz, 0:LENS[s]], ACT.Exp,
                                          bias=nb[0:tz, i, c:c + 1], scale=qkr[0:tz, i, c:c + 1],
                                          accum_out=sums[0:tz, i, c:c + 1]).then_inc(probs_ready, 1)
                        if i >= 2:
                            squared(i - 2)
                        turned(i)
                    squared(NT - 2)
                    squared(NT - 1)
                    sc.wait_ge(osq_ready, hd * 8 + 8)
                    sc.activation(rs[:, :], ss[:, :], ACT.Sqrt, bias=epsc, scale=1.0 / P).then_inc(oroot, 1)
                    high(wk[:, 8, :], yh[:, bass.ds(hd, 1), :].rearrange("p a b -> p (a b)"),
                         hd + (YL_AT[MIX1] + 1))
            out_blocks(OUT1, 3, FFNN + KT)
            ffn(FFN1, 1)


_INS = ['x_prompt', 'x_sample', 'meta_tokens', 'norm_mix', 'norm_ffn', 'm_w_in', 'm_b_gate', 'm_g_head', 'm_w_out',
        'd_w_in', 'd_g_q', 'd_g_k', 'd_lam_q1', 'd_lam_k1', 'd_lam_q2', 'd_lam_k2', 'd_g_sub', 'd_w_out',
        'ffn_w_in', 'ffn_w_out']
_OUTS = [((1, 512, D), 'float32'), ((1, 256, D), 'float32')]


def kernel(**inputs):
    import numpy as _np
    import concourse.bacc as _bacc
    from concourse import mybir as _mybir
    from concourse.bass_utils import run_bass_kernel_spmd as _run

    nc = _bacc.Bacc("TRN2", target_bir_lowering=False, num_devices=1)
    arrays, args = {}, []
    consts, rope = host_constants()
    for name, a in [(n, inputs[n]) for n in _INS] + [("consts", consts), ("rope", rope)]:
        a = _np.ascontiguousarray(a)
        arrays[f"in_{name}_dram"] = a
        args.append(nc.dram_tensor(f"in_{name}_dram", a.shape, _mybir.dt.from_np(a.dtype), kind="ExternalInput").ap())
    for i, (shape, dtype) in enumerate(_OUTS):
        dt = _mybir.dt.from_np(_np.dtype(dtype))
        args.append(nc.dram_tensor(f"out_{i}_dram", shape, dt, kind="ExternalOutput").ap())
    trunk(nc, *args)
    r = _run(nc, [arrays], core_ids=[0])
    return tuple(r.results[0][f"out_{i}_dram"] for i in range(len(_OUTS)))
```

```python
import math
from contextlib import ExitStack

import concourse.bass as bass
from concourse import mybir

F32 = mybir.dt.float32
F32R = mybir.dt.float32r
ALU = mybir.AluOpType
ACT = mybir.ActivationFunctionType
AX = mybir.AxisListType

P = 128
D = 1024
KT = D // P
META = 16
LENS = (META + 512, META + 256)
T = sum(LENS)
HT = T // 2
SEGS = ((0, LENS[0] - META, META), (LENS[0] - META, T - 2 * META, LENS[0] + META))
TQ = T - 2 * META
FF = 2816
FT = FF // P
GROUPS = (8, 8, 6)
M_HEADS, M_DK, M_DV = 4, 128, 256
D_HEADS, D_HD = 8, 64
EPS = 1e-6
FAR = 1e30
LAMBDA_INIT = 0.8 - 0.6 * math.exp(-0.3)
ROPE_THETA, ROPE_DIM = 500000.0, D_HD // 4

TILES = [(s, t0, min(P, LENS[s] - a)) for s in (0, 1) for a in range(0, LENS[s], P)
         for t0 in (sum(LENS[:s]) + a,)]
START = (0, LENS[0])
OF_SEQ = ([0, 1, 2, 3, 4], [5, 6, 7])
NT = len(TILES)
NQ = TQ // P
Q_SEQ = (0, 0, 0, 0, 1, 1)

MIX0 = 0
OUT0 = MIX0 + 6 * M_HEADS
FFN0 = OUT0 + KT
NFF = 2 * FT + KT * len(GROUPS)
MIX1 = FFN0 + NFF
OUT1 = MIX1 + 3 * D_HEADS
FFN1 = OUT1 + KT
BLOCKS = FFN1 + NFF
XT = 6
YL_AT = {OUT0: 2 * M_HEADS, FFN0: 2 * M_HEADS, MIX1: 2 * M_HEADS + FT,
         OUT1: 2 * M_HEADS + FT + D_HEADS, FFN1: 2 * M_HEADS + FT + D_HEADS}
GATE_COLS = 2 * M_HEADS * M_DK + 2 * M_HEADS * M_DV
M_PER = 57
A_PER = 78
ATTN_SET = 8
SWAP = [i ^ (ROPE_DIM // 2) if i < ROPE_DIM else i for i in range(32)]

MIXN, FFNN, GHEAD, GSUB, GQ, GK, BGATE = 0, 16, 32, 34, 35, 36, 37
NPAR = 38
IDENT, MASKF, MASKB, ONEHOT, COMP, NCONST = 0, 128, 256, 384, 388, 390


def host_constants():
    import numpy as np
    c = np.zeros((P, NCONST), np.float32)
    r = np.arange(P)
    c[r, IDENT + r] = 1.0
    c[:, MASKF:MASKF + P] = np.where(r[None, :] >= r[:, None], 0.0, FAR)
    c[:, MASKB:MASKB + P] = np.where(r[None, :] <= r[:, None], 0.0, FAR)
    half = ROPE_DIM // 2
    c[0:D_HD, COMP] = 1.0
    c[D_HD:P, COMP + 1] = 1.0
    for h in range(M_HEADS):
        c[h, ONEHOT + h] = 1.0
        c[64 + h, ONEHOT + h] = 1.0
    inv = np.float32(ROPE_THETA) ** (-np.arange(0, ROPE_DIM, 2, dtype=np.float32) / np.float32(ROPE_DIM))
    rope = np.zeros((P, 2, LENS[0]), np.float32)
    rope[:, 0, :] = 1.0
    ang = np.arange(LENS[0], dtype=np.float32)[:, None] * inv.astype(np.float32)[None, :]
    cos, sin = np.cos(ang).T, np.sin(ang).T
    for base in (0, D_HD):
        rope[base:base + half, 0, :] = cos
        rope[base + half:base + ROPE_DIM, 0, :] = cos
        rope[base:base + half, 1, :] = -sin
        rope[base + half:base + ROPE_DIM, 1, :] = sin
    return c, rope


class Steps:

    def __init__(self, eng, sem):
        self.eng, self.sem, self.base, self.n = eng, sem, 0, 0

    def __call__(self, ins):
        ins.then_inc(self.sem, 1)
        self.n += 1

    def wait(self):
        self.eng.wait_ge(self.sem, self.base + self.n)

    def loop_start(self, i, per):
        self.entry = self.base + self.n
        self.base = i * per + self.entry
        self.n = 0

    def loop_end(self, count, per):
        assert self.n == per, (self.n, per)
        self.base, self.n = self.entry + count * per, 0


def trunk(nc, x_prompt, x_sample, meta_tokens, norm_mix, norm_ffn, m_w_in, m_b_gate, m_g_head, m_w_out,
          d_w_in, d_g_q, d_g_k, d_lam_q1, d_lam_k1, d_lam_q2, d_lam_k2, d_g_sub, d_w_out,
          ffn_w_in, ffn_w_out, consts, rope, y_prompt, y_sample):
    ctx = ExitStack()
    with ctx:
        def sb(name, shape, dt=F32, where=None):
            return (where or ctx).enter_context(nc.sbuf_tensor(name, shape, dt))

        def sem(name):
            return ctx.enter_context(nc.semaphore(name))

        h = sb("h", [P, KT, T])
        xh, xl = sb("xh", [P, KT, T], F32R), sb("xl", [P, KT, T], F32R)
        y_memory = ExitStack()
        yh = sb("yh", [P, KT, T], F32R, y_memory)
        yl = sb("yl", [P, KT, T], F32R, y_memory)
        y_memory.close()
        spare = sb("spare", [P, 2, KT, T])
        raw = sb("raw", [P, 2, KT * P])
        wh, wl = sb("wh", [P, 2, KT * P], F32R), sb("wl", [P, 2, KT * P], F32R)
        rstd = sb("rstd", [P, T])
        cst = sb("cst", [P, NCONST])
        ones = sb("ones", [P, P])
        par = sb("par", [P, NPAR])
        small = sb("small", [P, 4])
        ss = sb("ss", [P, NT])
        rs = sb("rs", [P, NT])
        wk = sb("wk", [P, 9, T])
        wkf = wk[:, :, :].rearrange("p a b -> p (a b)")
        epsc = small[:, 0:1]

        gate_phase = ExitStack()
        graw = sb("graw", [P, KT, 16], F32, gate_phase)
        gwh = sb("gwh", [P, KT, P], F32R, gate_phase)
        gwl = sb("gwl", [P, KT, P], F32R, gate_phase)
        prow = sb("prow", [NPAR, P], F32, gate_phase)
        gate_phase.close()

        mlstm_phase = ExitStack()
        vn = sb("vn", [P, NT, M_DV + 1], F32, mlstm_phase)
        wt = sb("wt", [P, 5, LENS[0] + P], F32, mlstm_phase)
        mrow = sb("mrow", [P, T], F32, mlstm_phase)
        ce = sb("ce", [P, NT, 4], F32, mlstm_phase)
        dd = sb("dd", [P, 2, 2], F32, mlstm_phase)
        rd = sb("rd", [P, 2, 2], F32, mlstm_phase)
        mlstm_phase.close()

        attn_phase = ExitStack()
        cq = sb("cq", [P, LENS[0]], F32, attn_phase)
        ck = sb("ck", [P, LENS[0]], F32, attn_phase)
        sq = sb("sq", [P, LENS[0]], F32, attn_phase)
        sk = sb("sk", [P, LENS[0]], F32, attn_phase)
        va = sb("va", [P, 2, NT, P], F32, attn_phase)
        at = sb("at", [P, 2, 5, P], F32, attn_phase)
        qk2 = sb("qk2", [P, 2 * (NQ + NT)], F32, attn_phase)
        qkr = sb("qkr", [P, 2, 2 * (NQ + NT)], F32, attn_phase)
        oss = sb("oss", [P, 2, NQ], F32, attn_phase)
        mx = sb("mx", [P, NQ, 2], F32, attn_phase)
        nb = sb("nb", [P, NQ, 2], F32, attn_phase)
        sums = sb("sums", [P, NQ, 2], F32, attn_phase)
        rsum = sb("rsum", [P, NQ, 2], F32, attn_phase)
        ratio = sb("ratio", [P, NQ], F32, attn_phase)
        lv = sb("lv", [P, 4, D_HD], F32, attn_phase)
        lam = sb("lam", [P, 8], F32, attn_phase)
        gsub = sb("gsub", [P, 1], F32, attn_phase)
        gswap = sb("gswap", [P, 2], F32, attn_phase)
        attn_phase.close()

        ps = ctx.enter_context(nc.psum_tensor("ps", [P, 8, 512], F32))

        def pair(p, rows=P):
            return ps[0:rows, 2 * p:2 * p + 2, 0:HT]

        def flat(p):
            return ps[:, 2 * p:8 if p == 2 else 2 * p + 2, :].rearrange("p a b -> p (a b)")

        def two(x):
            return x.rearrange("p (a b) -> p a b", a=2)

        def packed_acc(p):
            return flat(p)[:, 0:TQ]

        def tile_of(x, k):
            return x[:, bass.ds(k, 1), :].rearrange("p a b -> p (a b)")

        ident = cst[:, IDENT:IDENT + P]

        cerow = wk[:, 8, :]
        q_sq, k_sq, swapped, v_raw = spare[:, 0, 6, 0:TQ], spare[:, 0, 7, :], spare[:, 1, 6, :], spare[:, 1, 7, :]
        key_roots = spare[:, 0, 6:8, :].rearrange("p a b -> p (a b)")[:, 0:NT * P]
        PROBS = 4 * T
        ON = PROBS + 4 * LENS[0]
        JUNK = ON + 2 * NQ * P
        junk = wkf[:, JUNK:JUNK + P]

        def hn(i):
            at_col = {4: T, 7: T + M_DV}[i] if TILES[i][2] < P else 6 * T + (i - (i > 4)) * M_DV
            return wkf[:, at_col:at_col + M_DV]

        def on(odd, i):
            at_col = ON + (odd * NQ + i) * P
            return wkf[:, at_col:at_col + P]

        def prob(i, c):
            at_col = PROBS + (2 * (i % 2) + c) * LENS[0]
            return wkf[:, at_col:at_col + LENS[0]]

        acc_o = ps[:, 5, P:2 * P]

        consts_in, params_in, meta_in, gate_in = sem("consts_in"), sem("params_in"), sem("meta_in"), sem("gate_in")
        x_in = [sem(f"x_in{r}") for r in range(XT)]
        raw_in = [sem("raw_in0"), sem("raw_in1")]
        rope_in, lam_in, out_done = sem("rope_in"), sem("lam_in"), sem("out_done")
        pool_set, w_hi, w_split = sem("pool_set"), sem("w_hi"), sem("w_split")
        gate_split = sem("gate_split")
        x_turned, meta_turned, par_turned, par_ready = sem("x_turned"), sem("meta_turned"), sem("par_turned"), sem("par_ready")
        h_ready, act_h = sem("h_ready"), sem("act_h")
        acc_free, block_done = sem("acc_free"), sem("block_done")
        xh_ready, xl_ready, sq_ready, sq_summed = sem("xh_ready"), sem("xl_ready"), sem("sq_ready"), sem("sq_summed")
        norm_sum, norm_root, rstd_ready = sem("norm_sum"), sem("norm_root"), sem("rstd_ready")
        vstep, astep, ones_set = sem("vstep"), sem("astep"), sem("ones_set")
        gates_done, gate_x, gate_soft, gate_m, gate_e = (sem(n) for n in ("gates_done", "gate_x", "gate_soft", "gate_m", "gate_e"))
        mrow_masked, mrep_done, mrep_ready = sem("mrow_masked"), sem("mrep_done"), sem("mrep_ready")
        ce_turned, ce_ready = sem("ce_turned"), sem("ce_ready")
        v_turned, vn_ready = sem("v_turned"), sem("vn_ready")
        s_ready, diag_ready, e_ready, wt_ready = sem("s_ready"), sem("diag_ready"), sem("e_ready"), sem("wt_ready")
        pv_done, hn_ready, hsq_ready, hroot = sem("pv_done"), sem("hn_ready"), sem("hsq_ready"), sem("hroot")
        hs_ready, sig_ready = sem("hs_ready"), sem("sig_ready")
        y_turned, yt_ready, yh_ready, yl_ready = sem("y_turned"), sem("yt_ready"), sem("yh_ready"), sem("yl_ready")
        gate_in_ready, silu_ready = sem("gate_in_ready"), sem("silu_ready")
        qsq_ready, qks_done, qk_root = sem("qsq_ready"), sem("qks_done"), sem("qk_root")
        lt_ready, lt_turned, kn_ready = sem("lt_ready"), sem("lt_turned"), sem("kn_ready")
        va_turned, va_ready = sem("va_turned"), sem("va_ready")
        sc_ready, nb_ready, probs_ready, a_ready = sem("sc_ready"), sem("nb_ready"), sem("probs_ready"), sem("a_ready")
        a_turned, at_ready, o_done, o_ready, osq_ready, oroot = (sem(n) for n in ("a_turned", "at_ready", "o_done", "o_ready", "osq_ready", "oroot"))
        os_ready, o_turned = sem("os_ready"), sem("o_turned")
        lam_sums, lam_exp, attn_set = sem("lam_sums"), sem("lam_exp"), sem("attn_set")
        out_turned, out_copied = sem("out_turned"), sem("out_copied")
        pool_passed, scalar_passed, vector_passed = sem("pool_passed"), sem("scalar_passed"), sem("vector_passed")

        block = ctx.enter_context(nc.Block())

        @block.sync
        def _(sp):
            def weights(n, slot, src, k=KT, wait=True):
                if wait:
                    sp.wait_ge(w_split, n - 1)
                sp.dma_start(raw[:, slot, 0:k * P].rearrange("p (k c) -> p k c", k=k),
                             src).then_inc(raw_in[slot], 16)

            def cols(w, c):
                return w.rearrange("(k p) n -> p k n", p=P)[:, :, bass.ds(c, P)]

            def mlstm_cols(hd, j):
                qk, v = M_HEADS * M_DK, M_HEADS * M_DV
                return cols(m_w_in[0], (hd * M_DK, qk + hd * M_DK, 2 * qk + hd * M_DV, 2 * qk + hd * M_DV + P,
                                        2 * qk + v + hd * M_DV, 2 * qk + v + hd * M_DV + P)[j])

            def out_blocks(n0, w):
                with sp.Fori(0, KT // 2) as i:
                    for j in range(2):
                        weights(n0 + 2 * i + j, j, cols(w, i * (2 * P) + j * P))

            def ffn_blocks(n0, layer):
                w_in, w_out = ffn_w_in[layer], ffn_w_out[layer]
                at_tile = 0
                for tiles in GROUPS:
                    with sp.Fori(0, tiles) as i:
                        for j in range(2):
                            weights(n0 + 2 * i + j, j, cols(w_in, i * P + (at_tile * P + j * FF)))
                    n0 += 2 * tiles
                    rows = w_out[at_tile * P:(at_tile + tiles) * P, :]
                    with sp.Fori(0, KT // 2) as i:
                        for j in range(2):
                            weights(n0 + 2 * i + j, j, cols(rows, i * (2 * P) + j * P), tiles)
                    n0 += KT
                    at_tile += tiles

            sp.dma_start(cst[:, :], consts).then_inc(consts_in, 16)
            for r in range(XT):
                src = x_prompt[0, r * P:(r + 1) * P, :] if r < 4 else x_sample[0, (r - 4) * P:(r - 3) * P, :]
                sp.dma_start(wkf[:, r * D:(r + 1) * D], src).then_inc(x_in[r], 16)
                if r == 0:
                    sp.dma_start(wkf[0:META, XT * D:(XT + 1) * D], meta_tokens).then_inc(meta_in, 16)
                    sp.wait_ge(pool_set, 1)
                    for at_row, src in ((MIXN, norm_mix.rearrange("l (k p) -> (l k) p", p=P)),
                                        (FFNN, norm_ffn.rearrange("l (k p) -> (l k) p", p=P)),
                                        (GHEAD, m_g_head[0].rearrange("(k p) -> k p", p=P)), (GSUB, d_g_sub)):
                        sp.dma_start(prow[at_row:at_row + src.shape[0], :], src).then_inc(params_in, 16)
                    for at_row, src in ((GQ, d_g_q), (GK, d_g_k)):
                        for c in range(2):
                            sp.dma_start(prow[at_row:at_row + 1, c * D_HD:(c + 1) * D_HD], src).then_inc(params_in, 16)
                    for g in range(4):
                        sp.dma_start(prow[BGATE:BGATE + 1, 32 * g:32 * g + M_HEADS],
                                     m_b_gate[:, M_HEADS * g:M_HEADS * (g + 1)]).then_inc(params_in, 16)
                    with nc.allow_non_contiguous_dma(reason="16 gate columns"):
                        sp.dma_start(graw[:, :, :], m_w_in[0].rearrange("(k p) n -> p k n", p=P)[:, :, GATE_COLS:GATE_COLS + 16])\
                          .then_inc(gate_in, 16)
            for j in range(6):
                weights(MIX0 + j, j % 2, mlstm_cols(0, j), wait=j >= 2)
            with sp.Fori(1, M_HEADS) as hd:
                for j in range(6):
                    weights(MIX0 + hd * 6 + j, j % 2, mlstm_cols(hd, j))
            out_blocks(OUT0, m_w_out[0])
            ffn_blocks(FFN0, 0)
            with sp.Fori(0, D_HEADS // 2) as i:
                for j in range(6):
                    weights(MIX1 + i * 6 + j, j % 2, cols(d_w_in[0], i * (2 * P) + (j // 3) * P + (j % 3) * D))
            out_blocks(OUT1, d_w_out[0])
            ffn_blocks(FFN1, 1)
            for r in range(XT):
                dst = y_prompt[0, r * P:(r + 1) * P, :] if r < 4 else y_sample[0, (r - 4) * P:(r - 3) * P, :]
                sp.wait_ge(out_copied, r + 1)
                sp.dma_start(dst, wkf[:, r * D:(r + 1) * D]).then_inc(out_done, 16)
            sp.wait_ge(out_done, 16 * XT)

        @block.gpsimd
        def _(pool):
            pool.memset(prow[:, :], 0.0).then_inc(pool_set, 1)
            pool.memset(gwh[:, :, :].bitcast(F32), 0.0).then_inc(pool_set, 1)
            pool.memset(gwl[:, :, :].bitcast(F32), 0.0).then_inc(pool_set, 1)
            pool.wait_ge(pool_set, 3)
            pool.wait_ge(gate_in, 16)
            spread = [x[:, :, :].rearrange("p k (g c) -> p k g c", g=4)[:, :, :, 0:M_HEADS] for x in (gwh, gwl)]
            source = graw[:, :, :].rearrange("p k (g c) -> p k g c", g=4)
            for k in range(KT):
                pool.tensor_copy(spread[0][:, k], source[:, k]).then_inc(gate_split, 1)
            pool.wait_ge(gate_split, KT)
            for k in range(KT):
                pool.tensor_tensor(spread[1][:, k], source[:, k], spread[0][:, k].bitcast(F32),
                                   ALU.subtract).then_inc(gate_split, 1)

            def split(n, slot, times, wait=True):
                if wait:
                    pool.wait_ge(block_done, n - 1)
                pool.wait_ge(raw_in[slot], 16 * times)
                pool.sem_inc(pool_passed, 1)
                pool.tensor_copy(wh[:, slot, :], raw[:, slot, :]).then_inc(w_hi, 1)
                pool.wait_ge(w_hi, n + 1)
                pool.tensor_tensor(wl[:, slot, :], raw[:, slot, :], wh[:, slot, :].bitcast(F32),
                                   ALU.subtract).then_inc(w_split, 1)

            for slot in range(2):
                split(slot, slot, 1, wait=False)
            with pool.Fori(1, BLOCKS // 2) as i:
                for slot in range(2):
                    split(i * 2 + slot, slot, i + 1)

        @block.tensor
        def _(pe):
            def run_block(n, slot, p, xs=(xh, xl), k_tiles=KT, between={}, tokens="all", free=True, k0=0, k1=None):
                if k0 == 0:
                    pe.wait_ge(w_split, n + 1)
                    if free:
                        pe.wait_ge(acc_free, n + XT - 1)
                parts = {"all": [(ps[:, 2 * p + half, 0:HT], half * HT, (half + 1) * HT) for half in range(2)],
                         "inner": [(flat(p)[:, a:b], t, t + b - a) for a, b, t in SEGS],
                         "packed": [(flat(p)[:, a:b], a, b) for a, b, t in SEGS]}[tokens]
                for k in range(k0, k1 or k_tiles):
                    for q, (w, x) in enumerate(((wh, xs[0]), (wh, xs[1]), (wl, xs[0]))):
                        for out, a, b in parts:
                            mm = pe.matmul(out, w[:, slot, k * P:(k + 1) * P], x[:, k, a:b], start=(k + q == 0),
                                           stop=(k == k_tiles - 1 and q == 2), skip_group_check=True)
                    if k == k_tiles - 1:
                        mm.then_inc(block_done, 1)
                    for f in between.get(k, ()):
                        f()

            def sum_squares(count):
                pe.wait_ge(sq_summed, KT * count)
                parts = ([(ps[:, 6 + half, 0:HT], half * HT, (half + 1) * HT) for half in range(2)] if count < 4 else
                         [(flat(3)[:, a:b], t, t + b - a) for a, b, t in SEGS])
                for out, a, b in parts:
                    mm = pe.matmul(out, ones[:, :], wk[:, 6, a:b], start=True, stop=True)
                mm.then_inc(norm_sum, 1)

            def out_blocks(n0):
                pe.wait_ge(yl_ready, YL_AT[n0])
                with pe.Fori(0, KT // 2) as i:
                    for j in range(2):
                        run_block(n0 + 2 * i + j, j, j, (yh, yl), tokens="all" if n0 < MIX1 else "packed")

            def ffn(n0, layer):
                pe.wait_ge(xl_ready, KT * (2 * layer + 2))
                sum_squares(2 * layer + 2)
                y = YL_AT[n0]
                for tiles in GROUPS:
                    with pe.Fori(0, tiles) as i:
                        for j in range(2):
                            run_block(n0 + 2 * i + j, j, j, tokens=("all", "inner")[layer])
                    n0 += 2 * tiles
                    y += tiles
                    pe.wait_ge(yl_ready, y)
                    with pe.Fori(0, KT // 2) as i:
                        for j in range(2):
                            run_block(n0 + 2 * i + j, j, j, (yh, yl), tiles, tokens=("all", "packed")[layer])
                    n0 += KT

            pe.wait_ge(consts_in, 16)
            for r in range(XT):
                pe.wait_ge(x_in[r], 16)
                if r >= 2:
                    pe.wait_ge(acc_free, r - 1)
                for k in range(KT):
                    mm = pe.transpose(flat(r % 2)[:, k * P:(k + 1) * P], wkf[:, r * D + k * P:r * D + (k + 1) * P], ident)
                mm.then_inc(x_turned, 1)
                if r == 0:
                    pe.wait_ge(meta_in, 16)
                    for k in range(KT):
                        mm = pe.transpose(ps[:, 4, k * META:(k + 1) * META],
                                          wkf[0:META, XT * D + k * P:XT * D + (k + 1) * P], ident[0:META, 0:META])
                    mm.then_inc(meta_turned, 1)
                    pe.wait_ge(params_in, 16 * 12)
                    pe.transpose(ps[:, 5, 0:NPAR], prow[:, :], ident[0:NPAR, 0:NPAR]).then_inc(par_turned, 1)

            pe.wait_ge(gate_split, 2 * KT)
            pe.wait_ge(par_ready, 1)
            pe.wait_ge(h_ready, 2)
            for k in range(KT):
                pe.wait_ge(xl_ready, k + 1)
                first = k == 0
                for w, x in ((gwh, xh), (gwh, xl), (gwl, xh)):
                    for half in range(2):
                        mm = pe.matmul(ps[:, 4 + half, 0:HT], w[:, k, :], x[:, k, half * HT:(half + 1) * HT],
                                       start=first, stop=(k == KT - 1 and w is gwl), skip_group_check=True)
                    first = False
            mm.then_inc(gates_done, 1)
            sum_squares(1)

            with pe.Fori(0, M_HEADS) as hd:
                n = MIX0 + hd * 6

                def repeat_m():
                    pe.wait_ge(mrow_masked, hd + 1)
                    for d in range(2):
                        for half in range(2):
                            mm = pe.matmul(ps[:, 4 + 2 * d + half, 0:HT], ones[64 * d:64 * d + 32, :],
                                           wk[64 * d:64 * d + 32, 4, half * HT:(half + 1) * HT], start=True, stop=True)
                    mm.then_inc(mrep_done, 1)

                def turn_ce():
                    pe.wait_ge(mrep_ready, hd * 2 + 2)
                    pe.wait_ge(gate_e, 2)
                    for i, (_, t0, tz) in enumerate(TILES):
                        mm = pe.transpose(flat(2)[0:tz, i * P:(i + 1) * P], cerow[:, t0:t0 + tz], ident)
                    mm.then_inc(ce_turned, 1)

                def turn_v():
                    pe.wait_ge(ce_ready, hd * 4 + 4)
                    pe.wait_ge(acc_free, n + XT + 4)
                    for i, (_, t0, tz) in enumerate(TILES):
                        at_col = (i if i < 4 else {5: 4, 6: 5, 4: 6, 7: 7}[i]) * M_DV
                        for c in range(2):
                            mm = pe.transpose(flat(2)[0:tz, at_col + c * P:at_col + (c + 1) * P],
                                              wk[:, 6 + c, t0:t0 + tz], ident)
                    mm.then_inc(v_turned, 1)

                def scores(j):
                    s, t0, tz = TILES[j]
                    if j == 0:
                        pe.wait_ge(vn_ready, hd * 3 + 3)
                    elif j == 5:
                        pe.wait_ge(hn_ready, hd * 8 + 5)
                    elif j not in (1, 6):
                        pe.wait_ge(wt_ready, hd * 8 + (j - 1))
                    for a in range(0, LENS[s], 512):
                        b = min(a + 512, LENS[s])
                        mm = pe.matmul(flat(2 + 0)[0:tz, (j % 2) * 1024 + a:(j % 2) * 1024 + b], wk[:, 1, t0:t0 + tz],
                                       wk[:, 0, START[s] + a:START[s] + b], start=True, stop=True)
                    mm.then_inc(s_ready, 1)

                def read_state(i):
                    s, t0, tz = TILES[i]
                    tiles, a = OF_SEQ[s], t0 - START[s]
                    if i == tiles[0]:
                        pe.wait_ge(wt_ready, hd * 8 + (tiles[-1] + 1))
                    elif i not in (1, 6):
                        pe.wait_ge(hn_ready, hd * 8 + (i - 1))
                    for d in range(2):
                        js = [j for j in tiles if (j <= i if d == 0 else j >= i)]
                        for j in js:
                            sz = TILES[j][2]
                            off = a + (sz if d == 0 else 0)
                            mm = pe.matmul(ps[0:tz, 4 + 2 * (i % 2) + d, 0:M_DV + 1],
                                           wt[0:sz, j - tiles[0], off:off + tz], vn[0:sz, j, :],
                                           start=(j == js[0]), stop=(j == js[-1]))
                    mm.then_inc(pv_done, 1)

                run_block(n, 0, 0)
                run_block(n + 1, 1, 1, between={3: [repeat_m]})
                run_block(n + 2, 0, 0, between={3: [turn_ce]})
                run_block(n + 3, 1, 1)
                turn_v()
                run_block(n + 4, 0, 0, between={j: [lambda j=j: scores(j)] for j in range(5)})
                for i in OF_SEQ[0]:
                    read_state(i)
                run_block(n + 5, 1, 1, between={0: [lambda: scores(5)], 1: [lambda: scores(6)], 2: [lambda: scores(7)],
                                                4: [lambda i=i: read_state(i) for i in OF_SEQ[1]]})
                for c in range(2):
                    pe.wait_ge(hs_ready, hd + 1)
                    for i, (_, t0, tz) in enumerate(TILES):
                        mm = pe.transpose(flat(2)[:, c * 1024 + t0:c * 1024 + t0 + tz],
                                          hn(i)[0:tz, c * P:(c + 1) * P], ident[0:tz, 0:tz])
                    mm.then_inc(y_turned, 1)

            out_blocks(OUT0)
            ffn(FFN0, 0)

            def square_sums(g):
                pe.wait_ge(qsq_ready, g * 2 + 2)
                for i in range(NQ + NT):
                    if i < NQ:
                        lhs = q_sq[:, i * P:(i + 1) * P]
                    elif i < NQ + NT - 1:
                        t0 = TILES[i - NQ][1]
                        lhs = k_sq[:, t0:t0 + P]
                    else:
                        lhs = k_sq[:, T - META:T]
                    mm = pe.matmul(ps[0:lhs.shape[1], 5, 2 * P + 2 * i:2 * P + 2 * i + 2], lhs, cst[:, COMP:COMP + 2],
                                   start=True, stop=True, skip_group_check=True)
                mm.then_inc(qks_done, 1)

            def turn_key_roots(g, n):
                pe.wait_ge(acc_free, n + (XT + 3))
                pe.wait_ge(lt_ready, g + 1)
                for i, (_, t0, tz) in enumerate(TILES):
                    mm = pe.transpose(flat(3)[:, t0:t0 + tz], key_roots[0:tz, i * P:(i + 1) * P], ident[0:tz, 0:tz])
                mm.then_inc(lt_turned, 1)

            def turn_va(hd, first):
                if first:
                    pe.wait_ge(acc_free, MIX1 + XT + 3)
                else:
                    pe.wait_ge(yl_ready, hd + (YL_AT[MIX1] - 1))
                for i, (_, t0, tz) in enumerate(TILES):
                    at_col = (i if i < 4 else {5: 4, 6: 5, 4: 6, 7: 7}[i]) * P
                    mm = pe.transpose(flat(3)[0:tz, at_col:at_col + P], v_raw[:, t0:t0 + tz], ident)
                mm.then_inc(va_turned, 1)

            def turn_output(hd, odd):
                pe.wait_ge(os_ready, hd + 1)
                for i in range(NQ):
                    mm = pe.transpose(flat(3)[:, i * P:(i + 1) * P], on(odd, i), ident)
                mm.then_inc(o_turned, 1)

            def attn_scores(hd, odd, i):
                s = Q_SEQ[i]
                if i == 0:
                    pe.wait_ge(kn_ready, hd + 1)
                for c in range(2):
                    if i:
                        pe.wait_ge(probs_ready, hd * (2 * NQ) + (2 * i - 1 + c))
                    rows = slice(D_HD * c, D_HD * (c + 1))
                    for a in range(0, LENS[s], 512):
                        b = min(a + 512, LENS[s])
                        mm = pe.matmul(flat(c)[:, a:b], wk[rows, odd, i * P:(i + 1) * P],
                                       wk[rows, 2 + odd, START[s] + a:START[s] + b], start=True, stop=True)
                    mm.then_inc(sc_ready, 1)

            def turn_attention(hd, i, first):
                if not (first and i == 0):
                    pe.wait_ge(o_ready, hd * NQ + i)
                pe.wait_ge(a_ready, hd * NQ + (i + 1))
                for q, j in enumerate(OF_SEQ[Q_SEQ[i]]):
                    sz = TILES[j][2]
                    dst = ps[:, 4, q * P:(q + 1) * P] if sz == P else ps[0:sz, 5, 0:P]
                    mm = pe.transpose(dst, prob(i, 0)[:, q * P:q * P + sz], ident)
                mm.then_inc(a_turned, 1)

            def attend(hd, odd, i):
                pe.wait_ge(at_ready, hd * NQ + (i + 1))
                if i == 0:
                    pe.wait_ge(va_ready, hd * 3 + 3)
                js = OF_SEQ[Q_SEQ[i]]
                for q, j in enumerate(js):
                    sz = TILES[j][2]
                    mm = pe.matmul(acc_o, at[0:sz, i % 2, q, :], va[0:sz, odd, j, :],
                                   start=(q == 0), stop=(j == js[-1]), skip_group_check=True)
                mm.then_inc(o_done, 1)

            def head(hd, odd, n, first=False, last=False):
                even = 1 - odd

                def between_tiles(i):
                    if i == 0 and not last:
                        pe.wait_ge(va_ready, hd * 3 + 3)
                        run_block(n, even, 3, tokens="inner", free=False)
                    elif i == 1 and not last:
                        pe.wait_ge(acc_free, n + (XT + 1))
                        run_block(n + 1, odd, 3, free=False, k1=3)
                    elif i == 2 and not last:
                        run_block(n + 1, odd, 3, free=False, k0=3)
                    elif i == 3 and not last:
                        pe.wait_ge(acc_free, n + (XT + 2))
                        run_block(n + 2, even, 3, free=False, k1=3)
                        pe.wait_ge(o_ready, hd * NQ + 3)
                        square_sums(hd + 1)
                    elif i == 4 and not last:
                        run_block(n + 2, even, 3, free=False, k0=3)
                    elif i == 5 and not last:
                        turn_key_roots(hd + 1, n)
                    elif i == 6 and not first:
                        if not last:
                            pe.wait_ge(kn_ready, hd + 2)
                        turn_output(hd - 1, even)

                attn_scores(hd, odd, 0)
                turn_va(hd, first)
                for i in range(NQ):
                    if i + 1 < NQ:
                        attn_scores(hd, odd, i + 1)
                    if i >= 1:
                        attend(hd, odd, i - 1)
                    between_tiles(i)
                    turn_attention(hd, i, first)
                between_tiles(NQ)
                attend(hd, odd, NQ - 1)

            pe.wait_ge(xl_ready, KT * 3)
            sum_squares(3)
            pe.wait_ge(attn_set, ATTN_SET)
            run_block(MIX1, 0, 0, tokens="inner")
            run_block(MIX1 + 1, 1, 1)
            run_block(MIX1 + 2, 0, 0, between={3: [lambda: square_sums(0)]})
            turn_key_roots(0, MIX1)
            head(0, 0, MIX1 + 3, first=True)
            with pe.Fori(0, (D_HEADS - 2) // 2) as it:
                for sub in range(2):
                    head(it * 2 + (1 + sub), 1 - sub, it * 6 + (MIX1 + 6 + 3 * sub))
            head(D_HEADS - 1, 1, None, last=True)
            turn_output(D_HEADS - 1, 1)

            out_blocks(OUT1)
            ffn(FFN1, 1)

            pe.wait_ge(acc_free, BLOCKS + XT)
            for r in range(XT):
                t0 = META + r * P if r < 4 else LENS[0] + META + (r - 4) * P
                if r >= 2:
                    pe.wait_ge(out_copied, r - 1)
                for k in range(KT):
                    mm = pe.transpose(flat(r % 2)[:, k * P:(k + 1) * P], h[:, k, t0:t0 + P], ident)
                mm.then_inc(out_turned, 1)

        @block.vector
        def _(ve):
            v = Steps(ve, vstep)

            def evacuate(n, p, dst):
                ve.wait_ge(block_done, n + 1)
                ve.tensor_tensor(two(dst), pair(p), two(rstd[:, :]), ALU.mult).then_inc(acc_free, 1)

            def evacuate_inner(n, p, dst, packed_rstd):
                ve.wait_ge(block_done, n + 1)
                if packed_rstd:
                    ve.tensor_tensor(dst, packed_acc(p), rstd[:, 0:TQ], ALU.mult).then_inc(acc_free, 1)
                else:
                    for a, b, t in SEGS:
                        ins = ve.tensor_tensor(dst[:, a:b], flat(p)[:, a:b], rstd[:, t:t + b - a], ALU.mult)
                    ins.then_inc(acc_free, 1)

            def split_low(src, dst_h, dst_l, ready, done):
                ve.wait_ge(yh_ready, ready)
                ve.tensor_tensor(dst_l, src, dst_h.bitcast(F32), ALU.subtract).then_inc(done, 1)

            def fold(count, k, gain):
                ve.wait_ge(xh_ready, count + 1)
                ve.scalar_tensor_tensor(xl[:, k, :], h[:, k, :], gain, xh[:, k, :].bitcast(F32),
                                        ALU.mult, ALU.subtract).then_inc(xl_ready, 1)

            def add_square(count, src, first):
                ve.wait_ge(sq_ready, count + 1)
                if first:
                    ve.tensor_copy(wk[:, 6, :], wk[:, src, :]).then_inc(sq_summed, 1)
                else:
                    ve.wait_ge(sq_summed, count)
                    ve.tensor_tensor(wk[:, 6, :], wk[:, 6, :], wk[:, src, :], ALU.add).then_inc(sq_summed, 1)

            def invert(count):
                ve.wait_ge(norm_root, count)
                ve.reciprocal(rstd[:, :], rstd[:, :]).then_inc(rstd_ready, 1)
                ve.wait_ge(rstd_ready, count)

            def out_blocks(n0, norm, gain_at):
                if norm is not None:
                    ve.memset(wk[:, 6, :], 0.0).then_inc(ones_set, 1)
                    ve.wait_ge(ones_set, 1 + norm)
                with ve.Fori(0, KT // 2) as i:
                    for j in range(2):
                        m = i * 2 + j
                        ve.wait_ge(block_done, n0 + m + 1)
                        hm = h[:, bass.ds(m, 1), :].rearrange("p a b -> p (a b)")
                        if n0 < MIX1:
                            ve.tensor_tensor(two(hm), two(hm), pair(j), ALU.add).then_inc(acc_free, 1)
                        else:
                            for a, b, t in SEGS:
                                ins = ve.tensor_tensor(hm[:, t:t + b - a], hm[:, t:t + b - a], flat(j)[:, a:b], ALU.add)
                            ins.then_inc(acc_free, 1)
                        if norm is not None:
                            c = m + KT * norm
                            ve.wait_ge(xh_ready, c + 1)
                            ve.scalar_tensor_tensor(
                                xl[:, bass.ds(m, 1), :].rearrange("p a b -> p (a b)"), hm,
                                par[:, bass.ds(m + gain_at, 1)],
                                xh[:, bass.ds(m, 1), :].rearrange("p a b -> p (a b)").bitcast(F32),
                                ALU.mult, ALU.subtract).then_inc(xl_ready, 1)
                            ve.wait_ge(sq_ready, c + 1)
                            ve.wait_ge(sq_summed, c)
                            ve.tensor_tensor(wk[:, 6, :], wk[:, 6, :], wk[:, 7, :], ALU.add).then_inc(sq_summed, 1)
                if norm is not None:
                    invert(norm + 1)

            def ffn(n0, layer):
                y0 = YL_AT[n0]
                for g, tiles in enumerate(GROUPS):
                    with ve.Fori(0, tiles) as i:
                        ft = y0 - YL_AT[FFN0] + i if layer == 0 else y0 - YL_AT[FFN1] + FT + i
                        if layer == 0:
                            evacuate(n0 + 2 * i, 0, wk[:, 0, :])
                            evacuate(n0 + 2 * i + 1, 1, wk[:, 2, :])
                        else:
                            evacuate_inner(n0 + 2 * i, 0, wk[:, 0, 0:TQ], True)
                            evacuate_inner(n0 + 2 * i + 1, 1, wk[:, 2, 0:TQ], True)
                        ve.wait_ge(silu_ready, ft + 1)
                        ve.wait_ge(acc_free, n0 + 2 * i + 2 + XT)
                        ve.wait_ge(yl_ready, y0 + i)
                        nt = (T, TQ)[layer]
                        ve.tensor_tensor(wk[:, 3, 0:nt], wk[:, 1, 0:nt], wk[:, 2, 0:nt], ALU.mult).then_inc(yt_ready, 1)
                        split_low(wk[:, 3, 0:nt], tile_of(yh, i)[:, 0:nt], tile_of(yl, i)[:, 0:nt], y0 + i + 1, yl_ready)
                    n0 += 2 * tiles
                    y0 += tiles
                    last = g == len(GROUPS) - 1
                    out_blocks(n0, {0: 2, 1: None}[layer] if last else None, MIXN + KT)
                    n0 += KT

            ve.memset(ones[:, :], 1.0).then_inc(ones_set, 1)
            v(ve.memset(epsc, EPS))
            v(ve.memset(ss[:, :], 1.0))
            for r in range(XT):
                t0 = META + r * P if r < 4 else LENS[0] + META + (r - 4) * P
                ve.wait_ge(x_turned, r + 1)
                ve.tensor_copy(h[:, :, t0:t0 + P], flat(r % 2).rearrange("p (k c) -> p k c", k=KT)).then_inc(acc_free, 1)
                if r == 0:
                    ve.wait_ge(meta_turned, 1)
                    for s in range(2):
                        ve.tensor_copy(h[:, :, START[s]:START[s] + META],
                                       ps[:, 4, 0:KT * META].rearrange("p (k c) -> p k c", k=KT)).then_inc(h_ready, 1)
                    ve.wait_ge(par_turned, 1)
                    ve.tensor_copy(par[:, :], ps[:, 5, 0:NPAR]).then_inc(par_ready, 1)
            ve.wait_ge(acc_free, XT)
            ve.wait_ge(h_ready, 2)
            ve.wait_ge(par_ready, 1)
            for k in range(KT):
                fold(k, k, par[:, MIXN + k:MIXN + k + 1])
                add_square(k, 7, k == 0)
            invert(1)

            ve.wait_ge(gates_done, 1)
            v(ve.tensor_tensor(two(wk[:, 0, :]), pair(2), two(rstd[:, :]), ALU.mult))
            v.wait()
            ve.tensor_scalar(wk[:, 0, :], wk[:, 0, :], par[:, BGATE:BGATE + 1], None, ALU.add).then_inc(gate_x, 1)
            v(ve.memset(wk[:, 4, :], 0.0))
            v(ve.memset(mrow[:, :], 0.0))
            v(ve.memset(vn[:, :, M_DV:M_DV + 1], 1.0))
            ve.wait_ge(gate_soft, 1)
            ve.wait_ge(gate_x, 1)
            v(ve.scalar_tensor_tensor(wk[:, 3, :], wk[:, 0, :], 0.0, wk[:, 5, :], ALU.min, ALU.subtract))
            v.wait()

            def span(s, back):
                a, b = START[s], START[s] + LENS[s]
                return slice(a, b) if not back else slice(b - 1, a - 1 if a else None, -1)

            for s in range(2):
                zero = small[:, 1:2]
                if s == 0:
                    v(ve.memset(zero, 0.0))
                    v.wait()
                for d in range(2):
                    src, dst = slice(32 + 64 * d, 36 + 64 * d), slice(64 * d, 64 * d + M_HEADS)
                    v(ve.tensor_tensor_scan(wk[dst, 4, span(s, d)], wk[src, 3, span(s, d)],
                                            small[src, 1:2].to_broadcast([M_HEADS, LENS[s]]), 0.0, ALU.add, ALU.add))
            v.wait()
            v(ve.tensor_tensor(cerow, wk[:, 0, :], wk[:, 4, :], ALU.subtract))
            v.wait()
            for s in range(2):
                for d in range(2):
                    rows = slice(64 * d, 64 * d + M_HEADS)
                    v(ve.tensor_tensor_scan(mrow[rows, span(s, d)], cerow[rows, span(s, d)],
                                            small[rows, 1:2].to_broadcast([M_HEADS, LENS[s]]), 0.0, ALU.max, ALU.add))
            v.wait()
            ve.tensor_tensor(wk[:, 5, :], wk[:, 4, :], mrow[:, :], ALU.add).then_inc(gate_m, 1)

            with ve.Fori(0, M_HEADS) as hd:
                v.loop_start(hd, M_PER)
                n = MIX0 + hd * 6
                ve.wait_ge(gate_m, 1)
                evacuate(n, 0, wk[:, 0, :])
                ve.tensor_scalar(wk[:, 4, :], mrow[:, :], cst[:, bass.ds(hd + ONEHOT, 1)], None, ALU.mult)\
                  .then_inc(mrow_masked, 1)
                evacuate(n + 1, 1, wk[:, 1, :])
                ve.wait_ge(ce_turned, hd + 1)
                turned = flat(2).rearrange("p (i g c) -> p i g c", i=2 * NT, g=4)
                for a, b, rows in ((0, 4, P), (5, 7, P), (4, 5, META), (7, 8, META)):
                    ve.tensor_copy(ce[0:rows, a:b, :],
                                   turned[0:rows, a:b, :, bass.ds(hd, 1)].rearrange("p i g c -> p i (g c)"))\
                      .then_inc(ce_ready, 1)
                evacuate(n + 2, 0, wk[:, 6, :])
                evacuate(n + 3, 1, wk[:, 7, :])

                def diagonals(j):
                    s, t0, tz = TILES[j]
                    q, a = j - OF_SEQ[s][0], t0 - START[s]
                    for d, mask in ((0, MASKF), (1, MASKB)):
                        off = a + (tz if d == 0 else 0)
                        ve.tensor_tensor(wt[0:tz, q, off:off + tz], wk[0:tz, 2 + d, t0:t0 + tz],
                                         cst[0:tz, mask:mask + tz], ALU.add).then_inc(diag_ready, 1)

                def state_weights(j):
                    s, t0, tz = TILES[j]
                    q, a = j - OF_SEQ[s][0], t0 - START[s]
                    ve.wait_ge(s_ready, hd * 8 + (j + 1))
                    ve.wait_ge(e_ready, hd * 8 + (j + 1))
                    base = (j % 2) * 1024
                    fwd = wt[0:tz, q, a + tz:LENS[s] + tz]
                    bwd = wt[0:tz, q, 0:a + tz]
                    v(ve.scalar_tensor_tensor(fwd, flat(2)[0:tz, base + a:base + LENS[s]], M_DK ** -0.5, fwd,
                                              ALU.mult, ALU.mult))
                    ve.scalar_tensor_tensor(bwd, flat(2)[0:tz, base:base + a + tz], M_DK ** -0.5, bwd,
                                            ALU.mult, ALU.mult).then_inc(wt_ready, 1)

                def normalise(i):
                    s, t0, tz = TILES[i]
                    ve.wait_ge(pv_done, hd * 8 + (i + 1))
                    den = [ps[0:tz, 4 + 2 * (i % 2) + d, M_DV:M_DV + 1] for d in range(2)]
                    low = [dd[0:tz, i % 2, d:d + 1] for d in range(2)]
                    for d in range(2):
                        v(ve.tensor_scalar(low[d], den[d], -1.0, ce[0:tz, i, 2 * d + 1:2 * d + 2], ALU.mult, ALU.max))
                    v.wait()
                    for d in range(2):
                        v(ve.tensor_scalar(low[d], den[d], low[d], None, ALU.max))
                    v.wait()
                    v(ve.reciprocal(rd[0:tz, i % 2, :], dd[0:tz, i % 2, :]))
                    v.wait()
                    v(ve.tensor_scalar(hn(i)[0:tz, :], ps[0:tz, 4 + 2 * (i % 2), 0:M_DV], rd[0:tz, i % 2, 0:1], None,
                                       ALU.mult))
                    v.wait()
                    ve.scalar_tensor_tensor(hn(i)[0:tz, :], ps[0:tz, 5 + 2 * (i % 2), 0:M_DV], rd[0:tz, i % 2, 1:2],
                                            hn(i)[0:tz, :], ALU.mult, ALU.add).then_inc(hn_ready, 1)

                ve.wait_ge(mrep_ready, hd * 2 + 2)
                for j in OF_SEQ[0]:
                    diagonals(j)
                for j in OF_SEQ[0]:
                    state_weights(j)
                evacuate(n + 4, 0, wk[:, 4, :])
                for i in OF_SEQ[0]:
                    normalise(i)
                for j in OF_SEQ[1]:
                    diagonals(j)
                for j in OF_SEQ[1]:
                    state_weights(j)
                for i in OF_SEQ[1]:
                    normalise(i)
                evacuate(n + 5, 1, wk[:, 5, :])
                ve.wait_ge(hroot, hd + 1)
                v(ve.reciprocal(rs[:, :], rs[:, :]))
                v.wait()
                ve.wait_ge(hn_ready, hd * 8 + 8)
                for i, (_, t0, tz) in enumerate(TILES):
                    ins = ve.tensor_scalar(hn(i)[0:tz, :], hn(i)[0:tz, :], rs[0:tz, i:i + 1], None, ALU.mult)
                ins.then_inc(hs_ready, 1)
                for c in range(2):
                    ve.wait_ge(y_turned, hd * 2 + (c + 1))
                    ve.wait_ge(sig_ready, hd * 2 + (c + 1))
                    ve.scalar_tensor_tensor(wk[:, c, :], flat(2)[:, c * 1024:c * 1024 + T],
                                            par[:, GHEAD + c:GHEAD + c + 1], wk[:, 4 + c, :],
                                            ALU.mult, ALU.mult).then_inc(yt_ready, 1)
                for c in range(2):
                    split_low(wk[:, c, :], yh[:, bass.ds(hd * 2 + c, 1), :].rearrange("p a b -> p (a b)"),
                              yl[:, bass.ds(hd * 2 + c, 1), :].rearrange("p a b -> p (a b)"), hd * 2 + (c + 1), yl_ready)
                ve.wait_ge(yl_ready, hd * 2 + 2)
            v.loop_end(M_HEADS, M_PER)

            out_blocks(OUT0, 1, FFNN)
            ve.wait_ge(rope_in, 32)
            ve.stream_shuffle(gswap[:, :], par[:, GQ:GQ + 2], SWAP).then_inc(attn_set, 1)
            ve.tensor_scalar(cq[:, :], ck[:, :], par[:, GQ:GQ + 1], None, ALU.mult).then_inc(attn_set, 1)
            ve.wait_ge(attn_set, 2)
            ve.tensor_scalar(ck[:, :], ck[:, :], par[:, GK:GK + 1], None, ALU.mult).then_inc(attn_set, 1)
            ve.tensor_scalar(sq[:, :], sk[:, :], gswap[:, 0:1], None, ALU.mult).then_inc(attn_set, 1)
            ve.wait_ge(attn_set, 4)
            ve.tensor_scalar(sk[:, :], sk[:, :], gswap[:, 1:2], None, ALU.mult).then_inc(attn_set, 1)
            ve.tensor_scalar(gsub[:, :], par[:, GSUB:GSUB + 1], 1.0 - LAMBDA_INIT, None, ALU.mult).then_inc(attn_set, 1)
            ve.wait_ge(lam_in, 64)
            for q in range(2):
                ve.tensor_tensor_reduce(lv[:, 2 * q, :], lv[:, 2 * q, :], lv[:, 2 * q + 1, :], 1.0, 0.0,
                                        ALU.mult, ALU.add, lam[:, q:q + 1]).then_inc(lam_sums, 1)
            ve.wait_ge(lam_exp, 1)
            v(ve.tensor_tensor(lam[:, 6:7], lam[:, 5:6], lam[:, 4:5], ALU.subtract))
            v.wait()
            ve.tensor_scalar(lam[:, 7:8], lam[:, 6:7], -LAMBDA_INIT, None, ALU.add).then_inc(attn_set, 1)
            ffn(FFN0, 0)
            ve.memset(qk2[:, :], 1.0).then_inc(attn_set, 1)
            ve.wait_ge(attn_set, ATTN_SET)
            ROPE_SEGS = ([(a, b, META) for a, b, _ in SEGS], [(0, LENS[0], 0), (LENS[0], T, 0)])

            def rope_start(which, x):
                segs, nt = ROPE_SEGS[which], (TQ, T)[which]
                ve.sem_inc(vector_passed, 1)
                v(ve.stream_shuffle(swapped[:, 0:nt], x, SWAP))
                v.wait()
                for a, b, t in segs:
                    v(ve.tensor_tensor(swapped[:, a:b], swapped[:, a:b], (sq, sk)[which][:, t:t + b - a], ALU.mult))

            def rope_end(which, x, g):
                segs, nt = ROPE_SEGS[which], (TQ, T)[which]
                ve.wait_ge(qsq_ready, g * 2 + (which + 1))
                for a, b, t in segs:
                    v(ve.tensor_tensor(x[:, a:b], x[:, a:b], (cq, ck)[which][:, t:t + b - a], ALU.mult))
                v.wait()
                v(ve.tensor_tensor(x, x, swapped[:, 0:nt], ALU.add))

            def invert_roots(g, odd):
                ve.wait_ge(qk_root, g + 1)
                v(ve.reciprocal(qkr[:, odd, :], qk2[:, :]))
                v.wait()
                v(ve.tensor_scalar(qkr[:, odd, 0:2 * NQ], qkr[:, odd, 0:2 * NQ], D_HD ** -0.5, None, ALU.mult))
                ve.tensor_copy(key_roots.rearrange("p (i f) -> p i f", i=2 * NT),
                               qkr[:, odd, 2 * NQ:2 * (NQ + NT)].unsqueeze(2).to_broadcast([P, 2 * NT, D_HD]))\
                  .then_inc(lt_ready, 1)

            def normalise_k(g, x):
                ve.wait_ge(lt_turned, g + 1)
                v.wait()
                ve.tensor_tensor(x, flat(3)[:, 0:T], x, ALU.mult).then_inc(kn_ready, 1)

            def maxima(hd, odd, i):
                for c in range(2):
                    ve.wait_ge(sc_ready, hd * (2 * NQ) + (2 * i + c + 1))
                    v(ve.tensor_reduce(mx[:, i, c:c + 1], flat(c)[:, 0:LENS[Q_SEQ[i]]], AX.X, ALU.max))
                    v.wait()
                    ve.tensor_scalar(nb[:, i, c:c + 1], mx[:, i, c:c + 1], qkr[:, odd, 2 * i + c:2 * i + c + 1], -1.0,
                                     ALU.mult, ALU.mult).then_inc(nb_ready, 1)

            def combine(hd, i):
                keys = LENS[Q_SEQ[i]]
                ve.wait_ge(probs_ready, hd * (2 * NQ) + (2 * i + 2))
                v(ve.reciprocal(rsum[:, i, :], sums[:, i, :]))
                v.wait()
                v(ve.scalar_tensor_tensor(ratio[:, i:i + 1], sums[:, i, 0:1], lam[:, 7:8], rsum[:, i, 1:2],
                                          ALU.mult, ALU.mult))
                v.wait()
                ve.scalar_tensor_tensor(prob(i, 0)[:, 0:keys], prob(i, 1)[:, 0:keys], ratio[:, i:i + 1],
                                        prob(i, 0)[:, 0:keys], ALU.mult, ALU.add).then_inc(a_ready, 1)

            def output(hd, odd, i):
                ve.wait_ge(o_done, hd * NQ + (i + 1))
                ve.tensor_scalar(on(odd, i), acc_o, rsum[:, i, 0:1], None, ALU.mult).then_inc(o_ready, 1)

            def scale_output(hd, odd):
                ve.wait_ge(oroot, hd + 1)
                v(ve.reciprocal(rs[:, 0:NQ], rs[:, 0:NQ]))
                v.wait()
                ve.wait_ge(o_ready, hd * NQ + NQ)
                for i in range(NQ):
                    ins = ve.tensor_scalar(on(odd, i), on(odd, i), rs[:, i:i + 1], None, ALU.mult)
                ins.then_inc(os_ready, 1)

            def deliver(hd):
                ve.wait_ge(yh_ready, hd + (YL_AT[MIX1] + 1))
                ve.scalar_tensor_tensor(tile_of(yl, hd)[:, 0:TQ], packed_acc(3), gsub[:, 0:1],
                                        tile_of(yh, hd)[:, 0:TQ].bitcast(F32), ALU.mult, ALU.subtract)\
                  .then_inc(yl_ready, 1)

            def head(hd, odd, n, first=False, last=False):
                even = 1 - odd
                qx, kx = wk[:, even, 0:TQ], wk[:, 2 + even, :]
                for i in range(NQ):
                    maxima(hd, odd, i)
                    if i == 5:
                        if not last:
                            invert_roots(hd + 1, even)
                        if not first:
                            scale_output(hd - 1, even)
                    combine(hd, i)
                    if not last:
                        if i == 1:
                            evacuate_inner(n, 3, qx, False)
                        elif i == 2:
                            ve.wait_ge(acc_free, n + (XT + 1))
                            rope_start(0, qx)
                        elif i == 3:
                            rope_end(0, qx, hd + 1)
                            evacuate(n + 1, 3, kx)
                        elif i == 5:
                            evacuate(n + 2, 3, v_raw)
                    if i == 4 and not last:
                        ve.wait_ge(acc_free, n + (XT + 2))
                        rope_start(1, kx)
                        rope_end(1, kx, hd + 1)
                    if i >= 1:
                        output(hd, odd, i - 1)
                if not last:
                    normalise_k(hd + 1, kx)
                output(hd, odd, NQ - 1)
                if not first:
                    deliver(hd - 1)

            evacuate_inner(MIX1, 0, wk[:, 0, 0:TQ], False)
            ve.wait_ge(acc_free, MIX1 + XT + 1)
            rope_start(0, wk[:, 0, 0:TQ])
            rope_end(0, wk[:, 0, 0:TQ], 0)
            evacuate(MIX1 + 1, 1, wk[:, 2, :])
            ve.wait_ge(acc_free, MIX1 + XT + 2)
            v.wait()
            rope_start(1, wk[:, 2, :])
            rope_end(1, wk[:, 2, :], 0)
            invert_roots(0, 0)
            evacuate(MIX1 + 2, 0, v_raw)
            normalise_k(0, wk[:, 2, :])
            head(0, 0, MIX1 + 3, first=True)
            with ve.Fori(0, (D_HEADS - 2) // 2) as it:
                v.loop_start(it, A_PER)
                for sub in range(2):
                    head(it * 2 + (1 + sub), 1 - sub, it * 6 + (MIX1 + 6 + 3 * sub))
            v.loop_end((D_HEADS - 2) // 2, A_PER)
            head(D_HEADS - 1, 1, None, last=True)
            scale_output(D_HEADS - 1, 1)
            deliver(D_HEADS - 1)

            out_blocks(OUT1, 3, FFNN + KT)
            ffn(FFN1, 1)
            for r in range(XT):
                ve.wait_ge(out_turned, r + 1)
                ve.tensor_copy(wkf[:, r * D:(r + 1) * D], flat(r % 2)).then_inc(out_copied, 1)

        @block.scalar
        def _(sc):
            def high(src, dst, ready, done=yh_ready):
                sc.wait_ge(yt_ready, ready)
                sc.sem_inc(scalar_passed, 1)
                sc.activation(dst, src, ACT.Copy).then_inc(done, 1)

            def root(count):
                sc.wait_ge(norm_sum, count)
                dst, src = (two(rstd[:, :]), pair(3)) if count < 4 else (rstd[:, 0:TQ], packed_acc(3))
                sc.activation(dst, src, ACT.Sqrt, bias=epsc, scale=1.0 / D).then_inc(norm_root, 1)

            def out_blocks(n0, norm, gain_at):
                if norm is None:
                    return
                with sc.Fori(0, KT // 2) as i:
                    for j in range(2):
                        m = i * 2 + j
                        c = m + KT * norm
                        hm = h[:, bass.ds(m, 1), :].rearrange("p a b -> p (a b)")
                        sc.wait_ge(acc_free, n0 + m + 1 + XT)
                        sc.sem_inc(scalar_passed, 1)
                        sc.activation(xh[:, bass.ds(m, 1), :].rearrange("p a b -> p (a b)"), hm, ACT.Copy,
                                      scale=par[:, bass.ds(m + gain_at, 1)]).then_inc(xh_ready, 1)
                        sc.wait_ge(sq_summed, c)
                        sc.sem_inc(scalar_passed, 1)
                        sc.activation(wk[:, 7, :], hm, ACT.Square).then_inc(sq_ready, 1)
                root(norm + 1)

            def ffn(n0, layer):
                y0 = YL_AT[n0]
                for g, tiles in enumerate(GROUPS):
                    with sc.Fori(0, tiles) as i:
                        sc.wait_ge(acc_free, n0 + 2 * i + 1 + XT)
                        nt = (T, TQ)[layer]
                        sc.activation(wk[:, 1, 0:nt], wk[:, 0, 0:nt], ACT.Silu).then_inc(silu_ready, 1)
                        high(wk[:, 3, 0:nt], tile_of(yh, i)[:, 0:nt], y0 - D_HEADS * layer + i + 1)
                    n0 += 2 * tiles
                    y0 += tiles
                    last = g == len(GROUPS) - 1
                    out_blocks(n0, {0: 2, 1: None}[layer] if last else None, MIXN + KT)
                    n0 += KT

            sc.wait_ge(acc_free, XT)
            sc.wait_ge(h_ready, 2)
            sc.wait_ge(par_ready, 1)
            for k in range(KT):
                sc.activation(xh[:, k, :], h[:, k, :], ACT.Copy, scale=par[:, MIXN + k:MIXN + k + 1]).then_inc(xh_ready, 1)
                if k:
                    sc.wait_ge(sq_summed, k)
                sc.activation(wk[:, 7, :], h[:, k, :], ACT.Square).then_inc(sq_ready, 1)
            root(1)

            a = Steps(sc, astep)
            sc.wait_ge(gate_x, 1)
            a(sc.activation(wk[:, 5, :], wk[:, 0, :], ACT.Abs))
            a.wait()
            a(sc.activation(wk[:, 5, :], wk[:, 5, :], ACT.Exp, scale=-1.0))
            a.wait()
            sc.wait_ge(ones_set, 1)
            sc.activation(wk[:, 5, :], wk[:, 5, :], ACT.Ln, bias=ones[:, 0:1]).then_inc(gate_soft, 1)
            sc.wait_ge(gate_m, 1)
            for d in range(2):
                sc.activation(cerow[32 + 64 * d:36 + 64 * d, :], wk[64 * d:64 * d + M_HEADS, 5, :], ACT.Exp,
                              scale=-1.0).then_inc(gate_e, 1)

            with sc.Fori(0, M_HEADS) as hd:
                sc.wait_ge(mrep_done, hd + 1)
                for d in range(2):
                    sc.activation(two(wk[:, 2 + d, :]), pair(2 + d), ACT.Copy).then_inc(mrep_ready, 1)
                sc.wait_ge(v_turned, hd + 1)
                sc.activation(vn[:, 0:4, 0:M_DV], flat(2)[:, 0:4 * M_DV].rearrange("p (i c) -> p i c", i=4),
                              ACT.Copy).then_inc(vn_ready, 1)
                sc.activation(vn[:, 5:7, 0:M_DV], flat(2)[:, 4 * M_DV:6 * M_DV].rearrange("p (i c) -> p i c", i=2),
                              ACT.Copy).then_inc(vn_ready, 1)
                sc.activation(vn[0:META, 4:8:3, 0:M_DV],
                              flat(2)[0:META, 6 * M_DV:8 * M_DV].rearrange("p (i c) -> p i c", i=2),
                              ACT.Copy).then_inc(vn_ready, 1)

                def decays(j):
                    s, t0, tz = TILES[j]
                    q, a = j - OF_SEQ[s][0], t0 - START[s]
                    first = OF_SEQ[s][0] if s else 0
                    sc.wait_ge(diag_ready, hd * 16 + (2 * j + 2))
                    ops = [(wt[0:tz, q, a + tz:a + 2 * tz], wt[0:tz, q, a + tz:a + 2 * tz], 0)]
                    if a + tz < LENS[s]:
                        ops.append((wt[0:tz, q, a + 2 * tz:LENS[s] + tz], wk[0:tz, 2, t0 + tz:START[s] + LENS[s]], 0))
                    if a:
                        ops.append((wt[0:tz, q, 0:a], wk[0:tz, 3, START[s]:t0], 1))
                    ops.append((wt[0:tz, q, a:a + tz], wt[0:tz, q, a:a + tz], 1))
                    for dst, src, d in ops:
                        ins = sc.activation(dst, src, ACT.Exp, bias=ce[0:tz, j, 2 * d:2 * d + 1], scale=-1.0)
                    ins.then_inc(e_ready, 1)

                def squares(i):
                    s, t0, tz = TILES[i]
                    sc.wait_ge(hn_ready, hd * 8 + (i + 1))
                    if i:
                        sc.wait_ge(hsq_ready, hd * 8 + i)
                    sc.activation(wkf[0:tz, 0:M_DV], hn(i)[0:tz, :], ACT.Square, accum_out=ss[0:tz, i:i + 1])\
                      .then_inc(hsq_ready, 1)

                sc.wait_ge(ce_ready, hd * 4 + 4)
                for j in OF_SEQ[0]:
                    decays(j)
                for i in OF_SEQ[0]:
                    squares(i)
                for j in OF_SEQ[1]:
                    decays(j)
                for i in OF_SEQ[1]:
                    squares(i)
                sc.wait_ge(hsq_ready, hd * 8 + 8)
                sc.activation(rs[:, :], ss[:, :], ACT.Sqrt, bias=epsc, scale=1.0 / M_DV).then_inc(hroot, 1)
                for c in range(2):
                    sc.wait_ge(acc_free, MIX0 + hd * 6 + (5 + c + XT))
                    sc.activation(wk[:, 4 + c, :], wk[:, 4 + c, :], ACT.Sigmoid).then_inc(sig_ready, 1)
                for c in range(2):
                    high(wk[:, c, :], yh[:, bass.ds(hd * 2 + c, 1), :].rearrange("p a b -> p (a b)"), hd * 2 + (c + 1))

            out_blocks(OUT0, 1, FFNN)
            sc.dma_start(ck[:, :], rope[:, 0, :]).then_inc(rope_in, 16)
            sc.dma_start(sk[:, :], rope[:, 1, :]).then_inc(rope_in, 16)
            for q, src in enumerate((d_lam_q1, d_lam_k1, d_lam_q2, d_lam_k2)):
                sc.dma_start(lv[:, q, :], src.to_broadcast([P, D_HD])).then_inc(lam_in, 16)
            sc.wait_ge(lam_sums, 2)
            sc.activation(lam[:, 4:6], lam[:, 0:2], ACT.Exp).then_inc(lam_exp, 1)
            ffn(FFN0, 0)

            def squares_of(which, x, done):
                sc.wait_ge(acc_free, done)
                sc.activation((q_sq, k_sq)[which], x, ACT.Square).then_inc(qsq_ready, 1)

            def qk_roots(g):
                sc.wait_ge(qks_done, g + 1)
                end = 2 * (NQ + NT - 1)
                for rows, a, b in ((P, 0, end), (META, end, end + 2)):
                    ins = sc.activation(qk2[0:rows, a:b], ps[0:rows, 5, 2 * P + a:2 * P + b], ACT.Sqrt,
                                        bias=epsc[0:rows, :], scale=1.0 / D_HD)
                ins.then_inc(qk_root, 1)

            def output_roots(hd, odd):
                sc.wait_ge(osq_ready, hd * NQ + NQ)
                sc.activation(rs[:, 0:NQ], oss[:, odd, :], ACT.Sqrt, bias=epsc, scale=1.0 / P).then_inc(oroot, 1)

            def values(g, odd):
                sc.wait_ge(va_turned, g + 1)
                src = flat(3).rearrange("p (i c) -> p i c", i=NT)
                sc.activation(va[:, odd, 0:4, :], src[:, 0:4, :], ACT.Copy).then_inc(va_ready, 1)
                sc.activation(va[:, odd, 5:7, :], src[:, 4:6, :], ACT.Copy).then_inc(va_ready, 1)
                sc.activation(va[0:META, odd, 4:8:3, :], src[0:META, 6:8, :], ACT.Copy).then_inc(va_ready, 1)

            def exps(hd, odd, i):
                keys = LENS[Q_SEQ[i]]
                for c in range(2):
                    sc.wait_ge(nb_ready, hd * (2 * NQ) + (2 * i + c + 1))
                    sc.activation(prob(i, c)[:, 0:keys], flat(c)[:, 0:keys], ACT.Exp, bias=nb[:, i, c:c + 1],
                                  scale=qkr[:, odd, 2 * i + c:2 * i + c + 1], accum_out=sums[:, i, c:c + 1]).then_inc(probs_ready, 1)

            def turned(hd, i):
                sc.wait_ge(a_turned, hd * NQ + (i + 1))
                full = len(OF_SEQ[Q_SEQ[i]]) - 1
                sc.activation(at[:, i % 2, 0:full, :], ps[:, 4, 0:full * P].rearrange("p (q c) -> p q c", q=full), ACT.Copy)
                sc.activation(at[0:META, i % 2, full, :], ps[0:META, 5, 0:P], ACT.Copy).then_inc(at_ready, 1)

            def squared(hd, odd, i):
                sc.wait_ge(o_ready, hd * NQ + (i + 1))
                if i:
                    sc.wait_ge(osq_ready, hd * NQ + i)
                sc.activation(junk, on(odd, i), ACT.Square, accum_out=oss[:, odd, i:i + 1]).then_inc(osq_ready, 1)

            def deliver(hd):
                sc.wait_ge(o_turned, hd + 1)
                sc.sem_inc(scalar_passed, 1)
                sc.activation(tile_of(yh, hd)[:, 0:TQ], packed_acc(3), ACT.Copy, scale=gsub[:, 0:1]).then_inc(yh_ready, 1)

            def head(hd, odd, n, first=False, last=False):
                even = 1 - odd
                exps(hd, odd, 0)
                values(hd, odd)
                exps(hd, odd, 1)
                turned(hd, 0)
                if not last:
                    squares_of(0, wk[:, even, 0:TQ], n + (XT + 1))
                exps(hd, odd, 2)
                turned(hd, 1)
                squared(hd, odd, 0)
                exps(hd, odd, 3)
                turned(hd, 2)
                squared(hd, odd, 1)
                if not last:
                    squares_of(1, wk[:, 2 + even, :], n + (XT + 2))
                exps(hd, odd, 4)
                squared(hd, odd, 2)
                sc.wait_ge(a_turned, hd * NQ + 4)
                if not last:
                    qk_roots(hd + 1)
                if not first:
                    output_roots(hd - 1, even)
                turned(hd, 3)
                exps(hd, odd, 5)
                turned(hd, 4)
                squared(hd, odd, 3)
                turned(hd, 5)
                squared(hd, odd, 4)
                if not first:
                    deliver(hd - 1)
                squared(hd, odd, 5)

            squares_of(0, wk[:, 0, 0:TQ], MIX1 + XT + 1)
            squares_of(1, wk[:, 2, :], MIX1 + XT + 2)
            qk_roots(0)
            head(0, 0, MIX1 + 3, first=True)
            with sc.Fori(0, (D_HEADS - 2) // 2) as it:
                for sub in range(2):
                    head(it * 2 + (1 + sub), 1 - sub, it * 6 + (MIX1 + 6 + 3 * sub))
            head(D_HEADS - 1, 1, None, last=True)
            output_roots(D_HEADS - 1, 1)
            deliver(D_HEADS - 1)
            out_blocks(OUT1, 3, FFNN + KT)
            ffn(FFN1, 1)


_INS = ['x_prompt', 'x_sample', 'meta_tokens', 'norm_mix', 'norm_ffn', 'm_w_in', 'm_b_gate', 'm_g_head', 'm_w_out',
        'd_w_in', 'd_g_q', 'd_g_k', 'd_lam_q1', 'd_lam_k1', 'd_lam_q2', 'd_lam_k2', 'd_g_sub', 'd_w_out',
        'ffn_w_in', 'ffn_w_out']
_OUTS = [((1, 512, D), 'float32'), ((1, 256, D), 'float32')]


def kernel(**inputs):
    import numpy as _np
    import concourse.bacc as _bacc
    from concourse import mybir as _mybir
    from concourse.bass_utils import run_bass_kernel_spmd as _run

    nc = _bacc.Bacc("TRN2", target_bir_lowering=False, num_devices=1)
    arrays, args = {}, []
    consts, rope = host_constants()
    for name, a in [(n, inputs[n]) for n in _INS] + [("consts", consts), ("rope", rope)]:
        a = _np.ascontiguousarray(a)
        arrays[f"in_{name}_dram"] = a
        args.append(nc.dram_tensor(f"in_{name}_dram", a.shape, _mybir.dt.from_np(a.dtype), kind="ExternalInput").ap())
    for i, (shape, dtype) in enumerate(_OUTS):
        dt = _mybir.dt.from_np(_np.dtype(dtype))
        args.append(nc.dram_tensor(f"out_{i}_dram", shape, dt, kind="ExternalOutput").ap())
    trunk(nc, *args)
    r = _run(nc, [arrays], core_ids=[0])
    return tuple(r.results[0][f"out_{i}_dram"] for i in range(len(_OUTS)))
```

```python
import math
from contextlib import ExitStack

import concourse.bass as bass
from concourse import mybir

F32 = mybir.dt.float32
F32R = mybir.dt.float32r
ALU = mybir.AluOpType
ACT = mybir.ActivationFunctionType
AX = mybir.AxisListType

P = 128
D = 1024
KT = D // P
META = 16
LENS = (META + 512, META + 256)
T = sum(LENS)
HT = T // 2
SEGS = ((0, LENS[0] - META, META), (LENS[0] - META, T - 2 * META, LENS[0] + META))
TQ = T - 2 * META
FF = 2816
FT = FF // P
GROUPS = (8, 8, 6)
M_HEADS, M_DK, M_DV = 4, 128, 256
D_HEADS, D_HD = 8, 64
EPS = 1e-6
FAR = 1e30
LAMBDA_INIT = 0.8 - 0.6 * math.exp(-0.3)
ROPE_THETA, ROPE_DIM = 500000.0, D_HD // 4

TILES = [(s, t0, min(P, LENS[s] - a)) for s in (0, 1) for a in range(0, LENS[s], P)
         for t0 in (sum(LENS[:s]) + a,)]
START = (0, LENS[0])
OF_SEQ = ([0, 1, 2, 3, 4], [5, 6, 7])
NT = len(TILES)
NQ = TQ // P
Q_SEQ = (0, 0, 0, 0, 1, 1)

MIX0 = 0
OUT0 = MIX0 + 6 * M_HEADS
FFN0 = OUT0 + KT
NFF = 2 * FT + KT * len(GROUPS)
MIX1 = FFN0 + NFF
OUT1 = MIX1 + 3 * D_HEADS
FFN1 = OUT1 + KT
BLOCKS = FFN1 + NFF
XT = 6
YL_AT = {OUT0: 2 * M_HEADS, FFN0: 2 * M_HEADS, MIX1: 2 * M_HEADS + FT,
         OUT1: 2 * M_HEADS + FT + D_HEADS, FFN1: 2 * M_HEADS + FT + D_HEADS}
GATE_COLS = 2 * M_HEADS * M_DK + 2 * M_HEADS * M_DV
M_PER = 57
A_PER = 78
ATTN_SET = 8
SWAP = [i ^ (ROPE_DIM // 2) if i < ROPE_DIM else i for i in range(32)]

MIXN, FFNN, GHEAD, GSUB, GQ, GK, BGATE = 0, 16, 32, 34, 35, 36, 37
NPAR = 38
IDENT, MASKF, MASKB, ONEHOT, COMP, NCONST = 0, 128, 256, 384, 388, 390


def host_constants():
    import numpy as np
    c = np.zeros((P, NCONST), np.float32)
    r = np.arange(P)
    c[r, IDENT + r] = 1.0
    c[:, MASKF:MASKF + P] = np.where(r[None, :] >= r[:, None], 0.0, FAR)
    c[:, MASKB:MASKB + P] = np.where(r[None, :] <= r[:, None], 0.0, FAR)
    half = ROPE_DIM // 2
    c[0:D_HD, COMP] = 1.0
    c[D_HD:P, COMP + 1] = 1.0
    for h in range(M_HEADS):
        c[h, ONEHOT + h] = 1.0
        c[64 + h, ONEHOT + h] = 1.0
    inv = np.float32(ROPE_THETA) ** (-np.arange(0, ROPE_DIM, 2, dtype=np.float32) / np.float32(ROPE_DIM))
    rope = np.zeros((P, 2, LENS[0]), np.float32)
    rope[:, 0, :] = 1.0
    ang = np.arange(LENS[0], dtype=np.float32)[:, None] * inv.astype(np.float32)[None, :]
    cos, sin = np.cos(ang).T, np.sin(ang).T
    for base in (0, D_HD):
        rope[base:base + half, 0, :] = cos
        rope[base + half:base + ROPE_DIM, 0, :] = cos
        rope[base:base + half, 1, :] = -sin
        rope[base + half:base + ROPE_DIM, 1, :] = sin
    return c, rope


class Steps:

    def __init__(self, eng, sem):
        self.eng, self.sem, self.base, self.n = eng, sem, 0, 0

    def __call__(self, ins):
        ins.then_inc(self.sem, 1)
        self.n += 1

    def wait(self):
        self.eng.wait_ge(self.sem, self.base + self.n)

    def loop_start(self, i, per):
        self.entry = self.base + self.n
        self.base = i * per + self.entry
        self.n = 0

    def loop_end(self, count, per):
        assert self.n == per, (self.n, per)
        self.base, self.n = self.entry + count * per, 0


def trunk(nc, x_prompt, x_sample, meta_tokens, norm_mix, norm_ffn, m_w_in, m_b_gate, m_g_head, m_w_out,
          d_w_in, d_g_q, d_g_k, d_lam_q1, d_lam_k1, d_lam_q2, d_lam_k2, d_g_sub, d_w_out,
          ffn_w_in, ffn_w_out, consts, rope, y_prompt, y_sample):
    ctx = ExitStack()
    with ctx:
        def sb(name, shape, dt=F32, where=None):
            return (where or ctx).enter_context(nc.sbuf_tensor(name, shape, dt))

        def sem(name):
            return ctx.enter_context(nc.semaphore(name))

        h = sb("h", [P, KT, T])
        xh, xl = sb("xh", [P, KT, T], F32R), sb("xl", [P, KT, T], F32R)
        y_memory = ExitStack()
        yh = sb("yh", [P, KT, T], F32R, y_memory)
        yl = sb("yl", [P, KT, T], F32R, y_memory)
        y_memory.close()
        spare = sb("spare", [P, 2, KT, T])
        raw = sb("raw", [P, 2, KT * P])
        wh, wl = sb("wh", [P, 2, KT * P], F32R), sb("wl", [P, 2, KT * P], F32R)
        rstd = sb("rstd", [P, T])
        cst = sb("cst", [P, NCONST])
        ones = sb("ones", [P, P])
        par = sb("par", [P, NPAR])
        small = sb("small", [P, 4])
        ss = sb("ss", [P, NT])
        rs = sb("rs", [P, NT])
        wk = sb("wk", [P, 9, T])
        wkf = wk[:, :, :].rearrange("p a b -> p (a b)")
        epsc = small[:, 0:1]

        gate_phase = ExitStack()
        graw = sb("graw", [P, KT, 16], F32, gate_phase)
        gwh = sb("gwh", [P, KT, P], F32R, gate_phase)
        gwl = sb("gwl", [P, KT, P], F32R, gate_phase)
        prow = sb("prow", [NPAR, P], F32, gate_phase)
        gate_phase.close()

        mlstm_phase = ExitStack()
        vn = sb("vn", [P, NT, M_DV + 1], F32, mlstm_phase)
        wt = sb("wt", [P, 5, LENS[0] + P], F32, mlstm_phase)
        mrow = sb("mrow", [P, T], F32, mlstm_phase)
        ce = sb("ce", [P, NT, 4], F32, mlstm_phase)
        dd = sb("dd", [P, 2, 2], F32, mlstm_phase)
        rd = sb("rd", [P, 2, 2], F32, mlstm_phase)
        mlstm_phase.close()

        attn_phase = ExitStack()
        cq = sb("cq", [P, LENS[0]], F32, attn_phase)
        ck = sb("ck", [P, LENS[0]], F32, attn_phase)
        sq = sb("sq", [P, LENS[0]], F32, attn_phase)
        sk = sb("sk", [P, LENS[0]], F32, attn_phase)
        va = sb("va", [P, 2, NT, P], F32, attn_phase)
        at = sb("at", [P, 2, 5, P], F32, attn_phase)
        qk2 = sb("qk2", [P, 2 * (NQ + NT)], F32, attn_phase)
        qkr = sb("qkr", [P, 2, 2 * (NQ + NT)], F32, attn_phase)
        oss = sb("oss", [P, 2, NQ], F32, attn_phase)
        mx = sb("mx", [P, NQ, 2], F32, attn_phase)
        nb = sb("nb", [P, NQ, 2], F32, attn_phase)
        sums = sb("sums", [P, NQ, 2], F32, attn_phase)
        rsum = sb("rsum", [P, NQ, 2], F32, attn_phase)
        ratio = sb("ratio", [P, NQ], F32, attn_phase)
        lv = sb("lv", [P, 4, D_HD], F32, attn_phase)
        lam = sb("lam", [P, 8], F32, attn_phase)
        gsub = sb("gsub", [P, 1], F32, attn_phase)
        gswap = sb("gswap", [P, 2], F32, attn_phase)
        attn_phase.close()

        ps = ctx.enter_context(nc.psum_tensor("ps", [P, 8, 512], F32))

        def pair(p, rows=P):
            return ps[0:rows, 2 * p:2 * p + 2, 0:HT]

        def flat(p):
            return ps[:, 2 * p:8 if p == 2 else 2 * p + 2, :].rearrange("p a b -> p (a b)")

        def two(x):
            return x.rearrange("p (a b) -> p a b", a=2)

        def packed_acc(p):
            return flat(p)[:, 0:TQ]

        def tile_of(x, k):
            return x[:, bass.ds(k, 1), :].rearrange("p a b -> p (a b)")

        ident = cst[:, IDENT:IDENT + P]

        cerow = wk[:, 8, :]
        q_sq, k_sq, swapped, v_raw = spare[:, 0, 6, 0:TQ], spare[:, 0, 7, :], spare[:, 1, 6, :], spare[:, 1, 7, :]
        key_roots = spare[:, 0, 6:8, :].rearrange("p a b -> p (a b)")[:, 0:NT * P]
        PROBS = 4 * T
        ON = PROBS + 4 * LENS[0]
        JUNK = ON + 2 * NQ * P
        junk = wkf[:, JUNK:JUNK + P]

        def hn(i):
            at_col = {4: T, 7: T + M_DV}[i] if TILES[i][2] < P else 6 * T + (i - (i > 4)) * M_DV
            return wkf[:, at_col:at_col + M_DV]

        def on(odd, i):
            at_col = ON + (odd * NQ + i) * P
            return wkf[:, at_col:at_col + P]

        def prob(i, c):
            at_col = PROBS + (2 * (i % 2) + c) * LENS[0]
            return wkf[:, at_col:at_col + LENS[0]]

        acc_o = ps[:, 5, P:2 * P]

        consts_in, params_in, meta_in, gate_in = sem("consts_in"), sem("params_in"), sem("meta_in"), sem("gate_in")
        x_in = [sem(f"x_in{r}") for r in range(XT)]
        raw_in = [sem("raw_in0"), sem("raw_in1")]
        rope_in, lam_in, out_done = sem("rope_in"), sem("lam_in"), sem("out_done")
        pool_set, w_hi, w_split = sem("pool_set"), sem("w_hi"), sem("w_split")
        gate_split = sem("gate_split")
        x_turned, meta_turned, par_turned, par_ready = sem("x_turned"), sem("meta_turned"), sem("par_turned"), sem("par_ready")
        h_ready = sem("h_ready")
        acc_free, block_done = sem("acc_free"), sem("block_done")
        xh_ready, xl_ready, sq_ready, sq_summed = sem("xh_ready"), sem("xl_ready"), sem("sq_ready"), sem("sq_summed")
        norm_sum, norm_root, rstd_ready = sem("norm_sum"), sem("norm_root"), sem("rstd_ready")
        vstep, astep, ones_set = sem("vstep"), sem("astep"), sem("ones_set")
        gates_done, gate_x, gate_soft, gate_m, gate_e = (sem(n) for n in ("gates_done", "gate_x", "gate_soft", "gate_m", "gate_e"))
        mrow_masked, mrep_done, mrep_ready = sem("mrow_masked"), sem("mrep_done"), sem("mrep_ready")
        ce_turned, ce_ready = sem("ce_turned"), sem("ce_ready")
        v_turned, vn_ready = sem("v_turned"), sem("vn_ready")
        s_ready, diag_ready, e_ready, wt_ready = sem("s_ready"), sem("diag_ready"), sem("e_ready"), sem("wt_ready")
        pv_done, hn_ready, hsq_ready, hroot = sem("pv_done"), sem("hn_ready"), sem("hsq_ready"), sem("hroot")
        hs_ready, sig_ready = sem("hs_ready"), sem("sig_ready")
        y_turned, yt_ready, yh_ready, yl_ready = sem("y_turned"), sem("yt_ready"), sem("yh_ready"), sem("yl_ready")
        silu_ready = sem("silu_ready")
        qsq_ready, qks_done, qk_root = sem("qsq_ready"), sem("qks_done"), sem("qk_root")
        lt_ready, lt_turned, kn_ready = sem("lt_ready"), sem("lt_turned"), sem("kn_ready")
        va_turned, va_ready = sem("va_turned"), sem("va_ready")
        sc_ready, nb_ready, probs_ready, a_ready = sem("sc_ready"), sem("nb_ready"), sem("probs_ready"), sem("a_ready")
        a_turned, at_ready, o_done, o_ready, osq_ready, oroot = (sem(n) for n in ("a_turned", "at_ready", "o_done", "o_ready", "osq_ready", "oroot"))
        os_ready, o_turned = sem("os_ready"), sem("o_turned")
        lam_sums, lam_exp, attn_set = sem("lam_sums"), sem("lam_exp"), sem("attn_set")
        out_turned, out_copied = sem("out_turned"), sem("out_copied")
        pool_passed, scalar_passed, vector_passed = sem("pool_passed"), sem("scalar_passed"), sem("vector_passed")

        block = ctx.enter_context(nc.Block())

        @block.sync
        def _(sp):
            def weights(n, slot, src, k=KT):
                sp.wait_ge(w_split, n - 1)
                sp.dma_start(raw[:, slot, 0:k * P].rearrange("p (k c) -> p k c", k=k),
                             src).then_inc(raw_in[slot], 16)

            def cols(w, c):
                return w.rearrange("(k p) n -> p k n", p=P)[:, :, bass.ds(c, P)]

            def mlstm_cols(hd, j):
                qk, v = M_HEADS * M_DK, M_HEADS * M_DV
                return cols(m_w_in[0], (hd * M_DK, qk + hd * M_DK, 2 * qk + hd * M_DV, 2 * qk + hd * M_DV + P,
                                        2 * qk + v + hd * M_DV, 2 * qk + v + hd * M_DV + P)[j])

            def out_blocks(n0, w):
                with sp.Fori(0, KT // 2) as i:
                    for j in range(2):
                        weights(n0 + 2 * i + j, j, cols(w, i * (2 * P) + j * P))

            def ffn_blocks(n0, layer):
                w_in, w_out = ffn_w_in[layer], ffn_w_out[layer]
                at_tile = 0
                for tiles in GROUPS:
                    with sp.Fori(0, tiles) as i:
                        for j in range(2):
                            weights(n0 + 2 * i + j, j, cols(w_in, i * P + (at_tile * P + j * FF)))
                    n0 += 2 * tiles
                    rows = w_out[at_tile * P:(at_tile + tiles) * P, :]
                    with sp.Fori(0, KT // 2) as i:
                        for j in range(2):
                            weights(n0 + 2 * i + j, j, cols(rows, i * (2 * P) + j * P), tiles)
                    n0 += KT
                    at_tile += tiles

            sp.dma_start(cst[:, :], consts).then_inc(consts_in, 16)
            for r in range(XT):
                src = x_prompt[0, r * P:(r + 1) * P, :] if r < 4 else x_sample[0, (r - 4) * P:(r - 3) * P, :]
                sp.dma_start(wkf[:, r * D:(r + 1) * D], src).then_inc(x_in[r], 16)
                if r == 0:
                    sp.dma_start(wkf[0:META, XT * D:(XT + 1) * D], meta_tokens).then_inc(meta_in, 16)
            for j in range(2, 6):
                weights(MIX0 + j, j % 2, mlstm_cols(0, j))
            with sp.Fori(1, M_HEADS) as hd:
                for j in range(6):
                    weights(MIX0 + hd * 6 + j, j % 2, mlstm_cols(hd, j))
            out_blocks(OUT0, m_w_out[0])
            ffn_blocks(FFN0, 0)
            with sp.Fori(0, D_HEADS // 2) as i:
                for j in range(6):
                    weights(MIX1 + i * 6 + j, j % 2, cols(d_w_in[0], i * (2 * P) + (j // 3) * P + (j % 3) * D))
            out_blocks(OUT1, d_w_out[0])
            ffn_blocks(FFN1, 1)
            for m in range(KT):
                sp.wait_ge(out_copied, m + 1)
                for y, a, b in ((y_prompt, 0, LENS[0] - META), (y_sample, LENS[0] - META, TQ)):
                    sp.dma_start(y[0].rearrange("(r p) n -> p r n", p=P)[:, :, m * P:(m + 1) * P],
                                 wkf[:, m * TQ + a:m * TQ + b].rearrange("p (r c) -> p r c", c=P)).then_inc(out_done, 16)
            sp.wait_ge(out_done, 16 * 2 * KT)

        @block.gpsimd
        def _(pool):
            pool.memset(prow[:, :], 0.0).then_inc(pool_set, 1)
            pool.memset(gwh[:, :, :].bitcast(F32), 0.0).then_inc(pool_set, 1)
            pool.memset(gwl[:, :, :].bitcast(F32), 0.0).then_inc(pool_set, 1)
            pool.wait_ge(pool_set, 3)
            pool.wait_ge(gate_in, 16)
            spread = [x[:, :, :].rearrange("p k (g c) -> p k g c", g=4)[:, :, :, 0:M_HEADS] for x in (gwh, gwl)]
            source = graw[:, :, :].rearrange("p k (g c) -> p k g c", g=4)
            for k in range(KT):
                pool.tensor_copy(spread[0][:, k], source[:, k]).then_inc(gate_split, 1)
            pool.wait_ge(gate_split, KT)
            for k in range(KT):
                pool.tensor_tensor(spread[1][:, k], source[:, k], spread[0][:, k].bitcast(F32),
                                   ALU.subtract).then_inc(gate_split, 1)

            def split(n, slot, times, wait=True):
                if wait:
                    pool.wait_ge(block_done, n - 1)
                pool.wait_ge(raw_in[slot], 16 * times)
                pool.sem_inc(pool_passed, 1)
                pool.tensor_copy(wh[:, slot, :], raw[:, slot, :]).then_inc(w_hi, 1)
                pool.wait_ge(w_hi, n + 1)
                pool.tensor_tensor(wl[:, slot, :], raw[:, slot, :], wh[:, slot, :].bitcast(F32),
                                   ALU.subtract).then_inc(w_split, 1)

            for slot in range(2):
                split(slot, slot, 1, wait=False)
            with pool.Fori(1, BLOCKS // 2) as i:
                for slot in range(2):
                    split(i * 2 + slot, slot, i + 1)

        @block.tensor
        def _(pe):
            def run_block(n, slot, p, xs=(xh, xl), k_tiles=KT, between={}, tokens="all", free=True, k0=0, k1=None,
                          weave={}):
                if k0 == 0:
                    pe.wait_ge(w_split, n + 1)
                    if free:
                        pe.wait_ge(acc_free, n + XT - 1)
                parts = {"all": [(ps[:, 2 * p + half, 0:HT], half * HT, (half + 1) * HT) for half in range(2)],
                         "inner": [(flat(p)[:, a:b], t, t + b - a) for a, b, t in SEGS],
                         "packed": [(flat(p)[:, a:b], a, b) for a, b, t in SEGS]}[tokens]
                for k in range(k0, k1 or k_tiles):
                    small = list(weave.get(k, ()))
                    for q, (w, x) in enumerate(((wh, xs[0]), (wh, xs[1]), (wl, xs[0]))):
                        for out, a, b in parts:
                            mm = pe.matmul(out, w[:, slot, k * P:(k + 1) * P], x[:, k, a:b], start=(k + q == 0),
                                           stop=(k == k_tiles - 1 and q == 2), skip_group_check=True)
                            for f in small[:2]:
                                f()
                            del small[:2]
                    if k == k_tiles - 1:
                        mm.then_inc(block_done, 1)
                    for f in between.get(k, ()):
                        f()

            def sum_squares(count):
                pe.wait_ge(sq_summed, KT * count)
                parts = ([(ps[:, 6 + half, 0:HT], half * HT, (half + 1) * HT) for half in range(2)] if count < 4 else
                         [(flat(3)[:, a:b], t, t + b - a) for a, b, t in SEGS])
                for out, a, b in parts:
                    mm = pe.matmul(out, ones[:, :], wk[:, 6, a:b], start=True, stop=True)
                mm.then_inc(norm_sum, 1)

            def out_blocks(n0, y, tiles, tokens, late=1, between=None):
                def tile_ready(count):
                    return lambda: pe.wait_ge(yl_ready, count)

                pe.wait_ge(yl_ready, y - late)
                between = dict(between or {})
                for q in range(late):
                    before = tiles - late + q - 1
                    between[before] = between.get(before, []) + [tile_ready(y - late + q + 1)]
                run_block(n0, 0, 0, (yh, yl), tiles, between, tokens)
                more_out_blocks(n0, tiles, tokens)

            def more_out_blocks(n0, tiles, tokens):
                run_block(n0 + 1, 1, 1, (yh, yl), tiles, tokens=tokens)
                with pe.Fori(1, KT // 2) as i:
                    for j in range(2):
                        run_block(n0 + 2 * i + j, j, j, (yh, yl), tiles, tokens=tokens)

            def turn_result(m):
                pe.wait_ge(acc_free, BLOCKS - KT + m + (1 + XT))
                if m >= 2:
                    pe.wait_ge(out_copied, m - 1)
                for r in range(NQ):
                    t0 = META + r * P if r < 4 else LENS[0] + META + (r - 4) * P
                    at_col = (m % 2) * 1024 + r * P
                    mm = pe.transpose(flat(2)[:, at_col:at_col + P], h[:, m, t0:t0 + P], ident)
                mm.then_inc(out_turned, 1)

            def last_blocks(n0, y, tiles):
                pe.wait_ge(yl_ready, y - 1)
                for m in range(KT):
                    inside = {tiles - 2: [lambda: pe.wait_ge(yl_ready, y)]} if m == 0 else \
                             {tiles - 3: [lambda m=m: turn_result(m - 1)]}
                    run_block(n0 + m, m % 2, m % 2, (yh, yl), tiles, inside, "packed")
                turn_result(KT - 1)

            def norm_ends(count):
                pe.wait_ge(xl_ready, KT * count)
                sum_squares(count)

            def ffn(n0, layer):
                y = YL_AT[n0]
                inner, packed = (("all", "all"), ("inner", "packed"))[layer]
                pe.wait_ge(xl_ready, KT * (2 * layer + 2) - 1)
                for g, tiles in enumerate(GROUPS):
                    run_block(n0, 0, 0, tokens=inner,
                              between={KT - 2: [lambda: norm_ends(2 * layer + 2)]} if g == 0 else {})
                    run_block(n0 + 1, 1, 1, tokens=inner)
                    with pe.Fori(1, tiles) as i:
                        for j in range(2):
                            run_block(n0 + 2 * i + j, j, j, tokens=inner)
                    n0 += 2 * tiles
                    y += tiles
                    if layer == 1 and g == len(GROUPS) - 1:
                        last_blocks(n0, y, tiles)
                    else:
                        out_blocks(n0, y, tiles, packed)
                    n0 += KT

            pe.wait_ge(consts_in, 16)
            for r in range(XT):
                pe.wait_ge(x_in[r], 16)
                if r >= 2:
                    pe.wait_ge(acc_free, r - 1)
                for k in range(KT):
                    mm = pe.transpose(flat(r % 2)[:, k * P:(k + 1) * P], wkf[:, r * D + k * P:r * D + (k + 1) * P], ident)
                mm.then_inc(x_turned, 1)
                if r == XT - 1:
                    pe.wait_ge(meta_in, 16)
                    for k in range(KT):
                        mm = pe.transpose(ps[:, 4, k * META:(k + 1) * META],
                                          wkf[0:META, XT * D + k * P:XT * D + (k + 1) * P], ident[0:META, 0:META])
                    mm.then_inc(meta_turned, 1)
                    pe.wait_ge(params_in, 16 * 12)
                    pe.transpose(ps[:, 5, 0:NPAR], prow[:, :], ident[0:NPAR, 0:NPAR]).then_inc(par_turned, 1)

            pe.wait_ge(gate_split, 2 * KT)
            pe.wait_ge(par_ready, 1)
            pe.wait_ge(h_ready, 2)
            for k in range(KT):
                pe.wait_ge(xl_ready, k + 1)
                first = k == 0
                for w, x in ((gwh, xh), (gwh, xl), (gwl, xh)):
                    for half in range(2):
                        mm = pe.matmul(ps[:, 4 + half, 0:HT], w[:, k, :], x[:, k, half * HT:(half + 1) * HT],
                                       start=first, stop=(k == KT - 1 and w is gwl), skip_group_check=True)
                    first = False
                if k == KT - 1:
                    mm.then_inc(gates_done, 1)
                run_block(MIX0, 0, 0, k0=k, k1=k + 1)
            sum_squares(1)

            def mlstm_head(hd, n, first=False, last=False):
                def repeat_m():
                    pe.wait_ge(mrow_masked, hd + 1)
                    for d in range(2):
                        for half in range(2):
                            mm = pe.matmul(ps[:, 4 + 2 * d + half, 0:HT], ones[64 * d:64 * d + 32, :],
                                           wk[64 * d:64 * d + 32, 4, half * HT:(half + 1) * HT], start=True, stop=True)
                    mm.then_inc(mrep_done, 1)

                def turn_ce():
                    pe.wait_ge(mrep_ready, hd * 2 + 2)
                    pe.wait_ge(gate_e, 2)
                    for i, (_, t0, tz) in enumerate(TILES):
                        mm = pe.transpose(flat(2)[0:tz, i * P:(i + 1) * P], cerow[:, t0:t0 + tz], ident)
                    mm.then_inc(ce_turned, 1)

                def turn_v(c):
                    pe.wait_ge(ce_ready, hd * 4 + 4)
                    pe.wait_ge(acc_free, n + (XT + 3 + c))
                    for i, (_, t0, tz) in enumerate(TILES):
                        at_col = (i if i < 4 else {5: 4, 6: 5, 4: 6, 7: 7}[i]) * M_DV
                        mm = pe.transpose(flat(2)[0:tz, at_col + c * P:at_col + (c + 1) * P],
                                          wk[:, 6 + c, t0:t0 + tz], ident)
                    if c == 1:
                        mm.then_inc(v_turned, 1)

                def scores(j):
                    s, t0, tz = TILES[j]
                    if j < 2:
                        pe.wait_ge(vn_ready, hd * 3 + (1, 3)[j])
                    elif j == 5:
                        pe.wait_ge(hn_ready, hd * 8 + 5)
                    elif j != 6:
                        pe.wait_ge(wt_ready, hd * 8 + (j - 1))
                    for a in range(0, LENS[s], 512):
                        b = min(a + 512, LENS[s])
                        mm = pe.matmul(flat(2 + 0)[0:tz, (j % 2) * 1024 + a:(j % 2) * 1024 + b], wk[:, 1, t0:t0 + tz],
                                       wk[:, 0, START[s] + a:START[s] + b], start=True, stop=True)
                    mm.then_inc(s_ready, 1)

                def read_state(i):
                    s, t0, tz = TILES[i]
                    tiles, a = OF_SEQ[s], t0 - START[s]
                    if i == tiles[0]:
                        pe.wait_ge(wt_ready, hd * 8 + (tiles[-1] + 1))
                    elif i not in (1, 6):
                        pe.wait_ge(hn_ready, hd * 8 + (i - 1))
                    for d in range(2):
                        js = [j for j in tiles if (j <= i if d == 0 else j >= i)]
                        for j in js:
                            sz = TILES[j][2]
                            off = a + (sz if d == 0 else 0)
                            mm = pe.matmul(ps[0:tz, 4 + 2 * (i % 2) + d, 0:M_DV + 1],
                                           wt[0:sz, j - tiles[0], off:off + tz], vn[0:sz, j, :],
                                           start=(j == js[0]), stop=(j == js[-1]))
                    mm.then_inc(pv_done, 1)

                def turn_y():
                    for c in range(2):
                        pe.wait_ge(hs_ready, hd + 1)
                        for i, (_, t0, tz) in enumerate(TILES):
                            mm = pe.transpose(flat(2)[:, c * 1024 + t0:c * 1024 + t0 + tz],
                                              hn(i)[0:tz, c * P:(c + 1) * P], ident[0:tz, 0:tz])
                        mm.then_inc(y_turned, 1)

                def call(f, *args):
                    return [lambda: f(*args)]

                run_block(n + 1, 1, 1, between={} if first else {5: [repeat_m]})
                run_block(n + 2, 0, 0, between={} if first else {4: [turn_ce]})
                run_block(n + 3, 1, 1, between={3: [repeat_m], 6: [turn_ce]} if first else {4: call(turn_v, 0)})
                if first:
                    turn_v(0)
                run_block(n + 4, 0, 0, between={0: call(turn_v, 1), **{j + 1: call(scores, j) for j in OF_SEQ[0]}})
                for i in OF_SEQ[0]:
                    read_state(i)
                run_block(n + 5, 1, 1, between={1: call(scores, 5), 2: call(scores, 6), 3: call(scores, 7),
                                                5: [lambda i=i: read_state(i) for i in OF_SEQ[1]]})
                if last:
                    out_blocks(OUT0, YL_AT[OUT0], KT, "all", late=2, between={3: [turn_y]})
                else:
                    run_block(n + 6, 0, 0)
                    turn_y()

            mlstm_head(0, MIX0, first=True)
            with pe.Fori(0, M_HEADS - 2) as i:
                mlstm_head(i + 1, i * 6 + (MIX0 + 6))
            mlstm_head(M_HEADS - 1, MIX0 + 6 * (M_HEADS - 1), last=True)
            ffn(FFN0, 0)

            def square_sum(g, i):
                if i < NQ:
                    lhs = q_sq[:, i * P:(i + 1) * P]
                elif i < NQ + NT - 1:
                    t0 = TILES[i - NQ][1]
                    lhs = k_sq[:, t0:t0 + P]
                else:
                    lhs = k_sq[:, T - META:T]
                mm = pe.matmul(ps[0:lhs.shape[1], 5, 2 * P + 2 * i:2 * P + 2 * i + 2], lhs, cst[:, COMP:COMP + 2],
                               start=True, stop=True, skip_group_check=True)
                if i == NQ + NT - 1:
                    mm.then_inc(qks_done, 1)

            def square_sums(g, k):
                return dict(between={k - 1: [lambda: pe.wait_ge(qsq_ready, g * 2 + 1)],
                                     k: [lambda: pe.wait_ge(qsq_ready, g * 2 + 2)]},
                            weave={k: [lambda i=i: square_sum(g, i) for i in range(NQ)],
                                   k + 1: [lambda i=i: square_sum(g, i) for i in range(NQ, NQ + NT)]})

            def turn_key_roots(g, n):
                pe.wait_ge(acc_free, n + (XT + 3))
                pe.wait_ge(lt_ready, g + 1)
                for i, (_, t0, tz) in enumerate(TILES):
                    mm = pe.transpose(flat(3)[:, t0:t0 + tz], key_roots[0:tz, i * P:(i + 1) * P], ident[0:tz, 0:tz])
                mm.then_inc(lt_turned, 1)

            def turn_va(hd, first):
                if first:
                    pe.wait_ge(acc_free, MIX1 + XT + 3)
                else:
                    pe.wait_ge(yl_ready, hd + (YL_AT[MIX1] - 1))
                for i, (_, t0, tz) in enumerate(TILES):
                    at_col = (i if i < 4 else {5: 4, 6: 5, 4: 6, 7: 7}[i]) * P
                    mm = pe.transpose(flat(3)[0:tz, at_col:at_col + P], v_raw[:, t0:t0 + tz], ident)
                mm.then_inc(va_turned, 1)

            def turn_output(hd, odd, p=3):
                pe.wait_ge(os_ready, hd + 1)
                for i in range(NQ):
                    mm = pe.transpose(flat(p)[:, i * P:(i + 1) * P], on(odd, i), ident)
                mm.then_inc(o_turned, 1)

            def attn_scores(hd, odd, i):
                s = Q_SEQ[i]
                if i == 0:
                    pe.wait_ge(kn_ready, hd + 1)
                for c in range(2):
                    if i:
                        pe.wait_ge(probs_ready, hd * (2 * NQ) + (2 * i - 1 + c))
                    rows = slice(D_HD * c, D_HD * (c + 1))
                    for a in range(0, LENS[s], 512):
                        b = min(a + 512, LENS[s])
                        mm = pe.matmul(flat(c)[:, a:b], wk[rows, odd, i * P:(i + 1) * P],
                                       wk[rows, 2 + odd, START[s] + a:START[s] + b], start=True, stop=True)
                    mm.then_inc(sc_ready, 1)

            def turn_attention(hd, i, first):
                if not (first and i == 0):
                    pe.wait_ge(o_ready, hd * NQ + i)
                pe.wait_ge(a_ready, hd * NQ + (i + 1))
                for q, j in enumerate(OF_SEQ[Q_SEQ[i]]):
                    sz = TILES[j][2]
                    dst = ps[:, 4, q * P:(q + 1) * P] if sz == P else ps[0:sz, 5, 0:P]
                    mm = pe.transpose(dst, prob(i, 0)[:, q * P:q * P + sz], ident)
                mm.then_inc(a_turned, 1)

            def attend(hd, odd, i):
                pe.wait_ge(at_ready, hd * NQ + (i + 1))
                if i == 0:
                    pe.wait_ge(va_ready, hd * 3 + 3)
                js = OF_SEQ[Q_SEQ[i]]
                for q, j in enumerate(js):
                    sz = TILES[j][2]
                    mm = pe.matmul(acc_o, at[0:sz, i % 2, q, :], va[0:sz, odd, j, :],
                                   start=(q == 0), stop=(j == js[-1]), skip_group_check=True)
                mm.then_inc(o_done, 1)

            def head(hd, odd, n, first=False, last=False):
                even = 1 - odd

                def between_tiles(i):
                    if i == 0 and not last:
                        pe.wait_ge(va_ready, hd * 3 + 3)
                        run_block(n, even, 3, tokens="inner", free=False)
                    elif i == 1 and not last:
                        pe.wait_ge(acc_free, n + (XT + 1))
                        run_block(n + 1, odd, 3, free=False, k1=3)
                    elif i == 2 and not last:
                        run_block(n + 1, odd, 3, free=False, k0=3)
                    elif i == 3 and not last:
                        pe.wait_ge(acc_free, n + (XT + 2))
                        pe.wait_ge(o_ready, hd * NQ + 3)
                        run_block(n + 2, even, 3, free=False, k1=3, **square_sums(hd + 1, 1))
                    elif i == 4 and not last:
                        run_block(n + 2, even, 3, free=False, k0=3, k1=6)
                    elif i == 5 and not last:
                        run_block(n + 2, even, 3, free=False, k0=6)
                    elif i == 6 and not last:
                        turn_key_roots(hd + 1, n)
                    elif i == 7 and not first and not last:
                        pe.wait_ge(kn_ready, hd + 2)
                        turn_output(hd - 1, even)
                    elif i == 6 and last:
                        pe.wait_ge(probs_ready, hd * (2 * NQ) + 2 * NQ - 1)
                        turn_output(hd - 1, even, 0)
                    elif last and i < 5:
                        if i == 0:
                            pe.wait_ge(va_ready, hd * 3 + 3)
                            pe.wait_ge(yl_ready, YL_AT[OUT1] - 2)
                        k = (0, 2, 3, 4, 5, 6)
                        run_block(OUT1, 0, 3, (yh, yl), tokens="packed", free=False, k0=k[i], k1=k[i + 1])

                attn_scores(hd, odd, 0)
                turn_va(hd, first)
                for i in range(NQ):
                    if i + 1 < NQ:
                        attn_scores(hd, odd, i + 1)
                    if i >= 4:
                        between_tiles(i)
                    if i >= 1:
                        attend(hd, odd, i - 1)
                    if i < 4:
                        between_tiles(i)
                    turn_attention(hd, i, first)
                between_tiles(NQ)
                attend(hd, odd, NQ - 1)
                between_tiles(NQ + 1)

            pe.wait_ge(xl_ready, KT * 3 - 1)
            run_block(MIX1, 0, 0, tokens="inner", between={KT - 2: [lambda: norm_ends(3)]})
            run_block(MIX1 + 1, 1, 1)
            run_block(MIX1 + 2, 0, 0, **square_sums(0, 3))
            turn_key_roots(0, MIX1)
            head(0, 0, MIX1 + 3, first=True)
            with pe.Fori(0, (D_HEADS - 2) // 2) as it:
                for sub in range(2):
                    head(it * 2 + (1 + sub), 1 - sub, it * 6 + (MIX1 + 6 + 3 * sub))
            head(D_HEADS - 1, 1, None, last=True)
            pe.wait_ge(yl_ready, YL_AT[OUT1] - 1)
            run_block(OUT1, 0, 3, (yh, yl), tokens="packed", k0=KT - 2, k1=KT - 1)
            turn_output(D_HEADS - 1, 1, 1)
            pe.wait_ge(yl_ready, YL_AT[OUT1])
            run_block(OUT1, 0, 3, (yh, yl), tokens="packed", k0=KT - 1)
            more_out_blocks(OUT1, KT, "packed")
            ffn(FFN1, 1)

        @block.vector
        def _(ve):
            v = Steps(ve, vstep)

            def evacuate(n, p, dst):
                ve.wait_ge(block_done, n + 1)
                ve.tensor_tensor(two(dst), pair(p), two(rstd[:, :]), ALU.mult).then_inc(acc_free, 1)

            def evacuate_inner(n, p, dst, packed_rstd):
                ve.wait_ge(block_done, n + 1)
                if packed_rstd:
                    ve.tensor_tensor(dst, packed_acc(p), rstd[:, 0:TQ], ALU.mult).then_inc(acc_free, 1)
                else:
                    for a, b, t in SEGS:
                        ins = ve.tensor_tensor(dst[:, a:b], flat(p)[:, a:b], rstd[:, t:t + b - a], ALU.mult)
                    ins.then_inc(acc_free, 1)

            def split_low(src, dst_h, dst_l, ready, done):
                ve.wait_ge(yh_ready, ready)
                ve.tensor_tensor(dst_l, src, dst_h.bitcast(F32), ALU.subtract).then_inc(done, 1)

            def fold(count, k, gain):
                ve.wait_ge(xh_ready, count + 1)
                ve.scalar_tensor_tensor(xl[:, k, :], h[:, k, :], gain, xh[:, k, :].bitcast(F32),
                                        ALU.mult, ALU.subtract).then_inc(xl_ready, 1)

            def add_square(count, src, first):
                ve.wait_ge(sq_ready, count + 1)
                if first:
                    ve.tensor_copy(wk[:, 6, :], wk[:, src, :]).then_inc(sq_summed, 1)
                else:
                    ve.wait_ge(sq_summed, count)
                    ve.tensor_tensor(wk[:, 6, :], wk[:, 6, :], wk[:, src, :], ALU.add).then_inc(sq_summed, 1)

            def invert(count):
                ve.wait_ge(norm_root, count)
                ve.reciprocal(rstd[:, :], rstd[:, :]).then_inc(rstd_ready, 1)
                ve.wait_ge(rstd_ready, count)

            def out_blocks(n0, norm, gain_at):
                if norm is not None:
                    ve.memset(wk[:, 6, :], 0.0).then_inc(ones_set, 1)
                    ve.wait_ge(ones_set, 1 + norm)
                def add_block(m, p):
                    ve.wait_ge(block_done, n0 + m + 1)
                    hm = h[:, bass.ds(m, 1), :].rearrange("p a b -> p (a b)")
                    if n0 < MIX1:
                        ve.tensor_tensor(two(hm), two(hm), pair(p), ALU.add).then_inc(acc_free, 1)
                    else:
                        for a, b, t in SEGS:
                            ins = ve.tensor_tensor(hm[:, t:t + b - a], hm[:, t:t + b - a], flat(p)[:, a:b], ALU.add)
                        ins.then_inc(acc_free, 1)
                    if norm is not None:
                        c = m + KT * norm
                        ve.wait_ge(xh_ready, c + 1)
                        ve.scalar_tensor_tensor(
                            xl[:, bass.ds(m, 1), :].rearrange("p a b -> p (a b)"), hm,
                            par[:, bass.ds(m + gain_at, 1)],
                            xh[:, bass.ds(m, 1), :].rearrange("p a b -> p (a b)").bitcast(F32),
                            ALU.mult, ALU.subtract).then_inc(xl_ready, 1)
                        ve.wait_ge(sq_ready, c + 1)
                        ve.wait_ge(sq_summed, c)
                        ve.tensor_tensor(wk[:, 6, :], wk[:, 6, :], wk[:, 7, :], ALU.add).then_inc(sq_summed, 1)

                if n0 == OUT1:
                    add_block(0, 3)
                    add_block(1, 1)
                with ve.Fori(1 if n0 == OUT1 else 0, KT // 2) as i:
                    for j in range(2):
                        add_block(i * 2 + j, j)
                if norm is not None:
                    invert(norm + 1)

            def ffn(n0, layer):
                y0 = YL_AT[n0]
                for g, tiles in enumerate(GROUPS):
                    with ve.Fori(0, tiles) as i:
                        ft = y0 - YL_AT[FFN0] + i if layer == 0 else y0 - YL_AT[FFN1] + FT + i
                        if layer == 0:
                            evacuate(n0 + 2 * i, 0, wk[:, 0, :])
                            evacuate(n0 + 2 * i + 1, 1, wk[:, 2, :])
                        else:
                            evacuate_inner(n0 + 2 * i, 0, wk[:, 0, 0:TQ], True)
                            evacuate_inner(n0 + 2 * i + 1, 1, wk[:, 2, 0:TQ], True)
                        ve.wait_ge(silu_ready, ft + 1)
                        ve.wait_ge(acc_free, n0 + 2 * i + 2 + XT)
                        ve.wait_ge(yl_ready, y0 + i)
                        nt = (T, TQ)[layer]
                        ve.tensor_tensor(wk[:, 3, 0:nt], wk[:, 1, 0:nt], wk[:, 2, 0:nt], ALU.mult).then_inc(yt_ready, 1)
                        split_low(wk[:, 3, 0:nt], tile_of(yh, i)[:, 0:nt], tile_of(yl, i)[:, 0:nt], y0 + i + 1, yl_ready)
                    n0 += 2 * tiles
                    y0 += tiles
                    last = g == len(GROUPS) - 1
                    out_blocks(n0, {0: 2, 1: None}[layer] if last else None, MIXN + KT)
                    n0 += KT

            ve.memset(ones[:, :], 1.0).then_inc(ones_set, 1)
            v(ve.memset(epsc, EPS))
            v(ve.memset(ss[:, :], 1.0))
            for r in range(XT):
                t0 = META + r * P if r < 4 else LENS[0] + META + (r - 4) * P
                ve.wait_ge(x_turned, r + 1)
                ve.tensor_copy(h[:, :, t0:t0 + P], flat(r % 2).rearrange("p (k c) -> p k c", k=KT)).then_inc(acc_free, 1)
                if r == XT - 1:
                    ve.wait_ge(meta_turned, 1)
                    for s in range(2):
                        ve.tensor_copy(h[:, :, START[s]:START[s] + META],
                                       ps[:, 4, 0:KT * META].rearrange("p (k c) -> p k c", k=KT)).then_inc(h_ready, 1)
                    ve.wait_ge(par_turned, 1)
                    ve.tensor_copy(par[:, :], ps[:, 5, 0:NPAR]).then_inc(par_ready, 1)
            ve.wait_ge(acc_free, XT)
            ve.wait_ge(h_ready, 2)
            ve.wait_ge(par_ready, 1)
            for k in range(KT):
                fold(k, k, par[:, MIXN + k:MIXN + k + 1])
                add_square(k, 7, k == 0)
            invert(1)

            ve.wait_ge(gates_done, 1)
            v(ve.tensor_tensor(two(wk[:, 2, :]), pair(2), two(rstd[:, :]), ALU.mult))
            v.wait()
            ve.tensor_scalar(wk[:, 2, :], wk[:, 2, :], par[:, BGATE:BGATE + 1], None, ALU.add).then_inc(gate_x, 1)
            evacuate(MIX0, 0, wk[:, 0, :])
            v(ve.memset(wk[:, 4, :], 0.0))
            v(ve.memset(mrow[:, :], 0.0))
            v(ve.memset(vn[:, :, M_DV:M_DV + 1], 1.0))
            ve.wait_ge(gate_soft, 1)
            ve.wait_ge(gate_x, 1)
            v(ve.scalar_tensor_tensor(wk[:, 3, :], wk[:, 2, :], 0.0, wk[:, 5, :], ALU.min, ALU.subtract))
            v.wait()

            def span(s, back):
                a, b = START[s], START[s] + LENS[s]
                return slice(a, b) if not back else slice(b - 1, a - 1 if a else None, -1)

            for s in range(2):
                zero = small[:, 1:2]
                if s == 0:
                    v(ve.memset(zero, 0.0))
                    v.wait()
                for d in range(2):
                    src, dst = slice(32 + 64 * d, 36 + 64 * d), slice(64 * d, 64 * d + M_HEADS)
                    v(ve.tensor_tensor_scan(wk[dst, 4, span(s, d)], wk[src, 3, span(s, d)],
                                            small[src, 1:2].to_broadcast([M_HEADS, LENS[s]]), 0.0, ALU.add, ALU.add))
            v.wait()
            v(ve.tensor_tensor(cerow, wk[:, 2, :], wk[:, 4, :], ALU.subtract))
            evacuate(MIX0 + 1, 1, wk[:, 1, :])
            v.wait()
            for s in range(2):
                for d in range(2):
                    rows = slice(64 * d, 64 * d + M_HEADS)
                    v(ve.tensor_tensor_scan(mrow[rows, span(s, d)], cerow[rows, span(s, d)],
                                            small[rows, 1:2].to_broadcast([M_HEADS, LENS[s]]), 0.0, ALU.max, ALU.add))
            v.wait()
            ve.tensor_tensor(wk[:, 5, :], wk[:, 4, :], mrow[:, :], ALU.add).then_inc(gate_m, 1)

            def mlstm_head(hd, n, first=False):
                if not first:
                    evacuate(n, 0, wk[:, 0, :])
                ve.wait_ge(gate_m, 1)
                ve.tensor_scalar(wk[:, 4, :], mrow[:, :], cst[:, bass.ds(hd + ONEHOT, 1)], None, ALU.mult)\
                  .then_inc(mrow_masked, 1)
                evacuate(*((n + 2, 0, wk[:, 6, :]) if first else (n + 1, 1, wk[:, 1, :])))
                ve.wait_ge(ce_turned, hd + 1)
                turned = flat(2).rearrange("p (i g c) -> p i g c", i=2 * NT, g=4)
                for a, b, rows in ((0, 4, P), (5, 7, P), (4, 5, META), (7, 8, META)):
                    ve.tensor_copy(ce[0:rows, a:b, :],
                                   turned[0:rows, a:b, :, bass.ds(hd, 1)].rearrange("p i g c -> p i (g c)"))\
                      .then_inc(ce_ready, 1)
                if not first:
                    evacuate(n + 2, 0, wk[:, 6, :])

                def diagonals(j):
                    s, t0, tz = TILES[j]
                    q, a = j - OF_SEQ[s][0], t0 - START[s]
                    for d, mask in ((0, MASKF), (1, MASKB)):
                        off = a + (tz if d == 0 else 0)
                        ve.tensor_tensor(wt[0:tz, q, off:off + tz], wk[0:tz, 2 + d, t0:t0 + tz],
                                         cst[0:tz, mask:mask + tz], ALU.add).then_inc(diag_ready, 1)

                def state_weights(j):
                    s, t0, tz = TILES[j]
                    q, a = j - OF_SEQ[s][0], t0 - START[s]
                    ve.wait_ge(s_ready, hd * 8 + (j + 1))
                    ve.wait_ge(e_ready, hd * 8 + (j + 1))
                    base = (j % 2) * 1024
                    fwd = wt[0:tz, q, a + tz:LENS[s] + tz]
                    bwd = wt[0:tz, q, 0:a + tz]
                    v(ve.scalar_tensor_tensor(fwd, flat(2)[0:tz, base + a:base + LENS[s]], M_DK ** -0.5, fwd,
                                              ALU.mult, ALU.mult))
                    ve.scalar_tensor_tensor(bwd, flat(2)[0:tz, base:base + a + tz], M_DK ** -0.5, bwd,
                                            ALU.mult, ALU.mult).then_inc(wt_ready, 1)

                def normalise(i):
                    s, t0, tz = TILES[i]
                    ve.wait_ge(pv_done, hd * 8 + (i + 1))
                    den = [ps[0:tz, 4 + 2 * (i % 2) + d, M_DV:M_DV + 1] for d in range(2)]
                    low = [dd[0:tz, i % 2, d:d + 1] for d in range(2)]
                    for d in range(2):
                        v(ve.tensor_scalar(low[d], den[d], -1.0, ce[0:tz, i, 2 * d + 1:2 * d + 2], ALU.mult, ALU.max))
                    v.wait()
                    for d in range(2):
                        v(ve.tensor_scalar(low[d], den[d], low[d], None, ALU.max))
                    v.wait()
                    v(ve.reciprocal(rd[0:tz, i % 2, :], dd[0:tz, i % 2, :]))
                    v.wait()
                    v(ve.tensor_scalar(hn(i)[0:tz, :], ps[0:tz, 4 + 2 * (i % 2), 0:M_DV], rd[0:tz, i % 2, 0:1], None,
                                       ALU.mult))
                    v.wait()
                    ve.scalar_tensor_tensor(hn(i)[0:tz, :], ps[0:tz, 5 + 2 * (i % 2), 0:M_DV], rd[0:tz, i % 2, 1:2],
                                            hn(i)[0:tz, :], ALU.mult, ALU.add).then_inc(hn_ready, 1)

                ve.wait_ge(mrep_ready, hd * 2 + 2)
                for j in OF_SEQ[0]:
                    diagonals(j)
                evacuate(n + 3, 1, wk[:, 7, :])
                for j in OF_SEQ[0]:
                    state_weights(j)
                evacuate(n + 4, 0, wk[:, 4, :])
                for i in OF_SEQ[0]:
                    normalise(i)
                for j in OF_SEQ[1]:
                    diagonals(j)
                for j in OF_SEQ[1]:
                    state_weights(j)
                for i in OF_SEQ[1]:
                    normalise(i)
                evacuate(n + 5, 1, wk[:, 5, :])
                ve.wait_ge(hroot, hd + 1)
                v(ve.reciprocal(rs[:, :], rs[:, :]))
                v.wait()
                ve.wait_ge(hn_ready, hd * 8 + 8)
                for i, (_, t0, tz) in enumerate(TILES):
                    ins = ve.tensor_scalar(hn(i)[0:tz, :], hn(i)[0:tz, :], rs[0:tz, i:i + 1], None, ALU.mult)
                ins.then_inc(hs_ready, 1)
                for c in range(2):
                    ve.wait_ge(y_turned, hd * 2 + (c + 1))
                    ve.wait_ge(sig_ready, hd * 2 + (c + 1))
                    ve.scalar_tensor_tensor(wk[:, c, :], flat(2)[:, c * 1024:c * 1024 + T],
                                            par[:, GHEAD + c:GHEAD + c + 1], wk[:, 4 + c, :],
                                            ALU.mult, ALU.mult).then_inc(yt_ready, 1)
                for c in range(2):
                    split_low(wk[:, c, :], yh[:, bass.ds(hd * 2 + c, 1), :].rearrange("p a b -> p (a b)"),
                              yl[:, bass.ds(hd * 2 + c, 1), :].rearrange("p a b -> p (a b)"), hd * 2 + (c + 1), yl_ready)
                ve.wait_ge(yl_ready, hd * 2 + 2)

            mlstm_head(0, MIX0, first=True)
            with ve.Fori(0, M_HEADS - 1) as i:
                v.loop_start(i, M_PER)
                mlstm_head(i + 1, i * 6 + (MIX0 + 6))
            v.loop_end(M_HEADS - 1, M_PER)

            out_blocks(OUT0, 1, FFNN)
            ve.wait_ge(rope_in, 32)
            ve.stream_shuffle(gswap[:, :], par[:, GQ:GQ + 2], SWAP).then_inc(attn_set, 1)
            ve.tensor_scalar(cq[:, :], ck[:, :], par[:, GQ:GQ + 1], None, ALU.mult).then_inc(attn_set, 1)
            ve.wait_ge(attn_set, 2)
            ve.tensor_scalar(ck[:, :], ck[:, :], par[:, GK:GK + 1], None, ALU.mult).then_inc(attn_set, 1)
            ve.tensor_scalar(sq[:, :], sk[:, :], gswap[:, 0:1], None, ALU.mult).then_inc(attn_set, 1)
            ve.wait_ge(attn_set, 4)
            ve.tensor_scalar(sk[:, :], sk[:, :], gswap[:, 1:2], None, ALU.mult).then_inc(attn_set, 1)
            ve.tensor_scalar(gsub[:, :], par[:, GSUB:GSUB + 1], 1.0 - LAMBDA_INIT, None, ALU.mult).then_inc(attn_set, 1)
            ve.wait_ge(lam_in, 64)
            for q in range(2):
                ve.tensor_tensor_reduce(lv[:, 2 * q, :], lv[:, 2 * q, :], lv[:, 2 * q + 1, :], 1.0, 0.0,
                                        ALU.mult, ALU.add, lam[:, q:q + 1]).then_inc(lam_sums, 1)
            ve.wait_ge(lam_exp, 1)
            v(ve.tensor_tensor(lam[:, 6:7], lam[:, 5:6], lam[:, 4:5], ALU.subtract))
            v.wait()
            ve.tensor_scalar(lam[:, 7:8], lam[:, 6:7], -LAMBDA_INIT, None, ALU.add).then_inc(attn_set, 1)
            ffn(FFN0, 0)
            ve.memset(qk2[:, :], 1.0).then_inc(attn_set, 1)
            ve.wait_ge(attn_set, ATTN_SET)
            ROPE_SEGS = ([(a, b, META) for a, b, _ in SEGS], [(0, LENS[0], 0), (LENS[0], T, 0)])

            def rope_start(which, x):
                segs, nt = ROPE_SEGS[which], (TQ, T)[which]
                ve.sem_inc(vector_passed, 1)
                v(ve.stream_shuffle(swapped[:, 0:nt], x, SWAP))
                v.wait()
                for a, b, t in segs:
                    v(ve.tensor_tensor(swapped[:, a:b], swapped[:, a:b], (sq, sk)[which][:, t:t + b - a], ALU.mult))

            def rope_end(which, x, g):
                segs, nt = ROPE_SEGS[which], (TQ, T)[which]
                ve.wait_ge(qsq_ready, g * 2 + (which + 1))
                for a, b, t in segs:
                    v(ve.tensor_tensor(x[:, a:b], x[:, a:b], (cq, ck)[which][:, t:t + b - a], ALU.mult))
                v.wait()
                v(ve.tensor_tensor(x, x, swapped[:, 0:nt], ALU.add))

            def invert_roots(g, odd):
                ve.wait_ge(qk_root, g + 1)
                v(ve.reciprocal(qkr[:, odd, :], qk2[:, :]))
                v.wait()
                v(ve.tensor_scalar(qkr[:, odd, 0:2 * NQ], qkr[:, odd, 0:2 * NQ], D_HD ** -0.5, None, ALU.mult))
                ve.tensor_copy(key_roots.rearrange("p (i f) -> p i f", i=2 * NT),
                               qkr[:, odd, 2 * NQ:2 * (NQ + NT)].unsqueeze(2).to_broadcast([P, 2 * NT, D_HD]))\
                  .then_inc(lt_ready, 1)

            def normalise_k(g, x):
                ve.wait_ge(lt_turned, g + 1)
                v.wait()
                ve.tensor_tensor(x, flat(3)[:, 0:T], x, ALU.mult).then_inc(kn_ready, 1)

            def maxima(hd, odd, i):
                for c in range(2):
                    ve.wait_ge(sc_ready, hd * (2 * NQ) + (2 * i + c + 1))
                    v(ve.tensor_reduce(mx[:, i, c:c + 1], flat(c)[:, 0:LENS[Q_SEQ[i]]], AX.X, ALU.max))
                    v.wait()
                    ve.tensor_scalar(nb[:, i, c:c + 1], mx[:, i, c:c + 1], qkr[:, odd, 2 * i + c:2 * i + c + 1], -1.0,
                                     ALU.mult, ALU.mult).then_inc(nb_ready, 1)

            def combine(hd, i):
                keys = LENS[Q_SEQ[i]]
                ve.wait_ge(probs_ready, hd * (2 * NQ) + (2 * i + 2))
                v(ve.reciprocal(rsum[:, i, :], sums[:, i, :]))
                v.wait()
                v(ve.scalar_tensor_tensor(ratio[:, i:i + 1], sums[:, i, 0:1], lam[:, 7:8], rsum[:, i, 1:2],
                                          ALU.mult, ALU.mult))
                v.wait()
                ve.scalar_tensor_tensor(prob(i, 0)[:, 0:keys], prob(i, 1)[:, 0:keys], ratio[:, i:i + 1],
                                        prob(i, 0)[:, 0:keys], ALU.mult, ALU.add).then_inc(a_ready, 1)

            def output(hd, odd, i):
                ve.wait_ge(o_done, hd * NQ + (i + 1))
                ve.tensor_scalar(on(odd, i), acc_o, rsum[:, i, 0:1], None, ALU.mult).then_inc(o_ready, 1)

            def scale_output(hd, odd):
                ve.wait_ge(oroot, hd + 1)
                v(ve.reciprocal(rs[:, 0:NQ], rs[:, 0:NQ]))
                v.wait()
                ve.wait_ge(o_ready, hd * NQ + NQ)
                for i in range(NQ):
                    ins = ve.tensor_scalar(on(odd, i), on(odd, i), rs[:, i:i + 1], None, ALU.mult)
                ins.then_inc(os_ready, 1)

            def deliver(hd, p=3):
                ve.wait_ge(yh_ready, hd + (YL_AT[MIX1] + 1))
                ve.scalar_tensor_tensor(tile_of(yl, hd)[:, 0:TQ], packed_acc(p), gsub[:, 0:1],
                                        tile_of(yh, hd)[:, 0:TQ].bitcast(F32), ALU.mult, ALU.subtract)\
                  .then_inc(yl_ready, 1)

            def head(hd, odd, n, first=False, last=False):
                even = 1 - odd
                qx, kx = wk[:, even, 0:TQ], wk[:, 2 + even, :]
                for i in range(NQ - 1):
                    maxima(hd, odd, i)
                    combine(hd, i)
                    if not last:
                        if i == 1:
                            evacuate_inner(n, 3, qx, False)
                        elif i == 2:
                            ve.wait_ge(acc_free, n + (XT + 1))
                            rope_start(0, qx)
                        elif i == 3:
                            evacuate(n + 1, 3, kx)
                    if i == 4 and not last:
                        ve.wait_ge(acc_free, n + (XT + 2))
                        rope_start(1, kx)
                        rope_end(1, kx, hd + 1)
                    elif i >= 1:
                        output(hd, odd, i - 1)
                        if i == 3 and not last:
                            rope_end(0, qx, hd + 1)
                maxima(hd, odd, NQ - 1)
                if not last:
                    invert_roots(hd + 1, even)
                    output(hd, odd, NQ - 3)
                combine(hd, NQ - 1)
                if not first:
                    scale_output(hd - 1, even)
                if not last:
                    evacuate(n + 2, 3, v_raw)
                output(hd, odd, NQ - 2)
                if not last:
                    normalise_k(hd + 1, kx)
                output(hd, odd, NQ - 1)
                if not first:
                    deliver(hd - 1, 0 if last else 3)

            evacuate_inner(MIX1, 0, wk[:, 0, 0:TQ], False)
            ve.wait_ge(acc_free, MIX1 + XT + 1)
            rope_start(0, wk[:, 0, 0:TQ])
            rope_end(0, wk[:, 0, 0:TQ], 0)
            evacuate(MIX1 + 1, 1, wk[:, 2, :])
            ve.wait_ge(acc_free, MIX1 + XT + 2)
            v.wait()
            rope_start(1, wk[:, 2, :])
            rope_end(1, wk[:, 2, :], 0)
            invert_roots(0, 0)
            evacuate(MIX1 + 2, 0, v_raw)
            normalise_k(0, wk[:, 2, :])
            head(0, 0, MIX1 + 3, first=True)
            with ve.Fori(0, (D_HEADS - 2) // 2) as it:
                v.loop_start(it, A_PER)
                for sub in range(2):
                    head(it * 2 + (1 + sub), 1 - sub, it * 6 + (MIX1 + 6 + 3 * sub))
            v.loop_end((D_HEADS - 2) // 2, A_PER)
            head(D_HEADS - 1, 1, None, last=True)
            scale_output(D_HEADS - 1, 1)
            deliver(D_HEADS - 1, 1)

            out_blocks(OUT1, 3, FFNN + KT)
            ffn(FFN1, 1)

        @block.scalar
        def _(sc):
            def high(src, dst, ready, done=yh_ready):
                sc.wait_ge(yt_ready, ready)
                sc.sem_inc(scalar_passed, 1)
                sc.activation(dst, src, ACT.Copy).then_inc(done, 1)

            def root(count):
                sc.wait_ge(norm_sum, count)
                dst, src = (two(rstd[:, :]), pair(3)) if count < 4 else (rstd[:, 0:TQ], packed_acc(3))
                sc.activation(dst, src, ACT.Sqrt, bias=epsc, scale=1.0 / D).then_inc(norm_root, 1)

            def out_blocks(n0, norm, gain_at):
                if norm is None:
                    return
                with sc.Fori(0, KT // 2) as i:
                    for j in range(2):
                        m = i * 2 + j
                        c = m + KT * norm
                        hm = h[:, bass.ds(m, 1), :].rearrange("p a b -> p (a b)")
                        sc.wait_ge(acc_free, n0 + m + 1 + XT)
                        sc.sem_inc(scalar_passed, 1)
                        sc.activation(xh[:, bass.ds(m, 1), :].rearrange("p a b -> p (a b)"), hm, ACT.Copy,
                                      scale=par[:, bass.ds(m + gain_at, 1)]).then_inc(xh_ready, 1)
                        sc.wait_ge(sq_summed, c)
                        sc.sem_inc(scalar_passed, 1)
                        sc.activation(wk[:, 7, :], hm, ACT.Square).then_inc(sq_ready, 1)
                root(norm + 1)

            def ffn(n0, layer):
                y0 = YL_AT[n0]
                for g, tiles in enumerate(GROUPS):
                    with sc.Fori(0, tiles) as i:
                        sc.wait_ge(acc_free, n0 + 2 * i + 1 + XT)
                        nt = (T, TQ)[layer]
                        sc.activation(wk[:, 1, 0:nt], wk[:, 0, 0:nt], ACT.Silu).then_inc(silu_ready, 1)
                        high(wk[:, 3, 0:nt], tile_of(yh, i)[:, 0:nt], y0 - D_HEADS * layer + i + 1)
                    n0 += 2 * tiles
                    y0 += tiles
                    last = g == len(GROUPS) - 1
                    out_blocks(n0, {0: 2, 1: None}[layer] if last else None, MIXN + KT)
                    n0 += KT

            with nc.allow_non_contiguous_dma(reason="16 gate columns"):
                sc.dma_start(graw[:, :, :], m_w_in[0].rearrange("(k p) n -> p k n", p=P)[:, :, GATE_COLS:GATE_COLS + 16])\
                  .then_inc(gate_in, 16)
            sc.wait_ge(pool_set, 1)
            for at_row, src in ((MIXN, norm_mix.rearrange("l (k p) -> (l k) p", p=P)),
                                (FFNN, norm_ffn.rearrange("l (k p) -> (l k) p", p=P)),
                                (GHEAD, m_g_head[0].rearrange("(k p) -> k p", p=P)), (GSUB, d_g_sub)):
                sc.dma_start(prow[at_row:at_row + src.shape[0], :], src).then_inc(params_in, 16)
            for at_row, src in ((GQ, d_g_q), (GK, d_g_k)):
                for c in range(2):
                    sc.dma_start(prow[at_row:at_row + 1, c * D_HD:(c + 1) * D_HD], src).then_inc(params_in, 16)
            for g in range(4):
                sc.dma_start(prow[BGATE:BGATE + 1, 32 * g:32 * g + M_HEADS],
                             m_b_gate[:, M_HEADS * g:M_HEADS * (g + 1)]).then_inc(params_in, 16)
            for j, col in enumerate((0, M_HEADS * M_DK)):
                sc.dma_start(raw[:, j, :].rearrange("p (k c) -> p k c", k=KT),
                             m_w_in[0].rearrange("(k p) n -> p k n", p=P)[:, :, col:col + P]).then_inc(raw_in[j], 16)
            sc.wait_ge(acc_free, XT)
            sc.wait_ge(h_ready, 2)
            sc.wait_ge(par_ready, 1)
            for k in range(KT):
                sc.activation(xh[:, k, :], h[:, k, :], ACT.Copy, scale=par[:, MIXN + k:MIXN + k + 1]).then_inc(xh_ready, 1)
                if k:
                    sc.wait_ge(sq_summed, k)
                sc.activation(wk[:, 7, :], h[:, k, :], ACT.Square).then_inc(sq_ready, 1)
            root(1)

            a = Steps(sc, astep)
            sc.wait_ge(gate_x, 1)
            a(sc.activation(wk[:, 5, :], wk[:, 2, :], ACT.Abs))
            a.wait()
            a(sc.activation(wk[:, 5, :], wk[:, 5, :], ACT.Exp, scale=-1.0))
            a.wait()
            sc.wait_ge(ones_set, 1)
            sc.activation(wk[:, 5, :], wk[:, 5, :], ACT.Ln, bias=ones[:, 0:1]).then_inc(gate_soft, 1)
            sc.wait_ge(gate_m, 1)
            for d in range(2):
                sc.activation(cerow[32 + 64 * d:36 + 64 * d, :], wk[64 * d:64 * d + M_HEADS, 5, :], ACT.Exp,
                              scale=-1.0).then_inc(gate_e, 1)

            def mlstm_head(hd, n, first=False):
                sc.wait_ge(mrep_done, hd + 1)
                for d in range(2):
                    sc.activation(two(wk[:, 2 + d, :]), pair(2 + d), ACT.Copy).then_inc(mrep_ready, 1)

                def values():
                    sc.wait_ge(v_turned, hd + 1)
                    sc.activation(vn[:, 0:4, 0:M_DV], flat(2)[:, 0:4 * M_DV].rearrange("p (i c) -> p i c", i=4),
                                  ACT.Copy).then_inc(vn_ready, 1)
                    sc.activation(vn[:, 5:7, 0:M_DV], flat(2)[:, 4 * M_DV:6 * M_DV].rearrange("p (i c) -> p i c", i=2),
                                  ACT.Copy).then_inc(vn_ready, 1)
                    sc.activation(vn[0:META, 4:8:3, 0:M_DV],
                                  flat(2)[0:META, 6 * M_DV:8 * M_DV].rearrange("p (i c) -> p i c", i=2),
                                  ACT.Copy).then_inc(vn_ready, 1)

                def decays(j):
                    s, t0, tz = TILES[j]
                    q, a = j - OF_SEQ[s][0], t0 - START[s]
                    first = OF_SEQ[s][0] if s else 0
                    sc.wait_ge(diag_ready, hd * 16 + (2 * j + 2))
                    ops = [(wt[0:tz, q, a + tz:a + 2 * tz], wt[0:tz, q, a + tz:a + 2 * tz], 0)]
                    if a + tz < LENS[s]:
                        ops.append((wt[0:tz, q, a + 2 * tz:LENS[s] + tz], wk[0:tz, 2, t0 + tz:START[s] + LENS[s]], 0))
                    if a:
                        ops.append((wt[0:tz, q, 0:a], wk[0:tz, 3, START[s]:t0], 1))
                    ops.append((wt[0:tz, q, a:a + tz], wt[0:tz, q, a:a + tz], 1))
                    for dst, src, d in ops:
                        ins = sc.activation(dst, src, ACT.Exp, bias=ce[0:tz, j, 2 * d:2 * d + 1], scale=-1.0)
                    ins.then_inc(e_ready, 1)

                def squares(i):
                    s, t0, tz = TILES[i]
                    sc.wait_ge(hn_ready, hd * 8 + (i + 1))
                    if i:
                        sc.wait_ge(hsq_ready, hd * 8 + i)
                    sc.activation(wkf[0:tz, 0:M_DV], hn(i)[0:tz, :], ACT.Square, accum_out=ss[0:tz, i:i + 1])\
                      .then_inc(hsq_ready, 1)

                sc.wait_ge(ce_ready, hd * 4 + 4)
                for j in OF_SEQ[0]:
                    if j == (2 if first else 4):
                        values()
                    decays(j)
                for i in OF_SEQ[0]:
                    squares(i)
                for j in OF_SEQ[1]:
                    decays(j)
                for i in OF_SEQ[1]:
                    squares(i)
                sc.wait_ge(hsq_ready, hd * 8 + 8)
                sc.activation(rs[:, :], ss[:, :], ACT.Sqrt, bias=epsc, scale=1.0 / M_DV).then_inc(hroot, 1)
                for c in range(2):
                    sc.wait_ge(acc_free, n + (5 + c + XT))
                    sc.activation(wk[:, 4 + c, :], wk[:, 4 + c, :], ACT.Sigmoid).then_inc(sig_ready, 1)
                for c in range(2):
                    high(wk[:, c, :], yh[:, bass.ds(hd * 2 + c, 1), :].rearrange("p a b -> p (a b)"), hd * 2 + (c + 1))

            mlstm_head(0, MIX0, first=True)
            with sc.Fori(0, M_HEADS - 1) as i:
                mlstm_head(i + 1, i * 6 + (MIX0 + 6))
            out_blocks(OUT0, 1, FFNN)
            sc.dma_start(ck[:, :], rope[:, 0, :]).then_inc(rope_in, 16)
            sc.dma_start(sk[:, :], rope[:, 1, :]).then_inc(rope_in, 16)
            for q, src in enumerate((d_lam_q1, d_lam_k1, d_lam_q2, d_lam_k2)):
                sc.dma_start(lv[:, q, :], src.to_broadcast([P, D_HD])).then_inc(lam_in, 16)
            sc.wait_ge(lam_sums, 2)
            sc.activation(lam[:, 4:6], lam[:, 0:2], ACT.Exp).then_inc(lam_exp, 1)
            ffn(FFN0, 0)

            def squares_of(which, x, done):
                sc.wait_ge(acc_free, done)
                sc.activation((q_sq, k_sq)[which], x, ACT.Square).then_inc(qsq_ready, 1)

            def qk_roots(g):
                sc.wait_ge(qks_done, g + 1)
                end = 2 * (NQ + NT - 1)
                for rows, a, b in ((P, 0, end), (META, end, end + 2)):
                    ins = sc.activation(qk2[0:rows, a:b], ps[0:rows, 5, 2 * P + a:2 * P + b], ACT.Sqrt,
                                        bias=epsc[0:rows, :], scale=1.0 / D_HD)
                ins.then_inc(qk_root, 1)

            def output_roots(hd, odd):
                sc.wait_ge(osq_ready, hd * NQ + NQ)
                sc.activation(rs[:, 0:NQ], oss[:, odd, :], ACT.Sqrt, bias=epsc, scale=1.0 / P).then_inc(oroot, 1)

            def values(g, odd):
                sc.wait_ge(va_turned, g + 1)
                src = flat(3).rearrange("p (i c) -> p i c", i=NT)
                sc.activation(va[:, odd, 0:4, :], src[:, 0:4, :], ACT.Copy).then_inc(va_ready, 1)
                sc.activation(va[:, odd, 5:7, :], src[:, 4:6, :], ACT.Copy).then_inc(va_ready, 1)
                sc.activation(va[0:META, odd, 4:8:3, :], src[0:META, 6:8, :], ACT.Copy).then_inc(va_ready, 1)

            def exps(hd, odd, i):
                keys = LENS[Q_SEQ[i]]
                for c in range(2):
                    sc.wait_ge(nb_ready, hd * (2 * NQ) + (2 * i + c + 1))
                    sc.activation(prob(i, c)[:, 0:keys], flat(c)[:, 0:keys], ACT.Exp, bias=nb[:, i, c:c + 1],
                                  scale=qkr[:, odd, 2 * i + c:2 * i + c + 1], accum_out=sums[:, i, c:c + 1]).then_inc(probs_ready, 1)

            def turned(hd, i):
                sc.wait_ge(a_turned, hd * NQ + (i + 1))
                full = len(OF_SEQ[Q_SEQ[i]]) - 1
                sc.activation(at[:, i % 2, 0:full, :], ps[:, 4, 0:full * P].rearrange("p (q c) -> p q c", q=full), ACT.Copy)
                sc.activation(at[0:META, i % 2, full, :], ps[0:META, 5, 0:P], ACT.Copy).then_inc(at_ready, 1)

            def squared(hd, odd, i):
                sc.wait_ge(o_ready, hd * NQ + (i + 1))
                if i:
                    sc.wait_ge(osq_ready, hd * NQ + i)
                sc.activation(junk, on(odd, i), ACT.Square, accum_out=oss[:, odd, i:i + 1]).then_inc(osq_ready, 1)

            def deliver(hd, p=3):
                sc.wait_ge(o_turned, hd + 1)
                sc.sem_inc(scalar_passed, 1)
                sc.activation(tile_of(yh, hd)[:, 0:TQ], packed_acc(p), ACT.Copy, scale=gsub[:, 0:1]).then_inc(yh_ready, 1)

            def head(hd, odd, n, first=False, last=False):
                even = 1 - odd
                exps(hd, odd, 0)
                values(hd, odd)
                exps(hd, odd, 1)
                turned(hd, 0)
                if not last:
                    squares_of(0, wk[:, even, 0:TQ], n + (XT + 1))
                exps(hd, odd, 2)
                turned(hd, 1)
                squared(hd, odd, 0)
                exps(hd, odd, 3)
                turned(hd, 2)
                squared(hd, odd, 1)
                if not last:
                    squares_of(1, wk[:, 2 + even, :], n + (XT + 2))
                exps(hd, odd, 4)
                squared(hd, odd, 2)
                sc.wait_ge(a_turned, hd * NQ + 4)
                if not last:
                    qk_roots(hd + 1)
                if not first:
                    output_roots(hd - 1, even)
                turned(hd, 3)
                exps(hd, odd, 5)
                turned(hd, 4)
                squared(hd, odd, 3)
                turned(hd, 5)
                squared(hd, odd, 4)
                if not first:
                    deliver(hd - 1, 0 if last else 3)
                squared(hd, odd, 5)

            squares_of(0, wk[:, 0, 0:TQ], MIX1 + XT + 1)
            squares_of(1, wk[:, 2, :], MIX1 + XT + 2)
            qk_roots(0)
            head(0, 0, MIX1 + 3, first=True)
            with sc.Fori(0, (D_HEADS - 2) // 2) as it:
                for sub in range(2):
                    head(it * 2 + (1 + sub), 1 - sub, it * 6 + (MIX1 + 6 + 3 * sub))
            head(D_HEADS - 1, 1, None, last=True)
            output_roots(D_HEADS - 1, 1)
            deliver(D_HEADS - 1, 1)
            out_blocks(OUT1, 3, FFNN + KT)
            ffn(FFN1, 1)
            for m in range(KT):
                at_col = (m % 2) * 1024
                sc.wait_ge(out_turned, m + 1)
                sc.activation(wkf[:, m * TQ:(m + 1) * TQ], flat(2)[:, at_col:at_col + TQ], ACT.Copy).then_inc(out_copied, 1)


_INS = ['x_prompt', 'x_sample', 'meta_tokens', 'norm_mix', 'norm_ffn', 'm_w_in', 'm_b_gate', 'm_g_head', 'm_w_out',
        'd_w_in', 'd_g_q', 'd_g_k', 'd_lam_q1', 'd_lam_k1', 'd_lam_q2', 'd_lam_k2', 'd_g_sub', 'd_w_out',
        'ffn_w_in', 'ffn_w_out']
_OUTS = [((1, 512, D), 'float32'), ((1, 256, D), 'float32')]


def kernel(**inputs):
    import numpy as _np
    import concourse.bacc as _bacc
    from concourse import mybir as _mybir
    from concourse.bass_utils import run_bass_kernel_spmd as _run

    nc = _bacc.Bacc("TRN2", target_bir_lowering=False, num_devices=1)
    arrays, args = {}, []
    consts, rope = host_constants()
    for name, a in [(n, inputs[n]) for n in _INS] + [("consts", consts), ("rope", rope)]:
        a = _np.ascontiguousarray(a)
        arrays[f"in_{name}_dram"] = a
        args.append(nc.dram_tensor(f"in_{name}_dram", a.shape, _mybir.dt.from_np(a.dtype), kind="ExternalInput").ap())
    for i, (shape, dtype) in enumerate(_OUTS):
        dt = _mybir.dt.from_np(_np.dtype(dtype))
        args.append(nc.dram_tensor(f"out_{i}_dram", shape, dt, kind="ExternalOutput").ap())
    trunk(nc, *args)
    r = _run(nc, [arrays], core_ids=[0])
    return tuple(r.results[0][f"out_{i}_dram"] for i in range(len(_OUTS)))
```
